# Optimizing a Trainium2 kernel written in Bass

```python
import math
import jax, jax.numpy as jnp
from jax import lax
import numpy as np

D_MODEL = 1024
BATCH = 1
SEQ = 256
DEPTH = 1

CHUNK = 64
N_META = 16
QBLK = 128
SB_HEADS = 8
SB_HEAD_DIM = D_MODEL // SB_HEADS
DF_HEADS = 8
DF_HEAD_DIM = D_MODEL // (2 * DF_HEADS)
SB_W = SB_HEADS * SB_HEAD_DIM
DF_QK_W = DF_HEADS * 2 * DF_HEAD_DIM
DF_V_W = DF_HEADS * 2 * DF_HEAD_DIM
IN_W = 3 * SB_W + 2 * DF_QK_W + DF_V_W
D_FF = -(-(8 * D_MODEL) // (3 * 256)) * 256
EPS = 1e-6


def rmsnorm(x, g):
    xf = x.astype(jnp.float32)
    y = xf * lax.rsqrt(jnp.mean(xf * xf, axis=-1, keepdims=True) + EPS)
    return (y * g.astype(jnp.float32)).astype(x.dtype)

def stick_breaking_block(q, k, v, qpos, kpos):
    z = jnp.einsum('bhqd,bhkd->bhqk', q, k).astype(jnp.float32) * (SB_HEAD_DIM ** -0.5)
    causal = kpos[None, :] < qpos[:, None]
    u = jnp.where(causal, jax.nn.log_sigmoid(-z), 0.0)
    rest = lax.cumsum(u, axis=3, reverse=True) - u
    log_a = jax.nn.log_sigmoid(z) + rest
    a = jnp.where(causal, jnp.exp(log_a), 0.0)
    return jnp.einsum('bhqk,bhkd->bhqd', a.astype(v.dtype), v)

def diff_attn_block(q, k, v, lam, slopes, qpos, kpos, qcid, kcid):
    s = jnp.einsum('bhcqd,bhckd->bhcqk', q, k).astype(jnp.float32) * (DF_HEAD_DIM ** -0.5)
    dist = jnp.abs(qpos[:, None] - kpos[None, :]).astype(jnp.float32)
    bias = -slopes[:, None, None] * dist
    mask = kcid[None, :] <= qcid[:, None]
    s = jnp.where(mask, s + bias[None, :, None], -jnp.inf)
    p = jax.nn.softmax(s, axis=-1)
    w = p[:, :, 0] - lam * p[:, :, 1]
    return jnp.einsum('bhqk,bhkd->bhqd', w.astype(v.dtype), v)

def first_inputs(seed: int = 0) -> dict:
    key = jax.random.key(seed)
    ks = jax.random.split(key, 20)
    f32 = jnp.float32
    nrm = lambda k, shape, scale: (jax.random.normal(k, shape, f32) * scale)
    gain = lambda k, shape: 1.0 + 0.05 * jax.random.normal(k, shape, f32)
    return {
        'x': jax.random.normal(ks[0], (BATCH, SEQ, D_MODEL), f32),
        'meta': nrm(ks[1], (N_META, D_MODEL), 1.0),
        'norm_mix_g': gain(ks[2], (DEPTH, D_MODEL)),
        'w_in': nrm(ks[3], (DEPTH, D_MODEL, IN_W), D_MODEL ** -0.5),
        'w_gate': nrm(ks[4], (DEPTH, D_MODEL, 2 * D_MODEL), D_MODEL ** -0.5),
        'b_gate': nrm(ks[5], (DEPTH, 2 * D_MODEL), 0.1),
        'lam_q1': nrm(ks[6], (DEPTH, DF_HEAD_DIM), 0.1),
        'lam_k1': nrm(ks[7], (DEPTH, DF_HEAD_DIM), 0.1),
        'lam_q2': nrm(ks[8], (DEPTH, DF_HEAD_DIM), 0.1),
        'lam_k2': nrm(ks[9], (DEPTH, DF_HEAD_DIM), 0.1),
        'subln_g': gain(ks[10], (DEPTH, 2 * DF_HEAD_DIM)),
        'w_br_sb': nrm(ks[11], (DEPTH, SB_W, D_MODEL), SB_W ** -0.5),
        'w_br_df': nrm(ks[12], (DEPTH, DF_V_W, D_MODEL), DF_V_W ** -0.5),
        'w_out': nrm(ks[13], (DEPTH, D_MODEL, D_MODEL), D_MODEL ** -0.5),
        'norm_ffn_g': gain(ks[14], (DEPTH, D_MODEL)),
        'w_ffn_gate': nrm(ks[15], (DEPTH, D_MODEL, D_FF), D_MODEL ** -0.5),
        'w_ffn_up': nrm(ks[16], (DEPTH, D_MODEL, D_FF), D_MODEL ** -0.5),
        'w_ffn_down': nrm(ks[17], (DEPTH, D_FF, D_MODEL), D_FF ** -0.5),
        'norm_final_g': gain(ks[18], (D_MODEL,)),
    }

def first_block(x, meta, norm_mix_g, w_in, w_gate, b_gate, lam_q1, lam_k1, lam_q2, lam_k2,
              subln_g, w_br_sb, w_br_df, w_out, norm_ffn_g, w_ffn_gate, w_ffn_up,
              w_ffn_down, norm_final_g):
    B, S, D = x.shape
    L = N_META + S
    L_pad = -(-L // QBLK) * QBLK
    h = jnp.concatenate([
        jnp.broadcast_to(meta[None].astype(x.dtype), (B, N_META, D)),
        x,
        jnp.zeros((B, L_pad - L, D), x.dtype)], axis=1)
    pos = jnp.arange(L_pad)
    cid = jnp.where(pos < N_META, 0, (pos - N_META) // CHUNK + 1)
    slopes = jnp.exp2(-8.0 * (jnp.arange(DF_HEADS) + 1) / DF_HEADS).astype(jnp.float32)
    splits = [SB_W, 2 * SB_W, 3 * SB_W, 3 * SB_W + DF_QK_W, 3 * SB_W + 2 * DF_QK_W]

    for l in range(DEPTH):
        lam_init = 0.8 - 0.6 * math.exp(-0.3 * l)
        xn = rmsnorm(h, norm_mix_g[l])
        proj = xn @ w_in[l]
        sb_q, sb_k, sb_v, df_q, df_k, df_v = jnp.split(proj, splits, axis=-1)
        to_heads = lambda t, nh, dh: t.reshape(B, L_pad, nh, dh).transpose(0, 2, 1, 3)
        sq = to_heads(sb_q, SB_HEADS, SB_HEAD_DIM)
        sk = to_heads(sb_k, SB_HEADS, SB_HEAD_DIM)
        sv = to_heads(sb_v, SB_HEADS, SB_HEAD_DIM)
        dq = df_q.reshape(B, L_pad, DF_HEADS, 2, DF_HEAD_DIM).transpose(0, 2, 3, 1, 4)
        dk = df_k.reshape(B, L_pad, DF_HEADS, 2, DF_HEAD_DIM).transpose(0, 2, 3, 1, 4)
        dv = to_heads(df_v, DF_HEADS, 2 * DF_HEAD_DIM)
        lam = (jnp.exp(jnp.sum(lam_q1[l].astype(jnp.float32) * lam_k1[l].astype(jnp.float32)))
               - jnp.exp(jnp.sum(lam_q2[l].astype(jnp.float32) * lam_k2[l].astype(jnp.float32)))
               + lam_init)

        sb_blocks = []
        df_blocks = []
        for i in range(L_pad // QBLK):
            q0 = i * QBLK
            qe = q0 + QBLK
            lk = min(qe + CHUNK, L_pad)
            sb_blocks.append(stick_breaking_block(
                sq[:, :, q0:qe], sk[:, :, :qe], sv[:, :, :qe], pos[q0:qe], pos[:qe]))
            df_blocks.append(diff_attn_block(
                dq[:, :, :, q0:qe], dk[:, :, :, :lk], dv[:, :, :lk], lam, slopes,
                pos[q0:qe], pos[:lk], cid[q0:qe], cid[:lk]))
        o_sb = jnp.concatenate(sb_blocks, axis=2).transpose(0, 2, 1, 3).reshape(B, L_pad, SB_W)
        o_df = jnp.concatenate(df_blocks, axis=2)
        o_df = (rmsnorm(o_df, subln_g[l]) * (1.0 - lam_init)).transpose(0, 2, 1, 3).reshape(B, L_pad, DF_V_W)

        y_sb = o_sb @ w_br_sb[l]
        y_df = o_df @ w_br_df[l]
        gates = jax.nn.sigmoid(xn @ w_gate[l] + b_gate[l]).reshape(B, L_pad, 2, D)
        merged = gates[:, :, 0] * y_sb + gates[:, :, 1] * y_df
        h = h + merged @ w_out[l]

        hn = rmsnorm(h, norm_ffn_g[l])
        h = h + (jax.nn.silu(hn @ w_ffn_gate[l]) * (hn @ w_ffn_up[l])) @ w_ffn_down[l]

    y = rmsnorm(h, norm_final_g)
    return y[:, N_META:N_META + S]


RET_HEADS = 4
RET_DK = 128
RET_DV = 256
RET_CHUNK = 128
ROPE_BASE = 10000.0
ATT_PATTERNS = ((128, 1), (512, 4), (2048, 16))
ATT_GROUPS = 3
ATT_HEADS_PER_GROUP = 4
ATT_HEADS = ATT_GROUPS * ATT_HEADS_PER_GROUP
ATT_DH = 128
ATT_QBLOCK = 128
REL_BUCKETS = 32
REL_MAX_EXACT = REL_BUCKETS // 2
REL_MAX_DIST = 2048
N_EXPERTS = 32
TOP_K = 4
D_EXPERT = D_MODEL
SWIGLU_LIMIT = 7.0
SWIGLU_ALPHA = 1.702
MOE_BLOCK = 128
GN_EPS = 1e-5

RET_QK_W = RET_HEADS * RET_DK
RET_V_W = RET_HEADS * RET_DV
ATT_W = ATT_HEADS * ATT_DH
ATT_OUT_W = ATT_HEADS_PER_GROUP * ATT_DH
IN_SPLITS = (RET_QK_W, RET_QK_W, RET_V_W, RET_V_W, ATT_W, ATT_W, ATT_W, D_MODEL, D_MODEL)
IN_W_2 = 9728


def _split_points(sizes):
    pts, acc = [], 0
    for s in sizes[:-1]:
        acc += s
        pts.append(acc)
    return pts

def rms_norm(x, g):
    xf = x.astype(jnp.float32)
    return xf * lax.rsqrt(jnp.mean(xf * xf, axis=-1, keepdims=True) + EPS) * g

def modulate(h, shift, scale):
    return h * (1.0 + scale[:, None, :]) + shift[:, None, :]

def rotary(t, pos):
    half = t.shape[-1] // 2
    inv = ROPE_BASE ** (-jnp.arange(half, dtype=jnp.float32) / half)
    ang = pos[:, None] * inv[None, :]
    cos, sin = jnp.cos(ang)[:, None, :], jnp.sin(ang)[:, None, :]
    t1, t2 = t[..., :half], t[..., half:]
    return jnp.concatenate([t1 * cos - t2 * sin, t1 * sin + t2 * cos], axis=-1)

def retention(q, k, v, g):
    B, S = q.shape[:2]
    H, dk, dv, C = RET_HEADS, RET_DK, RET_DV, RET_CHUNK
    nC = S // C
    pos = jnp.arange(S, dtype=jnp.float32)
    q = rotary(q.astype(jnp.float32).reshape(B, S, H, dk), pos)
    k = rotary(k.astype(jnp.float32).reshape(B, S, H, dk), pos) * (dk ** -0.5)
    v = v.astype(jnp.float32).reshape(B, S, H, dv)
    log_g = jnp.log1p(-jnp.exp2(-5.0 - jnp.arange(H, dtype=jnp.float32)))
    i = jnp.arange(C, dtype=jnp.float32)
    diff = i[:, None] - i[None, :]
    decay = jnp.where(diff[None] >= 0, jnp.exp(jnp.maximum(diff, 0.0)[None] * log_g[:, None, None]), 0.0)
    qc = q.reshape(B, nC, C, H, dk)
    kc = k.reshape(B, nC, C, H, dk)
    vc = v.reshape(B, nC, C, H, dv)
    scores = jnp.einsum('bnihd,bnjhd->bnhij', qc, kc) * decay
    inner = jnp.einsum('bnhij,bnjhe->bnihe', scores, vc)
    zeta = jnp.exp((C - 1.0 - i)[:, None] * log_g[None, :])
    kv = jnp.einsum('bnjhd,bnjhe->nbhde', kc * zeta[:, :, None], vc)
    g_chunk = jnp.exp(C * log_g)[None, :, None, None]

    def step(R, kv_n):
        return g_chunk * R + kv_n, R

    _, R_prev = lax.scan(step, jnp.zeros_like(kv[0]), kv)
    xi = jnp.exp((i + 1.0)[:, None] * log_g[None, :])
    cross = jnp.einsum('bnihd,nbhde->bnihe', qc * xi[:, :, None], R_prev)
    y = (inner + cross).reshape(B, S, H, dv)
    mu = jnp.mean(y, axis=-1, keepdims=True)
    var = jnp.mean(jnp.square(y - mu), axis=-1, keepdims=True)
    y = (y - mu) * lax.rsqrt(var + GN_EPS)
    return jax.nn.silu(g.astype(jnp.float32)) * y.reshape(B, S, H * dv)

def t5_bucket(dist):
    is_small = dist < REL_MAX_EXACT
    ratio = jnp.log(jnp.maximum(dist, 1).astype(jnp.float32) / REL_MAX_EXACT) / math.log(REL_MAX_DIST / REL_MAX_EXACT)
    large = REL_MAX_EXACT + (ratio * (REL_BUCKETS - REL_MAX_EXACT)).astype(jnp.int32)
    large = jnp.minimum(large, REL_BUCKETS - 1)
    return jnp.where(is_small, dist, large)

def dilated_attention(q, k, v, rel_bias):
    B, S = q.shape[:2]
    G, Hg, dh, QB = ATT_GROUPS, ATT_HEADS_PER_GROUP, ATT_DH, ATT_QBLOCK
    nb = S // QB
    q = q.reshape(B, S, G, Hg, dh)
    k = k.reshape(B, S, G, Hg, dh)
    v = v.reshape(B, S, G, Hg, dh)
    qb = q.reshape(B, nb, QB, G, Hg, dh).transpose(1, 0, 2, 3, 4, 5)
    ks = [k[:, :, g] for g in range(G)]
    vs = [v[:, :, g] for g in range(G)]
    biases = []
    for g, (w, r) in enumerate(ATT_PATTERNS):
        nk = w // r + 1
        bkt = t5_bucket(r * jnp.arange(nk, dtype=jnp.int32))
        biases.append(rel_bias[bkt, g * Hg:(g + 1) * Hg].T.astype(jnp.float32))
    scale = dh ** -0.5

    def block(args):
        n, qn = args
        pos = n * QB + jnp.arange(QB, dtype=jnp.int32)
        outs, lses = [], []
        for g, (w, r) in enumerate(ATT_PATTERNS):
            nk = w // r + 1
            idx = pos[:, None] - r * jnp.arange(nk, dtype=jnp.int32)[None, :]
            valid = idx >= 0
            idc = jnp.maximum(idx, 0)
            kg = jnp.take(ks[g], idc, axis=1)
            vg = jnp.take(vs[g], idc, axis=1)
            s = jnp.einsum('bqhd,bqjhd->bhqj', qn[:, :, g], kg).astype(jnp.float32) * scale
            s = s + biases[g][:, None, :]
            s = jnp.where(valid[None, None], s, -jnp.inf)
            m = jnp.max(s, axis=-1, keepdims=True)
            e = jnp.exp(s - m)
            l = jnp.sum(e, axis=-1, keepdims=True)
            o = jnp.einsum('bhqj,bqjhd->bqhd', e / l, vg.astype(jnp.float32))
            outs.append(o)
            lses.append((m + jnp.log(l))[..., 0].transpose(0, 2, 1))
        alpha = jax.nn.softmax(jnp.stack(lses, axis=0), axis=0)
        out = alpha[0][..., None] * outs[0]
        for g in range(1, G):
            out = out + alpha[g][..., None] * outs[g]
        return out

    out = lax.map(block, (jnp.arange(nb, dtype=jnp.int32), qb))
    return out.transpose(1, 0, 2, 3, 4).reshape(B, S, Hg * dh)

def moe(h, w_router, b_router, w1, b1, w2, b2):
    B, S, D = h.shape
    T = B * S
    xf = h.reshape(T, D)
    logits = (xf @ w_router + b_router).astype(jnp.float32)
    top_val, top_idx = lax.top_k(logits, TOP_K)
    gates = jax.nn.softmax(top_val, axis=-1)
    A = T * TOP_K
    flat_e = top_idx.reshape(A).astype(jnp.int32)
    flat_tok = jnp.arange(A, dtype=jnp.int32) // TOP_K
    flat_gate = gates.reshape(A)
    order = jnp.argsort(flat_e, stable=True)
    se = flat_e[order]
    counts = jnp.bincount(flat_e, length=N_EXPERTS)
    starts = jnp.cumsum(counts) - counts
    padded = (counts + MOE_BLOCK - 1) // MOE_BLOCK * MOE_BLOCK
    pend = jnp.cumsum(padded)
    pstart = pend - padded
    dest = pstart[se] + jnp.arange(A, dtype=jnp.int32) - starts[se]
    nblk = -(-A // MOE_BLOCK) + N_EXPERTS
    n_rows = nblk * MOE_BLOCK
    row_tok = jnp.full((n_rows,), T, jnp.int32).at[dest].set(flat_tok[order])
    row_gate = jnp.zeros((n_rows,), jnp.float32).at[dest].set(flat_gate[order])
    block_e = jnp.minimum(jnp.searchsorted(pend, jnp.arange(nblk, dtype=jnp.int32) * MOE_BLOCK, side='right'), N_EXPERTS - 1)
    x_pad = jnp.concatenate([xf, jnp.zeros((1, D), xf.dtype)], axis=0)
    xin = x_pad[row_tok].reshape(nblk, MOE_BLOCK, D)

    def expert_block(args):
        xb, e = args
        u = xb @ w1[e] + b1[e]
        glu = jnp.minimum(u[:, ::2], SWIGLU_LIMIT)
        lin = jnp.clip(u[:, 1::2], -SWIGLU_LIMIT, SWIGLU_LIMIT)
        a = glu * jax.nn.sigmoid(SWIGLU_ALPHA * glu) * (lin + 1.0)
        return a @ w2[e] + b2[e]

    yb = lax.map(expert_block, (xin, block_e)).reshape(n_rows, D)
    y = jnp.zeros((T + 1, D), jnp.float32).at[row_tok].add(yb.astype(jnp.float32) * row_gate[:, None])
    return y[:T].reshape(B, S, D)

def second_inputs(seed: int = 0) -> dict:
    key = jax.random.key(seed)
    ks = jax.random.split(key, 20)
    D, L, E, F = D_MODEL, DEPTH, N_EXPERTS, D_EXPERT
    nrm = jax.random.normal
    f32 = jnp.float32
    return {
        "x": nrm(ks[0], (BATCH, SEQ, D), f32),
        "c": nrm(ks[1], (BATCH, D), f32),
        "w_ada": nrm(ks[2], (L, D, 6 * D), f32) * (0.5 * D ** -0.5),
        "b_ada": nrm(ks[3], (L, 6 * D), f32) * 0.02,
        "g_mix": 1.0 + 0.02 * nrm(ks[4], (L, D), f32),
        "w_in": nrm(ks[5], (L, D, IN_W_2), f32) * D ** -0.5,
        "rel_bias": nrm(ks[6], (REL_BUCKETS, ATT_HEADS), f32) * 0.2,
        "w_ret_o": nrm(ks[7], (L, RET_V_W, D), f32) * RET_V_W ** -0.5,
        "w_att_o": nrm(ks[8], (L, ATT_OUT_W, D), f32) * ATT_OUT_W ** -0.5,
        "w_o": nrm(ks[9], (L, D, D), f32) * D ** -0.5,
        "g_ffn": 1.0 + 0.02 * nrm(ks[10], (L, D), f32),
        "w_router": nrm(ks[11], (L, D, E), f32) * D ** -0.5,
        "b_router": nrm(ks[12], (L, E), f32) * 0.01,
        "w_mlp1": nrm(ks[13], (L, E, D, 2 * F), f32) * D ** -0.5,
        "b_mlp1": nrm(ks[14], (L, E, 2 * F), f32) * 0.01,
        "w_mlp2": nrm(ks[15], (L, E, F, D), f32) * F ** -0.5,
        "b_mlp2": nrm(ks[16], (L, E, D), f32) * 0.01,
        "g_final": 1.0 + 0.02 * nrm(ks[17], (D,), f32),
    }

def second_block(x, c, w_ada, b_ada, g_mix, w_in, rel_bias, w_ret_o, w_att_o, w_o, g_ffn,
              w_router, b_router, w_mlp1, b_mlp1, w_mlp2, b_mlp2, g_final):
    cs = jax.nn.silu(c.astype(jnp.float32))
    pts = _split_points(IN_SPLITS)
    for l in range(DEPTH):
        mod = cs @ w_ada[l] + b_ada[l]
        sh_a, sc_a, gt_a, sh_f, sc_f, gt_f = jnp.split(mod, 6, axis=-1)
        h = modulate(rms_norm(x, g_mix[l]), sh_a, sc_a)
        u = h @ w_in[l]
        rq, rk, rv, rg, aq, ak, av, ga, gb = jnp.split(u, pts, axis=-1)
        ret = retention(rq, rk, rv, rg)
        att = dilated_attention(aq, ak, av, rel_bias)
        merged = jax.nn.sigmoid(ga) * (ret @ w_ret_o[l]) + jax.nn.sigmoid(gb) * (att @ w_att_o[l])
        x = x + gt_a[:, None, :] * (merged @ w_o[l])
        h = modulate(rms_norm(x, g_ffn[l]), sh_f, sc_f)
        x = x + gt_f[:, None, :] * moe(h, w_router[l], b_router[l], w_mlp1[l], b_mlp1[l], w_mlp2[l], b_mlp2[l])
    return rms_norm(x, g_final)


def setup_inputs(seed=0):
    out = dict(first_inputs(seed))
    for name, value in second_inputs(seed + 1).items():
        if name != "x":
            out[name + "_2"] = value
    return out


def reference(
    x, meta, norm_mix_g, w_in, w_gate, b_gate, lam_q1, lam_k1, lam_q2, lam_k2, subln_g, w_br_sb,
    w_br_df, w_out, norm_ffn_g, w_ffn_gate, w_ffn_up, w_ffn_down, norm_final_g, c_2, w_ada_2,
    b_ada_2, g_mix_2, w_in_2, rel_bias_2, w_ret_o_2, w_att_o_2, w_o_2, g_ffn_2, w_router_2,
    b_router_2, w_mlp1_2, b_mlp1_2, w_mlp2_2, b_mlp2_2, g_final_2,
):
    x = first_block(
        x, meta, norm_mix_g, w_in, w_gate, b_gate, lam_q1, lam_k1, lam_q2, lam_k2, subln_g,
        w_br_sb, w_br_df, w_out, norm_ffn_g, w_ffn_gate, w_ffn_up, w_ffn_down, norm_final_g,
    )
    return second_block(
        x, c_2, w_ada_2, b_ada_2, g_mix_2, w_in_2, rel_bias_2, w_ret_o_2, w_att_o_2, w_o_2,
        g_ffn_2, w_router_2, b_router_2, w_mlp1_2, b_mlp1_2, w_mlp2_2, b_mlp2_2, g_final_2,
    )


_drawn_inputs = setup_inputs


def setup_inputs(seed=0):
    import zlib

    import numpy as np

    out = dict(_drawn_inputs(seed))
    spreads = {}
    factors = {'lam_q1': 3.159,
     'lam_k2': 6.636,
     'g_mix_2': 4.868,
     'rel_bias_2': 4.562,
     'g_ffn_2': 3.333,
     'b_router_2': 10.583,
     'b_mlp1_2': 8.0,
     'b_mlp2_2': 63.818,
     'g_final_2': 8.156}
    for name, (base, spread) in spreads.items():
        noise = np.random.default_rng([zlib.crc32(name.encode()), seed]).standard_normal(out[name].shape)
        drawn = base * np.exp(spread * noise) if base else spread * noise
        out[name] = __import__('jax').numpy.asarray(drawn.astype(out[name].dtype))
    for name, factor in factors.items():
        out[name] = (out[name] * factor).astype(out[name].dtype)
    return out
```

```python
from contextlib import ExitStack

import concourse.bass as bass
import numpy as np
from concourse import mybir

F32 = mybir.dt.float32
U32 = mybir.dt.uint32
I32 = mybir.dt.int32
ALU = mybir.AluOpType
ACT = mybir.ActivationFunctionType
AX = mybir.AxisListType

P = 128
D = 1024
KT = D // P
T = 256
M = 16
TM = T + M
HEADS = 8
FF = 2816
FT = FF // P
E = 32
CAP = 64
RH = 4
GROUPS = 3
SLOTS = 4
DIL = ((128, 1), (512, 4), (2048, 16))
TOEP = 384
EPS = 1e-6
GN_EPS = 1e-5
LAM_INIT = 0.2
SB_SCALE = 128 ** -0.5
NEG = -1e30

VEC_ROWS = (("norm_mix_g", 8), ("b_gate", 16), ("norm_ffn_g", 8), ("norm_final_g", 8), ("c", 8), ("b_ada", 48),
            ("g_mix", 8), ("g_ffn", 8), ("g_final", 8), ("subln_g", 1))
VROW = {}
for _name, _n in VEC_ROWS:
    VROW[_name] = sum(n for _, n in VEC_ROWS[:len(VROW)])
NVEC = sum(n for _, n in VEC_ROWS)

C_ID, C_NTRI, C_TRI, C_NEGM, C_SWAP, C_IOTA, C_IE, C_DIST = 0, 128, 256, 384, 512, 640, 768, 800
NCST = C_DIST + 416


def constants():
    f = np.float32
    i = np.arange(P)
    cst = np.zeros((P, NCST), f)
    cst[:, C_ID:C_ID + P] = np.eye(P)
    cst[:, C_NTRI:C_NTRI + P] = -(i[:, None] >= i[None, :]).astype(f)
    cst[:, C_TRI:C_TRI + P] = (i[:, None] < i[None, :])
    cst[:, C_NEGM:C_NEGM + P] = np.where(i[:, None] < i[None, :], 0, NEG)
    cst[:, C_SWAP:C_SWAP + P] = np.eye(P)[(i + 64) % P]
    cst[:, C_IOTA:C_IOTA + P] = np.where(i % 64 < CAP, i % 64, -9)[None, :]
    cst[:, C_IE:C_IE + E] = np.arange(E)[None, :]
    keys = np.arange(TM)
    for qt in range(2):
        q = M + P * qt + i
        n = M + P * (qt + 1)
        cid = lambda t: np.where(t < M, 0, (t - M) // 64 + 1)
        dist = np.where(cid(keys[:n])[None, :] <= cid(q)[:, None], -np.abs(q[:, None] - keys[None, :n]), NEG)
        at = C_DIST + (M + P) * qt
        cst[:, at:at + n] = dist
    tab = np.zeros((P, 6, T), f)
    t = np.arange(T, dtype=f)
    logg = np.log1p(-np.exp2(-5.0 - np.arange(RH, dtype=f))).astype(f)
    diff = t[None, :] - i[:, None].astype(f)
    for h in range(RH):
        tab[:, h] = np.where(diff >= 0, np.exp(np.maximum(diff, 0).astype(f) * logg[h]), 0)
    inv = (f(10000.0) ** (-np.arange(64, dtype=f) / f(64))).astype(f)
    ang = (t[None, :] * inv[i % 64][:, None]).astype(f)
    tab[:, 4] = np.cos(ang)
    tab[:, 5] = np.sin(ang) * np.where(i < 64, -1, 1)[:, None]
    hot = np.zeros((E, GROUPS, TOEP), f)
    bad = np.zeros((SLOTS, GROUPS, TOEP), f)
    for g, (w, r) in enumerate(DIL):
        for n in range(TOEP):
            dist = 255 - n
            if dist < 0 or dist % r or dist > w:
                bad[:, g, n] = NEG
                continue
            if dist < 16:
                b = dist
            else:
                ratio = np.log(f(dist) / f(16)) / f(np.log(128.0))
                b = min(16 + int(f(ratio) * 16), 31)
            hot[b, g, n] = 1
    return cst, tab, hot, bad


def group_list(pieces):
    out = []
    for p, (kind, count, part) in enumerate(pieces):
        out += [(p, kind, n, count * part + n) for n in range(count)]
    return out


PIECES1 = ([(side + kind, n, i) for side in "sd" for i in range(2) for kind, n in (("q", 4), ("k", 4), ("v", 3))]
           + [("gate", 4, i) for i in range(4)]
           + [(k, 4, i) for k in ("ysb", "ydf", "out") for i in range(2)])
COL1 = {"sq": 0, "sk": 2, "sv": 4, "dq": 6, "dk": 8, "dv": 10}
PIECES2 = ([("rq", 4, 0), ("rk", 4, 0)] + [("rv", 2, i) for i in range(2)] + [("rg", 4, i) for i in range(2)]
           + [(k, n, i) for k, n in (("aq", 4), ("ak", 4), ("av", 2)) for i in range(3)]
           + [("gab", 4, i) for i in range(4)] + [("yret", 4, i) for i in range(2)] + [("yatt", 8, 0)]
           + [("o", 4, i) for i in range(2)])
GR1, GR2 = group_list(PIECES1), group_list(PIECES2)
DVE_KINDS = ("rg", "ysb", "ydf", "out", "yret", "yatt", "o")


def where(groups, kind, c=0):
    return next(g for g, x in enumerate(groups) if x[1] == kind and x[3] == c)


def first_of(groups, kind):
    return where(groups, kind)


def last_of(groups, kind):
    return max(g for g, x in enumerate(groups) if x[1] == kind)


def evac(groups, g):
    dve = groups[g][1] in DVE_KINDS
    return dve, sum((x[1] in DVE_KINDS) == dve for x in groups[:g + 1])


def weave(groups, *chains):
    timed = [(g, 1, 0, "G", g) for g in range(len(groups))]
    for start, period, heads, steps in chains:
        for h in range(heads):
            timed += [(start + period * h + at, 0, -h, s, h) for s, at in steps.items()]
    return [x[3:] for x in sorted(timed, key=lambda x: x[0:3])]


def order1():
    return weave(GR1, (SB_AT, 3, HEADS, {"sbA": 0, "sbB": 2, "sbC": 3}),
                 (SB_AT + 3 * HEADS + 1, 3, HEADS, {"dfA": 0, "dfB": 2, "dfC": 3, "dfD": 4}))


def order2():
    ga = first_of(GR2, "av")
    return weave(GR2, (12, 1, 2, {"rot": 0}), (14, 3, RH, {"rtA": 0, "rtB": 1, "rtC": 2, "rtD": 3}),
                 (ga + 3, 3, SLOTS, {"dlA": 0, "dlB": 2, "dlC": 3}))


SB_AT = 11
ORDER1, ORDER2 = order1(), order2()


class Count:

    def __init__(self, eng, sem):
        self.eng, self.sem, self.n = eng, sem, 0

    def do(self, ins):
        ins.then_inc(self.sem, 1)
        self.n += 1
        return self.n

    def wait(self, n=None):
        self.eng.wait_ge(self.sem, self.n if n is None else n)


def program(nc, a, ctx):
    def sb(name, shape, dt=F32):
        return ctx.enter_context(nc.sbuf_tensor("s_" + name, shape, dt))

    def sem(name):
        return ctx.enter_context(nc.semaphore(name))

    def area(base, at, *dims):
        n = 1
        for d in dims:
            n *= d
        v = base[:, at:at + n]
        return v.rearrange("p (a b) -> p a b", a=dims[0]) if len(dims) == 2 else v

    ring = sb("ring", [P, 6, 4096])
    hT = sb("hT", [P, KT, TM])
    cst = sb("cst", [P, NCST])
    ones = sb("ones", [P, P])
    nones = sb("nones", [P, P])
    vec = sb("vec", [P, NVEC])
    vx = sb("vx", [P, 64])
    sml = sb("sml", [P, 64])
    modT = sb("modT", [P, 48])
    W = sb("W", [P, 23680])
    taken = sml[:, 40:41]
    rks = sml[:, 42:44]
    topi = sb("topi", [P, 2, 8], U32)
    cnti = sb("cnti", [1, E + 1], I32)
    cntf = sb("cntf", [1, E + 1])
    banks = ctx.enter_context(nc.psum_tensor("banks", [P, 8, 512], F32))
    pb = [banks[:, n, :] for n in range(8)]
    hx = hT[:, :, M:TM]
    lent = ring[:, 0:3, :].rearrange("p a b -> p (a b)")
    ident = cst[:, C_ID:C_ID + P]
    ntri = cst[:, C_NTRI:C_NTRI + P]
    tri = cst[:, C_TRI:C_TRI + P]
    negm = cst[:, C_NEGM:C_NEGM + P]
    swap = cst[:, C_SWAP:C_SWAP + P]
    iotac = cst[:, C_IOTA:C_IOTA + P]
    iotae = cst[:, C_IE:C_IE + E]
    distt = cst[:, C_DIST:C_DIST + 416]
    nbg, gsub, lamc = vx[:, 0:16], vx[:, 16:17], vx[:, 17:20]
    gsa, gsf, epsc, gnepsc = vx[:, 20:28], vx[:, 28:36], vx[:, 36:37], vx[:, 37:38]
    onec = vx[:, 38:39]

    def two(ap):
        return ap[:, 0:512].rearrange("p (a b) -> p a b", a=2)[:, :, 0:P]

    def bc(ap, n):
        return ap.unsqueeze(1).broadcast_to([ap.shape[0], n, ap.shape[1]])

    xtok = area(lent, 8192, 2, D)
    mtok = lent[0:M, 4096:4096 + D]
    vrow = lent[0:NVEC, 5120:5248]
    lamv = area(lent, 5376, 4, 64)
    sqa = area(lent, 0, KT, TM)
    rms = lent[:, 2176:2176 + TM]
    xn = area(W, 0, KT, TM)
    sqT = area(W, 2176, HEADS, T)
    skT = area(W, 4224, HEADS, TM)
    sv = area(W, 6400, 3, D)
    dqT = area(W, 9472, HEADS, T)
    dkT = area(W, 11520, HEADS, TM)
    dv = area(W, 13696, 3, D)
    gate = area(W, 16768, 16, T)
    mT = area(W, 20864, KT, T)
    zs, ex, sp, la = (lent[:, 640 * n:640 * n + 640] for n in range(4))
    sc = area(lent, 2560, 2, 416)
    wv = lent[:, 3392:3392 + 416]
    wT = lent[:, 3808:4448]
    osq = lent[:, 4448:4704]
    ors = lent[:, 4704:4960]
    dtmp = lent[:, 4960:5216]
    xf = area(W, 0, KT, T)
    fT = area(W, 2176, FT, T)
    fe = area(lent, 4096, 2, T)
    fr = area(lent, 4608, 2, T)
    adac = area(lent, 5120, 2, 512)
    xn2 = area(W, 0, KT, T)
    m2T = xn2
    rqT = area(W, 2048, RH, T)
    rkT = area(W, 3072, RH, T)
    rv = area(W, 4096, 2, D)
    rg = area(W, 6144, KT, T)
    aqT = area(W, 8192, 12, T)
    akT = area(W, 11264, 12, T)
    av = area(W, 14336, 2, 1536)
    gab = area(W, 17408, 16, T)
    attT = area(W, 21504, SLOTS, T)
    bad = W[0:SLOTS, 22528:22528 + GROUPS * TOEP].rearrange("p (a b) -> p a b", a=GROUPS)
    raw = area(lent, 2560, 2, 1024)
    tab = area(lent, 4608, 6, T)
    BT = area(lent, 6144, 12, T)
    pT = lent[:, 9216:9600]
    ys = area(lent, 9600, 2, T)
    yq = area(lent, 10112, 2, T)
    yr = lent[:, 10624:10880]
    rsg = area(lent, 10880, 2, T)
    ds = lent[:, 0:1152]
    dwT = lent[:, 1152:2304]
    stg = lent[0:SLOTS, 9216:9216 + GROUPS * TOEP].rearrange("p (a b) -> p a b", a=GROUPS)
    hot = lent[0:E, 10368:10368 + GROUPS * TOEP].rearrange("p (a b) -> p a b", a=GROUPS)
    relb = lent[0:E, 11520:11532]
    dtmp2 = W[:, 8192:8448]
    hn = area(W, 0, KT, T)
    htok = area(W, 2048, 2, D)
    acc = area(W, 4096, KT, T)
    selU = area(W, 6144, 2, 64)
    selG = area(W, 6272, 2, P)
    selT = W[:, 6528:6784]
    XgT = area(W, 6784, KT, 64)
    gl = W[:, 7296:7808]
    li = W[:, 7808:8320]
    sg = W[:, 8320:8832]
    aa = W[:, 8832:9344]
    aT = area(W, 9344, 4, P)
    yv = W[:, 9856:10368]
    b1p = W[:, 10368:12416]
    wr = area(W, 12416, KT, E)
    b2s = W[0:E, 12672:13696]
    brow = W[:, 13696:13728]
    lg = area(W, 13728, 2, E)
    top8 = area(W, 13792, 2, 8)
    tif = area(W, 13824, 2, 8)
    gts = area(W, 13840, 2, 8)
    one = area(W, 13856, 2, E)
    msk = area(W, 13920, 2, E)
    gat = area(W, 13984, 2, E)
    rank = area(W, 18720, 2, E + 1)
    gatT = W[0:E, 14112:14368]
    otok = area(W, 14368, 2, D)
    nsq = area(W, 16416, KT, T)
    nrms = W[:, 18464:18720]

    S = {n: sem(n) for n in (
        "x_in", "vec_in", "cst_in", "lam_in", "tab_in", "hot_in", "toep_out", "toep_in", "moe_in", "b1_in", "stored",
        "x_turned", "x_kept", "vec_turned", "vec_kept", "filled", "lam_sum", "lam_exp", "lam_done",
        "norm_sq", "norm_ms", "norm_r", "norm_x", "norm_s",
        "gemm1", "act_evac1", "dve_evac1", "gate_done", "gemm2", "act_evac2", "dve_evac2", "gab_done", "rg_exp",
        "sb_scores", "sb_zs", "sb_min", "sb_ln", "sb_sp", "sb_rest", "sb_la", "sb_a", "sb_o", "sb_out",
        "df_scores", "df_s", "df_max", "df_exp", "df_w", "df_tr", "df_wt", "df_o", "df_sq", "df_ms", "df_rs", "df_out",
        "up", "up_free", "up_exp", "up_out", "up_step", "ada_step", "ada_sum", "ada_mm", "down", "down_out", "mod_done", "toep_mm", "toep_sum",
        "rot_mm", "rot_out", "rt_s", "rt_p", "rt_y", "rt_ys", "rt_m", "rt_yc", "rt_sq", "rt_v", "rt_r", "rt_out",
        "dl_s", "dl_b", "dl_max", "dl_e", "dl_p", "dl_t", "dl_wt", "dl_o", "dl_out",
        "act_step", "dve_step", "ht_mm", "ht_kept", "log_mm", "log_exp", "route", "rank_mm", "rank_done",
        "gt_mm", "gt_kept", "b2_mm", "acc_init",
        "selu", "selg", "selt_mm", "selt", "gath", "xg", "u_mm", "u_read", "u_sig", "a_mid", "a_done", "at_mm", "at", "y_mm", "yv_done",
        "sc_mm", "acc_done", "moe_dve",
        "over_in", "over_pe", "over_act", "over_dve", "round", "final_sum", "fin_mm", "fin_kept")}
    in1 = [sem(f"piece1_in{b}") for b in range(2)]
    inu = [sem(f"up_in{b}") for b in range(2)]
    ina = [sem(f"ada_in{b}") for b in range(2)]
    ind = [sem(f"down_in{b}") for b in range(2)]
    in2 = [sem(f"piece2_in{b}") for b in range(2)]
    inw = [sem(f"expert_in{b}") for b in range(6)]

    w_in, w_gate, w_in2 = a["w_in"][0], a["w_gate"][0], a["w_in_2"][0]

    def cols(w, c):
        return w[:, 512 * c:512 * c + 512].rearrange("(k p) n -> p k n", p=P)

    pieces1 = ([cols(w_in, COL1[kind] + part) for kind, _, part in PIECES1[:12]] + [cols(w_gate, c) for c in range(4)]
               + [cols(a[n][0], c) for n in ("w_br_sb", "w_br_df", "w_out") for c in range(2)])
    pieces2 = ([cols(w_in2, c) for c in range(19)] + [cols(a["w_ret_o_2"][0], c) for c in range(2)]
               + [a["w_att_o_2"][0].rearrange("(k p) n -> p k n", p=P)] + [cols(a["w_o_2"][0], c) for c in range(2)])
    up_g, up_u, down, w_ada = (a[n][0] for n in ("w_ffn_gate", "w_ffn_up", "w_ffn_down", "w_ada_2"))
    w1, w2 = a["w_mlp1_2"][0], a["w_mlp2_2"][0]
    ends1 = [max(g for g, x in enumerate(GR1) if x[0] == p) + 1 for p in range(len(PIECES1))]
    ends2 = [max(g for g, x in enumerate(GR2) if x[0] == p) + 1 for p in range(len(PIECES2))]
    UPS, ADAS = FF // T, 12
    DOWNS = [4, 4, 4, 4, 4, 2]

    def slot(n, k=KT):
        return ring[:, n, :].rearrange("p (k n) -> p k n", k=k)

    def since(eng, name, n):
        if not isinstance(n, int) or n > 0:
            eng.wait_ge(S[name], n)

    def further(eng, each, begin=None):
        eng.wait_ge(S["rank_done"], 1)
        most = eng.value_load(cnti[0:1, E:E + 1], min_val=0, max_val=T)
        with eng.If(most > CAP):
            done = eng.alloc_register("passes")
            eng.reg_mov(done, 0)
            with eng.Fori(1, T // CAP) as r:
                if begin is not None:
                    begin(r)
                with eng.Fori(0, E) as e:
                    here = eng.value_load(cnti[0:1, bass.ds(e, 1)], min_val=0, max_val=T)
                    with eng.If(here > r * CAP):
                        each(e, eng.snap(done), r)
                        eng.reg_add(done, done, 1)

    block = ctx.enter_context(nc.Block())

    @block.sync
    def _(sp):
        def piece1(p):
            if p >= 2:
                sp.wait_ge(S["gemm1"], ends1[p - 2])
            sp.dma_start(slot(4 + p % 2), pieces1[p]).then_inc(in1[p % 2], 16)

        sp.dma_start(xtok, a["x"][0].rearrange("(a p) d -> p a d", p=P)).then_inc(S["x_in"], 16)
        sp.dma_start(mtok, a["meta"]).then_inc(S["x_in"], 16)
        for p in range(len(pieces1)):
            piece1(p)

        def up(j, b):
            src = [w[:, bass.ds(j * T, T)].rearrange("(k p) n -> p k n", p=P) for w in (up_g, up_u)]
            sp.dma_start(slot(4 + b)[:, :, 0:T], src[0]).then_inc(inu[b], 16)
            sp.dma_start(slot(4 + b)[:, :, T:512], src[1]).then_inc(inu[b], 16)

        def ada(j, b):
            sp.dma_start(slot(2 + b), w_ada[:, bass.ds(j * 512, 512)].rearrange("(k p) n -> p k n", p=P))\
              .then_inc(ina[b], 16)

        for b in range(2):
            sp.wait_ge(S["gemm1"], ends1[len(pieces1) - 2 + b])
            up(b, b)
            ada(b, b)
        with sp.Fori(1, UPS // 2) as i:
            for b in range(2):
                sp.wait_ge(S["up"], i * 8 + (4 * b - 4))
                up(i * 2 + b, b)
                sp.wait_ge(S["ada_sum"], i * 2 + (b - 1))
                ada(i * 2 + b, b)
        sp.wait_ge(S["up"], 4 * (UPS - 2))
        up(UPS - 1, 0)
        for b in range(2):
            sp.wait_ge(S["ada_sum"], ADAS - 3 + b)
            ada(ADAS - 2 + b, b)
        for j, k in enumerate(DOWNS):
            if j < 2:
                sp.wait_ge(S["up"], 4 * (UPS - 1 + j))
            else:
                sp.wait_ge(S["down"], j - 1)
            b = (j + 1) % 2
            sp.dma_start(slot(4 + b, 4)[:, 0:k, :], down[512 * j:512 * j + P * k, :].rearrange("(k p) n -> p k n", p=P))\
              .then_inc(ind[b], 16)

        def piece2(p):
            if p < 2:
                sp.wait_ge(S["down"], 5 + 4 * p)
            else:
                sp.wait_ge(S["gemm2"], ends2[p - 2])
            k = 4 if PIECES2[p][0] == "yatt" else KT
            sp.dma_start(slot(5 - p % 2, k), pieces2[p]).then_inc(in2[p % 2], 16)

        for p in range(len(pieces2)):
            if p == len(pieces2) - 2:
                sp.wait_ge(S["dl_out"], SLOTS)
                sp.wait_ge(S["rt_out"], RH)
                for c in range(4):
                    sp.dma_start(slot(c, 2), w1[0, T * c:T * c + T, :].rearrange("(k p) n -> p k n", p=P))\
                      .then_inc(inw[c], 16)
            piece2(p)

        def first(e, c):
            sp.dma_start(slot(c, 2), w1[bass.ds(e, 1), T * c:T * c + T, :].rearrange("e (k p) n -> p (e k) n", p=P))\
              .then_inc(inw[c], 16)

        def second(e, c):
            sp.dma_start(slot(4 + c, 4), w2[bass.ds(e, 1), 512 * c:512 * c + 512, :].rearrange("e (k p) n -> p (e k) n", p=P))\
              .then_inc(inw[4 + c], 16)

        def bias(e):
            sp.dma_start(b1p[0:1, :], a["b_mlp1_2"][0, bass.ds(e, 1), :]).then_inc(S["b1_in"], 16)

        sp.wait_ge(S["filled"], 2)
        bias(0)
        sp.wait_ge(S["gemm2"], ends2[len(pieces2) - 1])

        def load(e):
            for c in range(2):
                sp.wait_ge(S["u_mm"], e * 5 + (c - 4))
                first(e, c)
            since(sp, "y_mm", e * 2 - 2)
            for c in range(2):
                second(e - 1, c)
            for c in range(2, 4):
                sp.wait_ge(S["u_mm"], e * 5 + (c - 4))
                first(e, c)
            sp.wait_ge(S["u_mm"], e * 5)
            bias(e)

        load(1)
        with sp.Fori(2, E) as e:
            load(e)
        sp.wait_ge(S["y_mm"], 2 * E - 2)
        for c in range(2):
            second(E - 1, c)

        def again(e, n, r):
            sp.wait_ge(S["over_pe"], n * 7 + 1)
            for c in range(4):
                sp.dma_start(slot(c, 2), w1[bass.ds(e, 1), T * c:T * c + T, :].rearrange("e (k p) n -> p (e k) n", p=P))\
                  .then_inc(S["over_in"], 16)
            for c in range(2):
                sp.dma_start(slot(4 + c, 4), w2[bass.ds(e, 1), 512 * c:512 * c + 512, :].rearrange("e (k p) n -> p (e k) n", p=P))\
                  .then_inc(S["over_in"], 16)
            sp.dma_start(b1p[0:1, :], a["b_mlp1_2"][0, bass.ds(e, 1), :]).then_inc(S["over_in"], 16)

        sp.wait_ge(S["y_mm"], 2 * E)
        further(sp, again)
        sp.wait_ge(S["fin_kept"], 4)
        sp.dma_start(a["out"][0].rearrange("(a p) d -> p a d", p=P), otok).then_inc(S["stored"], 16)
        sp.wait_ge(S["stored"], 16)

    @block.gpsimd
    def _(pool):
        pool.memset(ones[:, :], 1.0)
        pool.memset(nones[:, :], -1.0)
        pool.memset(epsc, EPS)
        pool.memset(gnepsc, GN_EPS)
        pool.memset(onec, 1.0).then_inc(S["filled"], 1)
        row = 0
        src = {"norm_mix_g": a["norm_mix_g"], "b_gate": a["b_gate"], "norm_ffn_g": a["norm_ffn_g"],
               "norm_final_g": a["norm_final_g"].unsqueeze(0), "c": a["c_2"], "b_ada": a["b_ada_2"], "g_mix": a["g_mix_2"],
               "g_ffn": a["g_ffn_2"], "g_final": a["g_final_2"].unsqueeze(0), "subln_g": a["subln_g"]}
        for name, n in VEC_ROWS:
            pool.dma_start(vrow[row:row + n, :], src[name].rearrange("a (r p) -> (a r) p", p=P)).then_inc(S["vec_in"], 16)
            row += n
        pool.dma_start(cst[:, :], a["cst"]).then_inc(S["cst_in"], 16)
        for n, name in enumerate(("lam_q1", "lam_q2", "lam_k1", "lam_k2")):
            pool.dma_start(lamv[:, n, :], a[name].partition_broadcast(P)).then_inc(S["lam_in"], 16)
        pool.wait_ge(S["up_free"], FT + 2)
        pool.wait_ge(S["ada_mm"], ADAS + 2)
        pool.wait_ge(S["norm_x"], 16)
        pool.dma_start(hot, a["hot"]).then_inc(S["hot_in"], 16)
        pool.dma_start(bad, a["bad"]).then_inc(S["hot_in"], 16)
        pool.dma_start(relb, a["rel_bias_2"]).then_inc(S["hot_in"], 16)
        pool.dma_start(tab, a["tab"]).then_inc(S["tab_in"], 16)
        pool.wait_ge(S["toep_sum"], GROUPS)
        pool.dma_start(a["toep"].rearrange("(g s) n -> s g n", g=GROUPS), stg).then_inc(S["toep_out"], 16)
        pool.wait_ge(S["toep_out"], 16)
        n = GROUPS * SLOTS * TOEP
        pool.dma_start(a["toeps"], bass.AP(a["toep"].tensor, 0, [[0, P], [1, n]])).then_inc(S["toep_out"], 16)
        pool.wait_ge(S["toep_out"], 32)
        pool.dma_start(BT, bass.AP(a["toeps"].tensor, P - 1, [[n - 1, P], [TOEP, GROUPS * SLOTS], [1, T]]))\
            .then_inc(S["toep_in"], 16)
        pool.wait_ge(S["dl_out"], SLOTS)
        pool.memset(b1p, 0.0).then_inc(S["filled"], 1)
        pool.dma_start(wr, a["w_router_2"][0].rearrange("(k p) e -> p k e", p=P)).then_inc(S["moe_in"], 16)
        pool.dma_start(b2s, a["b_mlp2_2"][0]).then_inc(S["moe_in"], 16)
        pool.dma_start(brow, a["b_router_2"].partition_broadcast(P)).then_inc(S["moe_in"], 16)

    @block.scalar
    def _(act):
        st = Count(act, S["act_step"])

        def norm(k, src, buf, r, n):
            for half in range(2):
                act.activation(buf[:, 4 * half:4 * half + 4, 0:n], src[:, 4 * half:4 * half + 4, :], ACT.Square)\
                   .then_inc(S["norm_sq"], 1)
            act.wait_ge(S["norm_ms"], k + 1)
            st.do(act.activation(r[:, 0:n], pb[3][:, 0:n], ACT.Ln, bias=epsc, scale=1.0 / D))
            st.wait()
            act.activation(r[:, 0:n], r[:, 0:n], ACT.Exp, scale=-0.5).then_inc(S["norm_r"], 1)

        act.wait_ge(S["vec_turned"], 1)
        act.activation(vec[:, 0:NVEC], pb[5][:, 0:NVEC], ACT.Copy).then_inc(S["vec_kept"], 1)
        for b in range(4):
            act.wait_ge(S["x_turned"], b + 1)
            act.activation(hx[:, 2 * b:2 * b + 2, :], pb[b].rearrange("p (a n) -> p a n", a=2), ACT.Copy)\
               .then_inc(S["x_kept"], 1)
        act.wait_ge(S["x_turned"], 5)
        act.activation(hT[:, :, 0:M], pb[4][:, 0:P].rearrange("p (a n) -> p a n", a=KT), ACT.Copy).then_inc(S["x_kept"], 1)
        act.wait_ge(S["lam_sum"], 1)
        act.activation(lamc[:, 0:2], sml[:, 0:2], ACT.Exp).then_inc(S["lam_exp"], 1)
        act.wait_ge(S["vec_kept"], 1)
        act.activation(sml[:, 8:16], vec[:, VROW["c"]:VROW["c"] + KT], ACT.Exp, scale=-1.0).then_inc(S["lam_exp"], 1)
        act.wait_ge(S["x_kept"], 5)
        act.wait_ge(S["filled"], 1)
        norm(0, hT[:, :, :], sqa, rms, TM)

        def keep1(g):
            p, kind, n, c = GR1[g]
            act.wait_ge(S["gemm1"], g + 1)
            src = pb[g % 3]
            if kind == "sq":
                dst, src, scale = sqT[:, c, :], src[:, 0:T], 1.0
            elif kind == "sk":
                dst, src, scale = skT[:, c, :], src[:, 0:TM], 1.0
            elif kind == "dq":
                dst, src, scale = dqT[:, c, :], src[:, 0:T], 0.125
            elif kind == "dk":
                dst, src, scale = dkT[:, c, :], src[:, 0:TM], 1.0
            elif kind in ("sv", "dv"):
                buf, rows, part = (sv, dv)[kind == "dv"], M if n == 2 else P, c // 3
                dst, src, scale = buf[0:rows, n, 512 * part:512 * part + 512], src[0:rows, :], 1.0
            elif kind == "gate":
                if c == 0:
                    act.wait_ge(S["lam_done"], 1)
                act.activation(gate[:, c, :], src[:, 0:T], ACT.Exp, scale=-1.0, bias=nbg[:, c:c + 1])\
                   .then_inc(S["act_evac1"], 1)
                return
            act.activation(dst, src, ACT.Copy, scale=scale).then_inc(S["act_evac1"], 1)

        def sb_step(s, h):
            if s == "sbA":
                act.wait_ge(S["sb_scores"], h + 1)
                if h:
                    act.wait_ge(S["sb_la"], h)
                act.activation(zs[:, 0:384], pb[3][:, 0:384], ACT.Copy, scale=SB_SCALE)
                act.activation(zs[0:M, 384:640], pb[4][0:M, 0:T], ACT.Copy, scale=SB_SCALE).then_inc(S["sb_zs"], 1)
                act.wait_ge(S["sb_min"], h + 1)
                st.do(act.activation(ex[:, 0:384], ex[:, 0:384], ACT.Exp))
                st.do(act.activation(ex[0:M, 384:640], ex[0:M, 384:640], ACT.Exp))
                st.wait()
                act.activation(sp_[:, 0:384], ex[:, 0:384], ACT.Ln, bias=onec)
                act.activation(sp_[0:M, 384:640], ex[0:M, 384:640], ACT.Ln, bias=onec[0:M]).then_inc(S["sb_ln"], 1)
            if s == "sbB":
                act.wait_ge(S["sb_la"], h + 1)
                act.activation(la[:, 0:384], la[:, 0:384], ACT.Exp)
                act.activation(la[0:M, 384:640], la[0:M, 384:640], ACT.Exp).then_inc(S["sb_a"], 1)
            if s == "sbC":
                act.wait_ge(S["sb_o"], h + 1)
                act.activation(sqT[:, h, :], pb[7][:, 0:T], ACT.Copy).then_inc(S["sb_out"], 1)

        def df_step(s, h):
            if s == "dfA":
                act.wait_ge(S["df_max"], h + 1)
                for qt in range(2):
                    for c in range(2):
                        v = sc[:, c, 144 * qt:144 + 272 * qt]
                        last = act.activation(v, v, ACT.Exp, bias=sml[:, 16 + 2 * qt + c:17 + 2 * qt + c],
                                              accum_out=sml[:, 20 + 2 * qt + c:21 + 2 * qt + c])
                last.then_inc(S["df_exp"], 1)
            if s == "dfB":
                act.wait_ge(S["df_tr"], h + 1)
                act.activation(wT[:, 0:384], pb[5][:, 0:384], ACT.Copy)
                act.activation(wT[0:M, 384:640], pb[6][0:M, 0:T], ACT.Copy).then_inc(S["df_wt"], 1)
            if s == "dfC":
                act.wait_ge(S["df_o"], h + 1)
                act.activation(osq, pb[7][:, 0:T], ACT.Square).then_inc(S["df_sq"], 1)
            if s == "dfD":
                act.wait_ge(S["df_ms"], h + 1)
                st.do(act.activation(ors, pb[6][:, T:512], ACT.Ln, bias=epsc, scale=1.0 / P))
                st.wait()
                act.activation(ors, ors, ACT.Exp, scale=-0.5).then_inc(S["df_rs"], 1)

        sp_ = sp
        for s, h in ORDER1:
            if s == "G" and not evac(GR1, h)[0]:
                keep1(h)
            elif s[0:2] == "sb":
                sb_step(s, h)
            elif s[0:2] == "df":
                df_step(s, h)

        act.wait_ge(S["dve_evac1"], evac(GR1, len(GR1) - 1)[1])
        norm(1, hx, sqa, rms, T)
        with act.Fori(0, UPS // 2) as i:
            for q in range(4):
                act.wait_ge(S["up"], i * 8 + (2 * q + 1))
                act.wait_ge(S["up_free"], i * 4 + (q + 1))
                act.activation(fe[:, q % 2, :], pb[2 * (q % 2)][:, 0:T], ACT.Exp, scale=-1.0).then_inc(S["up_exp"], 1)
        for q in range(2):
            act.wait_ge(S["up"], 4 * (UPS - 1) + 2 * q + 1)
            act.wait_ge(S["up_free"], 2 * (UPS - 1) + q + 1)
            act.activation(fe[:, q, :], pb[2 * q][:, 0:T], ACT.Exp, scale=-1.0).then_inc(S["up_exp"], 1)
        act.wait_ge(S["down_out"], 4)
        norm(2, hx, sqa, rms, T)
        act.wait_ge(S["norm_x"], 24)
        norm(3, hx, sqa, rms, T)

        def keep2(g):
            p, kind, n, c = GR2[g]
            act.wait_ge(S["gemm2"], g + 1)
            src, scale = pb[g % 3], 1.0
            if kind == "rq":
                dst, src = raw[:, 0, T * n:T * n + T], src[:, 0:T]
            elif kind == "rk":
                dst, src, scale = raw[:, 1, T * n:T * n + T], src[:, 0:T], P ** -0.5
            elif kind == "rv":
                dst = rv[:, n, 512 * (c // 2):512 * (c // 2) + 512]
            elif kind == "aq":
                dst, src, scale = aqT[:, c, :], src[:, 0:T], P ** -0.5
            elif kind == "ak":
                dst, src = akT[:, c, :], src[:, 0:T]
            elif kind == "av":
                dst = av[:, n, 512 * (c // 2):512 * (c // 2) + 512]
            elif kind == "gab":
                act.activation(gab[:, c, :], src[:, 0:T], ACT.Exp, scale=-1.0).then_inc(S["act_evac2"], 1)
                return
            act.activation(dst, src, ACT.Copy, scale=scale).then_inc(S["act_evac2"], 1)

        def rt_step(s, h):
            if s == "rtB":
                act.wait_ge(S["rt_y"], h + 1)
                if h:
                    act.wait_ge(S["rt_out"], h)
                act.activation(ys, pb[4].rearrange("p (a n) -> p a n", a=2), ACT.Copy).then_inc(S["rt_ys"], 1)
            if s == "rtC":
                act.wait_ge(S["rt_yc"], h + 1)
                act.activation(yq, ys, ACT.Square).then_inc(S["rt_sq"], 1)
            if s == "rtD":
                act.wait_ge(S["rt_v"], h + 1)
                st.do(act.activation(yr, pb[6][:, 0:T], ACT.Ln, bias=gnepsc, scale=1.0 / T))
                st.wait()
                act.activation(yr, yr, ACT.Exp, scale=-0.5).then_inc(S["rt_r"], 1)

        def dl_step(s, h):
            if s == "dlA":
                act.wait_ge(S["dl_max"], h + 1)
                for qt, v in enumerate((ds[:, 0:384], ds[:, 384:1152])):
                    last = act.activation(v, v, ACT.Exp, bias=sml[:, 16 + qt:17 + qt], accum_out=sml[:, 18 + qt:19 + qt])
                last.then_inc(S["dl_e"], 1)
            if s == "dlB":
                act.wait_ge(S["dl_t"], h + 1)
                for g in range(GROUPS):
                    last = act.activation(dwT[:, 384 * g:384 * g + 384], pb[3 + g][:, 0:384], ACT.Copy)
                last.then_inc(S["dl_wt"], 1)
            if s == "dlC":
                act.wait_ge(S["dl_o"], h + 1)
                act.activation(attT[:, h, :], pb[7][:, 0:T], ACT.Copy).then_inc(S["dl_out"], 1)

        for s, h in ORDER2:
            if s == "G":
                if GR2[h][1] == "rg":
                    act.wait_ge(S["gemm2"], h + 1)
                    c = h - first_of(GR2, "rg")
                    if c >= 2:
                        act.wait_ge(S["dve_evac2"], c - 1)
                    act.activation(rsg[:, c % 2, :], pb[h % 3][:, 0:T], ACT.Exp, scale=-1.0).then_inc(S["rg_exp"], 1)
                elif not evac(GR2, h)[0]:
                    keep2(h)
            elif s[0:2] == "rt":
                rt_step(s, h)
            elif s[0:2] == "dl":
                dl_step(s, h)
        act.wait_ge(S["dve_evac2"], evac(GR2, len(GR2) - 1)[1])
        norm(4, hx, nsq, nrms, T)
        for b in range(4):
            act.wait_ge(S["ht_mm"], b + 1)
            act.activation(htok[:, b // 2, 512 * (b % 2):512 * (b % 2) + 512], pb[4 + b], ACT.Copy).then_inc(S["ht_kept"], 1)
        act.wait_ge(S["route"], 1)
        act.activation(gts, gts, ACT.Exp).then_inc(S["log_exp"], 1)
        act.wait_ge(S["gt_mm"], 1)
        act.activation(gatT, pb[2][0:E, 0:T], ACT.Copy).then_inc(S["gt_kept"], 1)

        def expert(e, cur, prev):
            if cur:
                act.wait_ge(S["gath"], e + 1)
                since(act, "u_mm", e * 5)
                act.activation(XgT, pb[3].rearrange("p (a n) -> p a n", a=KT), ACT.Copy).then_inc(S["xg"], 1)
            if prev:
                act.wait_ge(S["at_mm"], e)
                since(act, "y_mm", e * 2 - 2)
                act.activation(aT, pb[4].rearrange("p (a n) -> p a n", a=4), ACT.Copy).then_inc(S["at"], 1)
                act.wait_ge(S["selt_mm"], e)
                since(act, "sc_mm", e * 2 - 2)
                act.activation(selT, pb[5][:, 0:T], ACT.Copy).then_inc(S["selt"], 1)
                act.wait_ge(S["y_mm"], e * 2)
                act.activation(yv, pb[2], ACT.Copy).then_inc(S["yv_done"], 1)
            if cur:
                act.wait_ge(S["u_read"], e + 1)
                since(act, "a_done", e)
                act.activation(sg, gl, ACT.Sigmoid, scale=1.702).then_inc(S["u_sig"], 1)

        expert(0, True, False)
        expert(1, True, True)
        with act.Fori(2, E) as e:
            expert(e, True, True)
        expert(E, False, True)

        def again(e, n, r):
            act.wait_ge(S["over_pe"], n * 7 + 2)
            act.activation(XgT, pb[3].rearrange("p (a n) -> p a n", a=KT), ACT.Copy).then_inc(S["over_act"], 1)
            act.wait_ge(S["over_pe"], n * 7 + 3)
            act.activation(selT, pb[5][:, 0:T], ACT.Copy).then_inc(S["over_act"], 1)
            act.wait_ge(S["over_dve"], n * 7 + 3)
            act.activation(sg, gl, ACT.Sigmoid, scale=1.702).then_inc(S["over_act"], 1)
            act.wait_ge(S["over_pe"], n * 7 + 5)
            act.activation(aT, pb[4].rearrange("p (a n) -> p a n", a=4), ACT.Copy).then_inc(S["over_act"], 1)
            act.wait_ge(S["over_pe"], n * 7 + 6)
            act.activation(yv, pb[2], ACT.Copy).then_inc(S["over_act"], 1)

        further(act, again)
        act.wait_ge(S["final_sum"], KT)
        norm(5, hx, nsq, nrms, T)
        for b in range(4):
            act.wait_ge(S["fin_mm"], b + 1)
            act.activation(otok[:, b // 2, 512 * (b % 2):512 * (b % 2) + 512], pb[4 + b], ACT.Copy).then_inc(S["fin_kept"], 1)

    @block.vector
    def _(dve):
        st = Count(dve, S["dve_step"])
        stt, tt, ts = nc.vector.scalar_tensor_tensor, nc.vector.tensor_tensor, nc.vector.tensor_scalar
        csil = vx[:, 40:48]

        def norm(k, dst, src, r, g):
            dve.wait_ge(S["norm_r"], k + 1)
            for t in range(KT):
                stt(dst[:, t, :], src[:, t, :], g[:, t:t + 1], r, ALU.mult, ALU.mult).then_inc(S["norm_x"], 1)

        def shift(k, n, dst, sh):
            for t in range(KT):
                dve.wait_ge(S["norm_x"], KT * k + t + 1)
                ts(dst[:, t, :], dst[:, t, :], sh[:, t:t + 1], None, ALU.add).then_inc(S["norm_s"], 1)

        def vrows(name, n=KT):
            return vec[:, VROW[name]:VROW[name] + n]

        dve.wait_ge(S["lam_in"], 64)
        st.do(tt(lamv[:, 0:2, :], lamv[:, 0:2, :], lamv[:, 2:4, :], ALU.mult))
        st.wait()
        nc.vector.tensor_reduce(sml[:, 0:2], lamv[:, 0:2, :], AX.X, ALU.add).then_inc(S["lam_sum"], 1)
        dve.wait_ge(S["vec_kept"], 1)
        ts(nbg, vrows("b_gate", 16), -1.0, None, ALU.mult).then_inc(S["lam_done"], 1)
        st.do(ts(gsub, vrows("subln_g", 1), 1.0 - LAM_INIT, None, ALU.mult))
        dve.wait_ge(S["lam_exp"], 1)
        st.do(tt(lamc[:, 2:3], lamc[:, 1:2], lamc[:, 0:1], ALU.subtract))
        st.wait()
        st.do(ts(lamc[:, 2:3], lamc[:, 2:3], -LAM_INIT, None, ALU.add))
        dve.wait_ge(S["lam_exp"], 2)
        st.do(ts(sml[:, 8:16], sml[:, 8:16], 1.0, None, ALU.add))
        st.wait()
        st.do(nc.vector.reciprocal(sml[:, 8:16], sml[:, 8:16]))
        st.wait()
        st.do(tt(csil, sml[:, 8:16], vrows("c"), ALU.mult))

        norm(0, xn, hT, rms[:, 0:TM], vrows("norm_mix_g"))

        def sigmoid_rest(v):
            st.do(ts(v, v, 1.0, None, ALU.add))
            st.wait()
            return nc.vector.reciprocal(v, v)

        def keep1(g):
            p, kind, n, c = GR1[g]
            src = pb[g % 3][:, 0:T]
            if kind == "gate":
                dve.wait_ge(S["act_evac1"], evac(GR1, g)[1])
                sigmoid_rest(gate[:, c, :]).then_inc(S["gate_done"], 1)
                return
            if kind not in DVE_KINDS:
                return
            dve.wait_ge(S["gemm1"], g + 1)
            if kind == "ysb":
                dve.wait_ge(S["gate_done"], c + 1)
                tt(mT[:, c, :], src, gate[:, c, :], ALU.mult).then_inc(S["dve_evac1"], 1)
            if kind == "ydf":
                dve.wait_ge(S["gate_done"], KT + c + 1)
                dve.wait_ge(S["dve_evac1"], KT + c)
                st.do(tt(dtmp, src, gate[:, KT + c, :], ALU.mult))
                st.wait()
                tt(mT[:, c, :], mT[:, c, :], dtmp, ALU.add).then_inc(S["dve_evac1"], 1)
            if kind == "out":
                tt(hx[:, c, :], src, hx[:, c, :], ALU.add).then_inc(S["dve_evac1"], 1)

        def sb_step(s, h):
            if s == "sbA":
                dve.wait_ge(S["sb_zs"], h + 1)
                if h:
                    dve.wait_ge(S["sb_ln"], h)
                ts(ex[:, 0:384], zs[:, 0:384], 40.0, None, ALU.min)
                ts(ex[0:M, 384:640], zs[0:M, 384:640], 40.0, None, ALU.min).then_inc(S["sb_min"], 1)
                dve.wait_ge(S["sb_ln"], h + 1)
                st.do(tt(sp[:, 0:384], sp[:, 0:384], zs[:, 0:384], ALU.max))
                st.do(tt(sp[0:M, 384:640], sp[0:M, 384:640], zs[0:M, 384:640], ALU.max))
                st.wait()
                tt(two(sp), two(sp), bc(tri, 2), ALU.mult).then_inc(S["sb_sp"], 1)
            if s == "sbB":
                dve.wait_ge(S["sb_rest"], h + 1)
                if h:
                    dve.wait_ge(S["sb_o"], h)
                st.do(tt(la[:, 0:384], pb[5][:, 0:384], zs[:, 0:384], ALU.add))
                st.do(tt(la[0:M, 384:640], pb[6][0:M, 0:T], zs[0:M, 384:640], ALU.add))
                st.wait()
                tt(two(la), two(la), bc(negm, 2), ALU.add).then_inc(S["sb_la"], 1)

        def df_step(s, h):
            if s == "dfA":
                dve.wait_ge(S["df_scores"], h + 1)
                for c in range(2):
                    last = stt(sc[:, c, :], distt, 2.0 ** -(h + 1), pb[3 + c][:, 0:416], ALU.mult, ALU.add)
                last.then_inc(S["df_s"], 1)
                dve.wait_ge(S["df_s"], h + 1)
                for qt in range(2):
                    st.do(nc.vector.tensor_reduce(sml[:, 16 + 2 * qt:18 + 2 * qt], sc[:, :, 144 * qt:144 + 272 * qt],
                                                  AX.X, ALU.max))
                st.wait()
                ts(sml[:, 16:20], sml[:, 16:20], -1.0, None, ALU.mult).then_inc(S["df_max"], 1)
                dve.wait_ge(S["df_exp"], h + 1)
                st.do(nc.vector.reciprocal(sml[:, 24:28], sml[:, 20:24]))
                st.wait()
                for qt in range(2):
                    st.do(ts(sml[:, 25 + 2 * qt:26 + 2 * qt], sml[:, 25 + 2 * qt:26 + 2 * qt], lamc[:, 2:3], None, ALU.mult))
                if h:
                    dve.wait_ge(S["df_tr"], h)
                for qt in range(2):
                    v = slice(144 * qt, 144 + 272 * qt)
                    st.do(ts(wv[:, v], sc[:, 0, v], sml[:, 24 + 2 * qt:25 + 2 * qt], None, ALU.mult))
                st.wait()
                for qt in range(2):
                    v = slice(144 * qt, 144 + 272 * qt)
                    last = stt(wv[:, v], sc[:, 1, v], sml[:, 25 + 2 * qt:26 + 2 * qt], wv[:, v], ALU.mult, ALU.add)
                last.then_inc(S["df_w"], 1)
            if s == "dfD":
                dve.wait_ge(S["df_rs"], h + 1)
                stt(dqT[:, h, :], pb[7][:, 0:T], gsub, ors, ALU.mult, ALU.mult).then_inc(S["df_out"], 1)

        dve.wait_ge(S["cst_in"], 16)
        for s, h in ORDER1:
            if s == "G":
                keep1(h)
            elif s[0:2] == "sb":
                sb_step(s, h)
            elif s[0:2] == "df":
                df_step(s, h)

        norm(1, xf, hx, rms[:, 0:T], vrows("norm_ffn_g"))

        def mlp(f, u, q):
            step = lambda k: dve.wait_ge(S["up_step"], f * 3 + k)
            dve.wait_ge(S["up_exp"], f + 1)
            ts(fr[:, q, :], fe[:, q, :], 1.0, None, ALU.add).then_inc(S["up_step"], 1)
            step(1)
            nc.vector.reciprocal(fr[:, q, :], fr[:, q, :]).then_inc(S["up_step"], 1)
            step(2)
            tt(fr[:, q, :], pb[2 * q][:, 0:T], fr[:, q, :], ALU.mult).then_inc(S["up_step"], 1)
            step(3)
            dve.wait_ge(S["up"], u)
            tt(fT[:, bass.ds(f, 1), :].rearrange("p a n -> p (a n)"), pb[2 * q + 1][:, 0:T], fr[:, q, :], ALU.mult)\
                .then_inc(S["up_free"], 1)

        def ada(j, n, b):
            dve.wait_ge(ina[b], n)
            dve.wait_ge(S["ada_mm"], j + 1)
            w = slot(2 + b)
            ts(adac[:, b, :], w[:, 0, :], csil[:, 0:1], None, ALU.mult).then_inc(S["ada_step"], 1)
            for k in range(1, KT):
                dve.wait_ge(S["ada_step"], j * 7 + k)
                stt(adac[:, b, :], w[:, k, :], csil[:, k:k + 1], adac[:, b, :], ALU.mult, ALU.add)\
                    .then_inc(S["ada_step" if k < KT - 1 else "ada_sum"], 1)

        dve.sem_inc(S["up_free"], 2)
        with dve.Fori(0, UPS // 2) as i:
            for b in range(2):
                ada(i * 2 + b, i * 16 + 16, b)
                for q in range(2):
                    mlp(i * 4 + (2 * b + q), i * 8 + (4 * b + 2 * q + 2), q)
        for b in range(2):
            ada(ADAS - 2 + b, 16 * (ADAS // 2), b)
        for q in range(2):
            mlp(FT - 2 + q, 2 * (FT - 1 + q), q)
        dve.wait_ge(S["ada_mm"], ADAS + 2)
        st.do(tt(modT[:, :], pb[7][:, 0:48], vrows("b_ada", 48), ALU.add))
        st.wait()
        st.do(stt(gsa, modT[:, 8:16], 1.0, vrows("g_mix"), ALU.add, ALU.mult))
        st.do(stt(gsf, modT[:, 32:40], 1.0, vrows("g_ffn"), ALU.add, ALU.mult))
        st.n_mod = st.n
        dve.sem_inc(S["mod_done"], 1)
        for b in range(4):
            dve.wait_ge(S["down"], 6 + b)
            v = hx[:, 2 * b:2 * b + 2, :]
            tt(v, pb[4 + b].rearrange("p (a n) -> p a n", a=2), v, ALU.add).then_inc(S["down_out"], 1)
        st.wait()
        norm(2, hx, hx, rms[:, 0:T], vrows("norm_final_g"))
        norm(3, xn2, hx, rms[:, 0:T], gsa)
        shift(3, 0, xn2, modT[:, 0:8])
        dve.wait_ge(S["hot_in"], 48)
        for g in range(GROUPS):
            dve.wait_ge(S["toep_mm"], g + 1)
            tt(stg[:, g, :], pb[4 + g][0:SLOTS, 0:TOEP], bad[:, g, :], ALU.add).then_inc(S["toep_sum"], 1)

        def keep2(g):
            p, kind, n, c = GR2[g]
            src = pb[g % 3][:, 0:T]
            if kind == "gab":
                dve.wait_ge(S["act_evac2"], evac(GR2, g)[1])
                sigmoid_rest(gab[:, c, :]).then_inc(S["gab_done"], 1)
                return
            if kind not in DVE_KINDS:
                return
            dve.wait_ge(S["gemm2"], g + 1)
            if kind == "rg":
                dve.wait_ge(S["rg_exp"], c + 1)
                st.do(sigmoid_rest(rsg[:, c % 2, :]))
                st.wait()
                tt(rg[:, c, :], src, rsg[:, c % 2, :], ALU.mult).then_inc(S["dve_evac2"], 1)
            if kind == "yret":
                dve.wait_ge(S["gab_done"], c + 1)
                tt(m2T[:, c, :], src, gab[:, c, :], ALU.mult).then_inc(S["dve_evac2"], 1)
            if kind == "yatt":
                dve.wait_ge(S["gab_done"], KT + c + 1)
                dve.wait_ge(S["dve_evac2"], evac(GR2, g)[1] - 1)
                st.do(tt(dtmp2, src, gab[:, KT + c, :], ALU.mult))
                st.wait()
                tt(m2T[:, c, :], m2T[:, c, :], dtmp2, ALU.add).then_inc(S["dve_evac2"], 1)
            if kind == "o":
                stt(hx[:, c, :], src, modT[:, 16 + c:17 + c], hx[:, c, :], ALU.mult, ALU.add).then_inc(S["dve_evac2"], 1)

        def rotary(i):
            g = first_of(GR2, ("rq", "rk")[i]) + 3
            dve.wait_ge(S["act_evac2"], evac(GR2, g)[1])
            if i == 0:
                dve.wait_ge(S["tab_in"], 16)
            dst = (rqT, rkT)[i]
            r = raw[:, i, :].rearrange("p (a n) -> p a n", a=RH)
            st.do(tt(dst, r, bc(tab[:, RH, :], RH), ALU.mult))
            st.wait()
            dve.wait_ge(S["rot_mm"], i + 1)
            for j in range(2):
                st.do(tt(r[:, 2 * j:2 * j + 2, :], pb[3 + j].rearrange("p (a n) -> p a n", a=2),
                         bc(tab[:, RH + 1, :], 2), ALU.mult))
            st.wait()
            tt(dst, dst, r, ALU.add).then_inc(S["rot_out"], 1)

        def rt_step(s, h):
            if s == "rtA":
                dve.wait_ge(S["rt_s"], h + 1)
                if h:
                    dve.wait_ge(S["rt_y"], h)
                else:
                    dve.wait_ge(S["toep_out"], 16)
                tt(pT[:, 0:T], pb[3][:, 0:T], tab[:, h, :], ALU.mult)
                tt(pT[:, T:384], pb[3][:, T:384], tab[:, h, 0:P], ALU.mult).then_inc(S["rt_p"], 1)
            if s == "rtC":
                dve.wait_ge(S["rt_m"], h + 1)
                for e in range(2):
                    last = stt(ys[:, e, :], pb[5][:, 0:T], -1.0 / T, ys[:, e, :], ALU.mult, ALU.add)
                last.then_inc(S["rt_yc"], 1)
            if s == "rtD":
                dve.wait_ge(S["rt_r"], h + 1)
                st.do(tt(ys, ys, bc(yr, 2), ALU.mult))
                st.wait()
                v = rg[:, 2 * h:2 * h + 2, :]
                tt(v, v, ys, ALU.mult).then_inc(S["rt_out"], 1)

        def dl_step(s, h):
            bt = BT.rearrange("p (g s) n -> p s g n", g=GROUPS)[:, h, :, :]
            if s == "dlA":
                dve.wait_ge(S["dl_s"], h + 1)
                tt(ds[:, 0:384].rearrange("p (g n) -> p g n", g=3), pb[3][:, 0:384].rearrange("p (g n) -> p g n", g=3),
                   bt[:, :, P:T], ALU.add)
                tt(ds[:, 384:896].rearrange("p (g n) -> p g n", g=2), pb[4].rearrange("p (g n) -> p g n", g=2),
                   bt[:, 0:2, :], ALU.add)
                tt(ds[:, 896:1152], pb[5][:, 0:T], bt[:, 2, :], ALU.add).then_inc(S["dl_b"], 1)
                dve.wait_ge(S["dl_b"], h + 1)
                for qt, v in enumerate((ds[:, 0:384], ds[:, 384:1152])):
                    st.do(nc.vector.tensor_reduce(sml[:, 16 + qt:17 + qt], v, AX.X, ALU.max))
                st.wait()
                ts(sml[:, 16:18], sml[:, 16:18], -1.0, None, ALU.mult).then_inc(S["dl_max"], 1)
                dve.wait_ge(S["dl_e"], h + 1)
                st.do(nc.vector.reciprocal(sml[:, 20:22], sml[:, 18:20]))
                st.wait()
                for qt, v in enumerate((ds[:, 0:384], ds[:, 384:1152])):
                    last = ts(v, v, sml[:, 20 + qt:21 + qt], None, ALU.mult)
                last.then_inc(S["dl_p"], 1)

        for s, h in ORDER2:
            if s == "G":
                keep2(h)
            elif s == "rot":
                rotary(h)
            elif s[0:2] == "rt":
                rt_step(s, h)
            elif s[0:2] == "dl":
                if s == "dlA" and h == 0:
                    dve.wait_ge(S["toep_in"], 16)
                dl_step(s, h)

        norm(4, hn, hx, nrms, gsf)
        shift(4, 1, hn, modT[:, 24:32])
        dve.wait_ge(S["moe_in"], 48)
        dve.wait_ge(S["log_mm"], 1)
        st.do(tt(lg, pb[1][:, 0:2 * E].rearrange("p (a e) -> p a e", a=2), bc(brow, 2), ALU.add))
        st.do(nc.vector.memset(msk, 0.0))
        st.do(nc.vector.memset(gat, 0.0))
        st.do(nc.vector.memset(rank, -1.0))
        st.wait()
        for t in range(2):
            st.do(nc.vector.max(top8[:, t, :], lg[:, t, :]))
        st.wait()
        for t in range(2):
            st.do(nc.vector.max_index(topi[:, t, :], top8[:, t, :], lg[:, t, :]))
            st.do(ts(gts[:, t, :], top8[:, t, :], top8[:, t, 0:1], None, ALU.subtract))
        st.wait()
        nc.vector.tensor_copy(tif, topi[:, :, :]).then_inc(S["route"], 1)
        dve.wait_ge(S["log_exp"], 1)
        st.do(nc.vector.tensor_reduce(sml[:, 32:34], gts[:, :, 0:4], AX.X, ALU.add))
        st.wait()
        st.do(nc.vector.reciprocal(sml[:, 34:36], sml[:, 32:34]))
        st.wait()
        for t in range(2):
            st.do(ts(gts[:, t, 0:4], gts[:, t, 0:4], sml[:, 34 + t:35 + t], None, ALU.mult))
        dve.wait_ge(S["route"], 1)
        for j in range(4):
            for t in range(2):
                st.do(ts(one[:, t, :], iotae, tif[:, t, j:j + 1], None, ALU.is_equal))
            st.wait()
            for t in range(2):
                st.do(stt(gat[:, t, :], one[:, t, :], gts[:, t, j:j + 1], gat[:, t, :], ALU.mult, ALU.add))
                st.do(tt(msk[:, t, :], msk[:, t, :], one[:, t, :], ALU.add))
            st.wait()
        dve.sem_inc(S["route"], 1)
        dve.wait_ge(S["rank_mm"], 1)
        st.do(stt(rank[:, :, 0:E], pb[0][:, 0:2 * E].rearrange("p (a e) -> p a e", a=2), 1.0, msk, ALU.add, ALU.mult))
        st.do(nc.vector.tensor_copy(cntf[0:1, 0:E], pb[0][0:1, 64:64 + E]))
        st.wait()
        st.do(ts(rank[:, :, 0:E], rank[:, :, 0:E], -1.0, None, ALU.add))
        st.do(nc.vector.tensor_reduce(cntf[0:1, E:E + 1], cntf[0:1, 0:E], AX.X, ALU.max))
        st.wait()
        nc.vector.tensor_copy(cnti[0:1, :], cntf[0:1, :]).then_inc(S["rank_done"], 1)
        for b in range(4):
            dve.wait_ge(S["b2_mm"], b + 1)
            nc.vector.tensor_copy(acc[:, 2 * b:2 * b + 2, :], pb[4 + b].rearrange("p (a n) -> p a n", a=2))\
                .then_inc(S["acc_init"], 1)
        dve.wait_ge(S["acc_init"], 4)

        def choose_u(e):
            for t in range(2):
                last = ts(selU[:, t, :], iotac[:, 0:64], rank[:, t, bass.ds(e, 1)], None, ALU.is_equal)
            last.then_inc(S["selu"], 1)

        def choose_g(e):
            for t in range(2):
                last = ts(selG[:, t, :], iotac, rank[:, t, bass.ds(e, 1)], gat[:, t, bass.ds(e, 1)], ALU.is_equal, ALU.mult)
            last.then_inc(S["selg"], 1)

        def add_up(r, n):
            dve.wait_ge(S["sc_mm"], n)
            for h in range(2):
                v = acc[:, 4 * h + 2 * r:4 * h + 2 * r + 2, :]
                last = tt(v, pb[6 + h].rearrange("p (a n) -> p a n", a=2), v, ALU.add)
            last.then_inc(S["acc_done"], 1)

        def expert(e, cur, prev):
            if prev:
                since(dve, "selt_mm", e - 1)
                choose_g(e - 1)
            if cur:
                dve.wait_ge(S["gath"], e + 1)
                choose_u(e + 1)
            if prev:
                since(dve, "acc_done", e * 2 - 2)
                add_up(0, e * 2 - 1)
            if cur:
                dve.wait_ge(S["u_mm"], e * 5 + 5)
                since(dve, "a_done", e)
                u = banks[:, 0:2, :].rearrange("p a (n c) -> p a n c", c=2)
                ts(gl.rearrange("p (a n) -> p a n", a=2), u[:, :, :, 0], 7.0, None, ALU.min)
                ts(li.rearrange("p (a n) -> p a n", a=2), u[:, :, :, 1], 7.0, -7.0, ALU.min, ALU.max).then_inc(S["u_read"], 1)
            if prev:
                add_up(1, e * 2)
            if cur:
                dve.wait_ge(S["u_read"], e + 1)
                since(dve, "at_mm", e)
                stt(aa, li, 1.0, gl, ALU.add, ALU.mult).then_inc(S["a_mid"], 1)
                dve.wait_ge(S["u_sig"], e + 1)
                dve.wait_ge(S["a_mid"], e + 1)
                tt(aa, aa, sg, ALU.mult).then_inc(S["a_done"], 1)

        nc.vector.memset(taken, 0.0).then_inc(S["round"], 1)
        dve.wait_ge(S["round"], 1)
        dve.wait_ge(S["rank_done"], 1)
        choose_u(0)
        expert(0, True, False)
        expert(1, True, True)
        with dve.Fori(2, E) as e:
            expert(e, True, True)
        expert(E, False, True)
        dve.wait_ge(S["acc_done"], 2 * E)

        def next_round(r):
            ts(taken, taken, float(CAP), None, ALU.add).then_inc(S["round"], 1)

        def again(e, n, r):
            dve.wait_ge(S["over_pe"], n * 7 + 1)
            dve.wait_ge(S["round"], r + 1)
            for t in range(2):
                last = tt(rks[:, t:t + 1], rank[:, t, bass.ds(e, 1)], taken, ALU.subtract)
            last.then_inc(S["over_dve"], 1)
            dve.wait_ge(S["over_dve"], n * 7 + 1)
            for t in range(2):
                ts(selU[:, t, :], iotac[:, 0:64], rks[:, t:t + 1], None, ALU.is_equal)
                last = ts(selG[:, t, :], iotac, rks[:, t:t + 1], gat[:, t, bass.ds(e, 1)], ALU.is_equal, ALU.mult)
            last.then_inc(S["over_dve"], 1)
            dve.wait_ge(S["over_pe"], n * 7 + 4)
            u = banks[:, 0:2, :].rearrange("p a (n c) -> p a n c", c=2)
            ts(gl.rearrange("p (a n) -> p a n", a=2), u[:, :, :, 0], 7.0, None, ALU.min)
            ts(li.rearrange("p (a n) -> p a n", a=2), u[:, :, :, 1], 7.0, -7.0, ALU.min, ALU.max).then_inc(S["over_dve"], 1)
            dve.wait_ge(S["over_dve"], n * 7 + 3)
            stt(aa, li, 1.0, gl, ALU.add, ALU.mult).then_inc(S["over_dve"], 1)
            dve.wait_ge(S["over_act"], n * 5 + 3)
            dve.wait_ge(S["over_dve"], n * 7 + 4)
            tt(aa, aa, sg, ALU.mult).then_inc(S["over_dve"], 1)
            for q in range(2):
                dve.wait_ge(S["over_pe"], n * 7 + (7 + q))
                for h in range(2):
                    v = acc[:, 4 * h + 2 * q:4 * h + 2 * q + 2, :]
                    last = tt(v, pb[6 + h].rearrange("p (a n) -> p a n", a=2), v, ALU.add)
                last.then_inc(S["over_dve"], 1)
            dve.wait_ge(S["over_dve"], n * 7 + 7)

        further(dve, again, next_round)
        for t in range(KT):
            stt(hx[:, t, :], acc[:, t, :], modT[:, 40 + t:41 + t], hx[:, t, :], ALU.mult, ALU.add).then_inc(S["final_sum"], 1)
        norm(5, hn, hx, nrms, vrows("g_final"))

    @block.tensor
    def _(pe):
        mm = nc.tensor.matmul

        def norm(k, buf, n, banks_free=()):
            for t in range(KT):
                if t % 4 == 0:
                    pe.wait_ge(S["norm_sq"], 2 * k + t // 4 + 1)
                last = mm(pb[3][:, 0:n], ones[:, :], buf[:, t, 0:n], start=t == 0, stop=t == KT - 1)
            last.then_inc(S["norm_ms"], 1)

        pe.wait_ge(S["cst_in"], 16)
        pe.wait_ge(S["vec_in"], 16 * len(VEC_ROWS))
        nc.tensor.transpose(pb[5][:, 0:NVEC], vrow, ident[0:NVEC, 0:NVEC]).then_inc(S["vec_turned"], 1)
        pe.wait_ge(S["x_in"], 32)
        for b in range(4):
            for j in range(4):
                d, t = 2 * b + j // 2, j % 2
                last = nc.tensor.transpose(pb[b][:, P * j:P * j + P], xtok[:, t, P * d:P * d + P], ident)
            last.then_inc(S["x_turned"], 1)
        for d in range(KT):
            last = nc.tensor.transpose(pb[4][:, M * d:M * d + M], mtok[:, P * d:P * d + P], ident[0:M, 0:M])
        last.then_inc(S["x_turned"], 1)
        pe.wait_ge(S["x_kept"], 5)
        norm(0, sqa, TM)

        def group(GR, g, w, x, sem_name, evacs):
            p, kind, n, _ = GR[g]
            if g >= 3:
                who, count = evac(GR, g - 3)
                pe.wait_ge(S[evacs[who]], count)
            nk = w.shape[1]
            out = pb[g % 3]
            for k in range(nk):
                if kind in ("sv", "dv"):
                    lhs = x[:, k, 0:M] if n == 2 else x[:, k, M + P * n:M + P * n + P]
                    o, rhs = out[0:M if n == 2 else P, :], w[:, k, :]
                elif kind in ("rv", "av"):
                    lhs, o, rhs = x[:, k, P * n:P * n + P], out, w[:, k, :]
                else:
                    lhs, o, rhs = w[:, k, P * n:P * n + P], out[:, 0:x.shape[2]], x[:, k, :]
                last = mm(o, lhs, rhs, start=k == 0, stop=k == nk - 1)
            last.then_inc(S[sem_name], 1)

        def gemm1(g):
            p, kind, n, c = GR1[g]
            if n == 0:
                pe.wait_ge(in1[p % 2], 16 * (p // 2 + 1))
            if g == 0:
                pe.wait_ge(S["norm_x"], KT)
                pe.wait_ge(S["norm_r"], 1)
            if g == first_of(GR1, "ysb"):
                pe.wait_ge(S["sb_out"], HEADS)
            if g == first_of(GR1, "ydf"):
                pe.wait_ge(S["df_out"], HEADS)
            if g == first_of(GR1, "out"):
                pe.wait_ge(S["dve_evac1"], 2 * KT)
            x = {"sk": xn, "dk": xn, "sv": xn, "dv": xn, "ysb": sqT, "ydf": dqT, "out": mT}.get(kind, xn[:, :, M:TM])
            group(GR1, g, slot(4 + p % 2), x, "gemm1", ("act_evac1", "dve_evac1"))

        def sb_step(s, h):
            if s == "sbA":
                pe.wait_ge(S["act_evac1"], evac(GR1, where(GR1, "sk", h))[1])
                if h:
                    pe.wait_ge(S["sb_zs"], h)
                q = sqT[:, h, :]
                mm(pb[3][:, 0:T], skT[:, h, M:M + P], q, start=True, stop=True)
                mm(pb[3][:, T:384], skT[:, h, M + P:TM], q[:, P:T], start=True, stop=True)
                mm(pb[4][0:M, 0:T], skT[:, h, 0:M], q, start=True, stop=True).then_inc(S["sb_scores"], 1)
            if s == "sbB":
                pe.wait_ge(S["sb_sp"], h + 1)
                if h:
                    pe.wait_ge(S["sb_la"], h)
                mm(pb[5][:, T:384], ntri, sp[:, T:384], start=True, stop=True)
                mm(pb[5][:, 0:T], ntri, sp[:, 0:T], start=True, stop=False)
                mm(pb[5][:, P:T], nones[:, :], sp[:, T:384], start=False, stop=True)
                mm(pb[6][0:M, 0:T], ntri[0:M, 0:M], sp[0:M, 384:640], start=True, stop=False)
                mm(pb[6][0:M, 0:T], nones[:, 0:M], sp[:, 0:T], start=False, stop=False)
                mm(pb[6][0:M, P:T], nones[:, 0:M], sp[:, T:384], start=False, stop=True).then_inc(S["sb_rest"], 1)
            if s == "sbC":
                pe.wait_ge(S["sb_a"], h + 1)
                if h % 4 == 0:
                    pe.wait_ge(S["act_evac1"], evac(GR1, where(GR1, "sv", 3 * (h // 4) + 2))[1])
                if h:
                    pe.wait_ge(S["sb_out"], h)
                v = slice(P * h, P * h + P)
                mm(pb[7][:, 0:T], sv[:, 0, v], la[:, 0:T], start=True, stop=False)
                mm(pb[7][:, P:T], sv[:, 1, v], la[:, T:384], start=False, stop=False)
                mm(pb[7][:, 0:T], sv[0:M, 2, v], la[0:M, 384:640], start=False, stop=True).then_inc(S["sb_o"], 1)

        def df_step(s, h):
            if s == "dfA":
                pe.wait_ge(S["act_evac1"], evac(GR1, where(GR1, "dk", h))[1])
                if h:
                    pe.wait_ge(S["df_s"], h)
                else:
                    pe.wait_ge(S["sb_zs"], HEADS)
                for qt in range(2):
                    for c in range(2):
                        v = slice(64 * c, 64 * c + 64)
                        last = mm(pb[3 + c][:, 144 * qt:144 + 272 * qt], dqT[v, h, P * qt:P * qt + P],
                                  dkT[v, h, 0:144 + P * qt], start=True, stop=True)
                last.then_inc(S["df_scores"], 1)
            if s == "dfB":
                pe.wait_ge(S["df_w"], h + 1)
                if h:
                    pe.wait_ge(S["df_wt"], h)
                    pe.wait_ge(S["df_rs"], h)
                else:
                    pe.wait_ge(S["sb_la"], HEADS)
                tr = nc.tensor.transpose
                tr(pb[5][:, 0:P], wv[:, M:144], ident)
                tr(pb[5][:, P:T], wv[:, 160:288], ident)
                tr(pb[5][:, T:384], wv[:, 288:416], ident)
                tr(pb[6][0:M, 0:P], wv[:, 0:M], ident)
                tr(pb[6][0:M, P:T], wv[:, 144:160], ident).then_inc(S["df_tr"], 1)
            if s == "dfC":
                pe.wait_ge(S["df_wt"], h + 1)
                if h % 4 == 0:
                    pe.wait_ge(S["act_evac1"], evac(GR1, where(GR1, "dv", 3 * (h // 4) + 2))[1])
                if h:
                    pe.wait_ge(S["df_out"], h)
                else:
                    pe.wait_ge(S["sb_out"], HEADS)
                v = slice(P * h, P * h + P)
                mm(pb[7][:, 0:T], dv[:, 0, v], wT[:, 0:T], start=True, stop=False)
                mm(pb[7][:, P:T], dv[:, 1, v], wT[:, T:384], start=False, stop=False)
                mm(pb[7][:, 0:T], dv[0:M, 2, v], wT[0:M, 384:640], start=False, stop=True).then_inc(S["df_o"], 1)
            if s == "dfD":
                pe.wait_ge(S["df_sq"], h + 1)
                mm(pb[6][:, T:512], ones[:, :], osq, start=True, stop=True).then_inc(S["df_ms"], 1)

        for s, h in ORDER1:
            if s == "G":
                gemm1(h)
            elif s[0:2] == "sb":
                sb_step(s, h)
            elif s[0:2] == "df":
                df_step(s, h)

        pe.wait_ge(S["df_rs"], HEADS)
        norm(1, sqa, T)
        pe.wait_ge(S["norm_x"], 2 * KT)

        def up(j, b, f, n):
            pe.wait_ge(inu[b], n)
            for q in range(2):
                pe.wait_ge(S["up_free"], f + (q + 1))
                for side in range(2):
                    for k in range(KT):
                        last = mm(pb[2 * q + side][:, 0:T], slot(4 + b)[:, k, T * side + P * q:T * side + P * q + P], xf[:, k, :],
                                  start=k == 0, stop=k == KT - 1)
                    last.then_inc(S["up"], 1)

        def ada_mm(j, b):
            pe.wait_ge(S["ada_sum"], j + 1)
            for n in range(4):
                last = mm(pb[7][:, bass.ds(j * 4 + n, 1)], adac[:, b, P * n:P * n + P], ones[:, 0:1], start=True, stop=True)
            last.then_inc(S["ada_mm"], 1)

        pe.sem_inc(S["ada_mm"], 2)
        with pe.Fori(0, UPS // 2) as i:
            for b in range(2):
                up(i, b, i * 4 + 2 * b, i * 32 + 32)
                ada_mm(i * 2 + b, b)
        up(UPS - 1, 0, 2 * (UPS - 1), 32 * (UPS // 2 + 1))
        for b in range(2):
            ada_mm(ADAS - 2 + b, b)
        pe.wait_ge(S["up_free"], FT + 2)
        pe.wait_ge(S["mod_done"], 1)
        for j, nk in enumerate(DOWNS):
            b = (j + 1) % 2
            pe.wait_ge(ind[b], 16 * (j // 2 + 1))
            for n in range(KT):
                for k in range(nk):
                    kk = 4 * j + k
                    last = mm(pb[4 + n // 2][:, T * (n % 2):T * (n % 2) + T], slot(4 + b, 4)[:, k, P * n:P * n + P], fT[:, kk, :],
                              start=kk == 0 and n % 2 == 0, stop=kk == FT - 1, skip_group_check=True)
                if j == len(DOWNS) - 1 and n % 2:
                    last.then_inc(S["down"], 1)
            if j < len(DOWNS) - 1:
                last.then_inc(S["down"], 1)
        norm(2, sqa, T)
        norm(3, sqa, T)
        pe.wait_ge(S["hot_in"], 48)
        for g in range(GROUPS):
            mm(pb[4 + g][0:SLOTS, 0:TOEP], relb[:, SLOTS * g:SLOTS * g + SLOTS], hot[:, g, :], start=True, stop=True)\
                .then_inc(S["toep_mm"], 1)

        def gemm2(g):
            p, kind, n, c = GR2[g]
            if n == 0:
                pe.wait_ge(in2[p % 2], 16 * (p // 2 + 1))
            if g == 0:
                pe.wait_ge(S["norm_s"], KT)
            if g == first_of(GR2, "yret"):
                pe.wait_ge(S["rt_out"], RH)
            if g == first_of(GR2, "yatt"):
                pe.wait_ge(S["dl_out"], SLOTS)
            if g == first_of(GR2, "o"):
                pe.wait_ge(S["dve_evac2"], evac(GR2, g - 1)[1])
            x = {"yret": rg, "yatt": attT, "o": m2T}.get(kind, xn2)
            group(GR2, g, slot(5 - p % 2, 4 if kind == "yatt" else KT), x, "gemm2", ("act_evac2", "dve_evac2"))

        def rotary(i):
            g = first_of(GR2, ("rq", "rk")[i]) + 3
            pe.wait_ge(S["act_evac2"], evac(GR2, g)[1])
            if i:
                pe.wait_ge(S["rot_out"], 1)
            else:
                pe.wait_ge(S["toep_sum"], GROUPS)
            for j in range(2):
                last = mm(pb[3 + j], swap, raw[:, i, 512 * j:512 * j + 512], start=True, stop=True)
            last.then_inc(S["rot_mm"], 1)

        def rt_step(s, h):
            if s == "rtA":
                pe.wait_ge(S["rot_out"], 2)
                if h:
                    pe.wait_ge(S["rt_p"], h)
                mm(pb[3][:, 0:T], rkT[:, h, 0:P], rqT[:, h, :], start=True, stop=True)
                mm(pb[3][:, T:384], rkT[:, h, P:T], rqT[:, h, P:T], start=True, stop=True).then_inc(S["rt_s"], 1)
            if s == "rtB":
                pe.wait_ge(S["rt_p"], h + 1)
                if h:
                    pe.wait_ge(S["rt_ys"], h)
                else:
                    pe.wait_ge(S["act_evac2"], evac(GR2, last_of(GR2, "rv"))[1])
                for e in range(2):
                    v = slice(T * h + P * e, T * h + P * e + P)
                    mm(pb[4][:, T * e:T * e + T], rv[:, 0, v], pT[:, 0:T], start=True, stop=False)
                    last = mm(pb[4][:, T * e + P:T * e + T], rv[:, 1, v], pT[:, T:384], start=False, stop=True)
                last.then_inc(S["rt_y"], 1)
            if s == "rtC":
                pe.wait_ge(S["rt_ys"], h + 1)
                for e in range(2):
                    last = mm(pb[5][:, 0:T], ones[:, :], ys[:, e, :], start=e == 0, stop=e == 1)
                last.then_inc(S["rt_m"], 1)
            if s == "rtD":
                pe.wait_ge(S["rt_sq"], h + 1)
                for e in range(2):
                    last = mm(pb[6][:, 0:T], ones[:, :], yq[:, e, :], start=e == 0, stop=e == 1)
                last.then_inc(S["rt_v"], 1)

        def dl_step(s, h):
            if s == "dlA":
                if h == 0:
                    pe.wait_ge(S["act_evac2"], evac(GR2, last_of(GR2, "ak"))[1])
                    pe.wait_ge(S["rt_yc"], RH)
                else:
                    pe.wait_ge(S["dl_wt"], h)
                for g in range(GROUPS):
                    n = SLOTS * g + h
                    mm(pb[3][:, P * g:P * g + P], aqT[:, n, 0:P], akT[:, n, 0:P], start=True, stop=True)
                for g in range(GROUPS):
                    n = SLOTS * g + h
                    last = mm(pb[4 + g // 2][:, T * (g % 2):T * (g % 2) + T], aqT[:, n, P:T], akT[:, n, :], start=True, stop=True)
                last.then_inc(S["dl_s"], 1)
            if s == "dlB":
                pe.wait_ge(S["dl_p"], h + 1)
                for g in range(GROUPS):
                    for j, at in enumerate((P * g, 384 + T * g, 384 + T * g + P)):
                        last = nc.tensor.transpose(pb[3 + g][:, P * j:P * j + P], ds[:, at:at + P], ident)
                last.then_inc(S["dl_t"], 1)
            if s == "dlC":
                pe.wait_ge(S["dl_wt"], h + 1)
                if h:
                    pe.wait_ge(S["dl_out"], h)
                else:
                    pe.wait_ge(S["act_evac2"], evac(GR2, last_of(GR2, "av"))[1])
                for g in range(GROUPS):
                    v = slice(P * (SLOTS * g + h), P * (SLOTS * g + h) + P)
                    mm(pb[7][:, 0:T], av[:, 0, v], dwT[:, 384 * g:384 * g + T], start=g == 0, stop=False)
                    last = mm(pb[7][:, P:T], av[:, 1, v], dwT[:, 384 * g + T:384 * g + 384], start=False, stop=g == 2)
                last.then_inc(S["dl_o"], 1)

        for s, h in ORDER2:
            if s == "G":
                gemm2(h)
            elif s == "rot":
                rotary(h)
            elif s[0:2] == "rt":
                rt_step(s, h)
            elif s[0:2] == "dl":
                dl_step(s, h)

        norm(4, nsq, T)

        def turn_back(name, wait):
            for b in range(4):
                t, half = b // 2, b % 2
                for j in range(4):
                    if wait is not None:
                        pe.wait_ge(*wait(4 * half + j))
                    last = nc.tensor.transpose(pb[4 + b][:, P * j:P * j + P], hn[:, 4 * half + j, P * t:P * t + P], ident)
                last.then_inc(S[name], 1)

        turn_back("ht_mm", lambda t: (S["norm_s"], KT + t + 1))
        pe.wait_ge(S["moe_in"], 48)
        for t in range(2):
            for k in range(KT):
                last = mm(pb[1][:, E * t:E * t + E], hn[:, k, P * t:P * t + P], wr[:, k, :], start=k == 0, stop=k == KT - 1)
        last.then_inc(S["log_mm"], 1)
        pe.wait_ge(S["route"], 2)
        mm(pb[0][:, 0:E], tri, msk[:, 0, :], start=True, stop=True)
        mm(pb[0][:, E:2 * E], ones[:, :], msk[:, 0, :], start=True, stop=False)
        mm(pb[0][:, E:2 * E], tri, msk[:, 1, :], start=False, stop=True)
        mm(pb[0][0:1, 2 * E:3 * E], ones[:, 0:1], msk[:, 0, :], start=True, stop=False)
        mm(pb[0][0:1, 2 * E:3 * E], ones[:, 0:1], msk[:, 1, :], start=False, stop=True).then_inc(S["rank_mm"], 1)
        for t in range(2):
            last = nc.tensor.transpose(pb[2][0:E, P * t:P * t + P], gat[:, t, :], ident)
        last.then_inc(S["gt_mm"], 1)
        pe.wait_ge(S["gt_kept"], 1)
        pe.wait_ge(S["ht_kept"], 4)
        for b in range(4):
            for j in range(2):
                n = 2 * b + j
                last = mm(pb[4 + b][:, T * j:T * j + T], b2s[:, P * n:P * n + P], gatT, start=True, stop=True)
            last.then_inc(S["b2_mm"], 1)
        pe.wait_ge(S["rank_done"], 1)

        def scatter(r, n):
            since(pe, "acc_done", n)
            for j in range(2):
                for h in range(2):
                    v = slice(64 * h, 64 * h + 64)
                    last = mm(pb[6 + h][:, T * j:T * j + T], yv[v, P * (2 * r + j):P * (2 * r + j) + P], selT[v, :],
                              start=True, stop=True)
            last.then_inc(S["sc_mm"], 1)

        def up1(e, c):
            pe.wait_ge(inw[c], e * 16 + 16)
            for k in range(2):
                for b in range(2):
                    for h in range(2):
                        last = mm(pb[b][64 * h:64 * h + 64, :], XgT[:, 2 * c + k, :], slot(c, 2)[:, k, 1024 * h + 512 * b:1024 * h + 512 * b + 512],
                                  start=c == 0 and k == 0, stop=False, skip_group_check=True)
            last.then_inc(S["u_mm"], 1)

        def expert(e, cur, prev):
            if cur:
                pe.wait_ge(S["selu"], e + 1)
                since(pe, "xg", e)
                for k in range(KT):
                    for t in range(2):
                        last = mm(pb[3][:, 64 * k:64 * k + 64], htok[:, t, P * k:P * k + P], selU[:, t, :], start=t == 0, stop=t == 1)
                last.then_inc(S["gath"], 1)
            if prev:
                since(pe, "a_done", e)
                since(pe, "at", e - 1)
                for j in range(4):
                    last = nc.tensor.transpose(pb[4][:, P * j:P * j + P], aa[:, P * j:P * j + P], ident)
                last.then_inc(S["at_mm"], 1)
                since(pe, "selg", e)
                since(pe, "selt", e - 1)
                for t in range(2):
                    last = nc.tensor.transpose(pb[5][:, P * t:P * t + P], selG[:, t, :], ident)
                last.then_inc(S["selt_mm"], 1)
            if cur:
                pe.wait_ge(S["xg"], e + 1)
                since(pe, "u_read", e)
                up1(e, 0)
                up1(e, 1)
            if prev:
                since(pe, "at", e)
                since(pe, "yv_done", e - 1)
                for c in range(2):
                    pe.wait_ge(inw[4 + c], e * 16)
                    for k in range(4):
                        for h in range(2):
                            last = mm(pb[2][64 * h:64 * h + 64, :], aT[:, k, 64 * c:64 * c + 64], slot(4 + c, 4)[:, k, 512 * h:512 * h + 512],
                                      start=c == 0 and k == 0, stop=c == 1 and k == 3, skip_group_check=True)
                    last.then_inc(S["y_mm"], 1)
            if cur:
                up1(e, 2)
            if prev:
                since(pe, "yv_done", e)
                since(pe, "selt", e)
                scatter(0, e * 2 - 2)
            if cur:
                up1(e, 3)
                pe.wait_ge(S["b1_in"], e * 16 + 16)
                for b in range(2):
                    for h in range(2):
                        last = mm(pb[b][64 * h:64 * h + 64, :], ones[:, 0:64], b1p[:, 1024 * h + 512 * b:1024 * h + 512 * b + 512],
                                  start=False, stop=True, skip_group_check=True)
                last.then_inc(S["u_mm"], 1)
            if prev:
                scatter(1, e * 2 - 1)

        expert(0, True, False)
        expert(1, True, True)
        with pe.Fori(2, E) as e:
            expert(e, True, True)
        expert(E, False, True)

        def again(e, n, r):
            pe.wait_ge(S["over_dve"], n * 7 + 2)
            for k in range(KT):
                for t in range(2):
                    last = mm(pb[3][:, 64 * k:64 * k + 64], htok[:, t, P * k:P * k + P], selU[:, t, :], start=t == 0, stop=t == 1)
            last.then_inc(S["over_pe"], 1)
            for t in range(2):
                last = nc.tensor.transpose(pb[5][:, P * t:P * t + P], selG[:, t, :], ident)
            last.then_inc(S["over_pe"], 1)
            pe.wait_ge(S["over_act"], n * 5 + 1)
            pe.wait_ge(S["over_in"], n * 112 + 112)
            for k in range(KT):
                for b in range(2):
                    for h in range(2):
                        mm(pb[b][64 * h:64 * h + 64, :], XgT[:, k, :], slot(k // 2, 2)[:, k % 2, 1024 * h + 512 * b:1024 * h + 512 * b + 512],
                           start=k == 0, stop=False, skip_group_check=True)
            for b in range(2):
                for h in range(2):
                    last = mm(pb[b][64 * h:64 * h + 64, :], ones[:, 0:64], b1p[:, 1024 * h + 512 * b:1024 * h + 512 * b + 512],
                              start=False, stop=True, skip_group_check=True)
            last.then_inc(S["over_pe"], 1)
            pe.wait_ge(S["over_dve"], n * 7 + 5)
            for j in range(4):
                last = nc.tensor.transpose(pb[4][:, P * j:P * j + P], aa[:, P * j:P * j + P], ident)
            last.then_inc(S["over_pe"], 1)
            pe.wait_ge(S["over_act"], n * 5 + 4)
            for k in range(KT):
                for h in range(2):
                    last = mm(pb[2][64 * h:64 * h + 64, :], aT[:, k % 4, 64 * (k // 4):64 * (k // 4) + 64],
                              slot(4 + k // 4, 4)[:, k % 4, 512 * h:512 * h + 512], start=k == 0, stop=k == KT - 1, skip_group_check=True)
            last.then_inc(S["over_pe"], 1)
            pe.wait_ge(S["over_act"], n * 5 + 5)
            for q in range(2):
                if q:
                    pe.wait_ge(S["over_dve"], n * 7 + 6)
                for j in range(2):
                    for h in range(2):
                        v = slice(64 * h, 64 * h + 64)
                        last = mm(pb[6 + h][:, T * j:T * j + T], yv[v, P * (2 * q + j):P * (2 * q + j) + P], selT[v, :],
                                  start=True, stop=True)
                last.then_inc(S["over_pe"], 1)

        pe.sem_inc(S["over_pe"], 1)
        further(pe, again)
        norm(5, nsq, T)
        turn_back("fin_mm", lambda t: (S["norm_x"], 5 * KT + t + 1))


_INS = ["x", "meta", "norm_mix_g", "w_in", "w_gate", "b_gate", "lam_q1", "lam_k1", "lam_q2", "lam_k2", "subln_g",
        "w_br_sb", "w_br_df", "w_out", "norm_ffn_g", "w_ffn_gate", "w_ffn_up", "w_ffn_down", "norm_final_g", "c_2",
        "w_ada_2", "b_ada_2", "g_mix_2", "w_in_2", "rel_bias_2", "w_ret_o_2", "w_att_o_2", "w_o_2", "g_ffn_2",
        "w_router_2", "b_router_2", "w_mlp1_2", "b_mlp1_2", "w_mlp2_2", "b_mlp2_2", "g_final_2"]


def kernel(**inputs):
    import numpy as _np
    import concourse.bacc as _bacc
    from concourse import mybir as _mybir
    from concourse.bass_utils import run_bass_kernel_spmd as _run

    nc = _bacc.Bacc("TRN2", target_bir_lowering=False, num_devices=1)
    arrays, args = {}, {}
    for name in _INS:
        arrays[f"in_{name}"] = _np.ascontiguousarray(inputs[name])
    for name, table in zip(("cst", "tab", "hot", "bad"), constants()):
        arrays[f"in_{name}"] = table
    for name, v in arrays.items():
        args[name[3:]] = nc.dram_tensor(name, v.shape, _mybir.dt.from_np(v.dtype), kind="ExternalInput").ap()
    args["toep"] = nc.dram_tensor("toep", (GROUPS * SLOTS, TOEP), F32, kind="Internal").ap()
    args["toeps"] = nc.dram_tensor("toeps", (P, GROUPS * SLOTS * TOEP), F32, kind="Internal").ap()
    args["out"] = nc.dram_tensor("out_0", (1, T, D), F32, kind="ExternalOutput").ap()
    with ExitStack() as ctx:
        program(nc, args, ctx)
    r = _run(nc, [arrays], core_ids=[0])
    return r.results[0]["out_0"]
```

```python
from contextlib import ExitStack

import concourse.bass as bass
import numpy as np
from concourse import mybir

F32 = mybir.dt.float32
F32R = mybir.dt.float32r
U32 = mybir.dt.uint32
I32 = mybir.dt.int32
ALU = mybir.AluOpType
ACT = mybir.ActivationFunctionType
AX = mybir.AxisListType

P = 128
D = 1024
KT = D // P
T = 256
M = 16
TM = T + M
HEADS = 8
FF = 2816
FT = FF // P
E = 32
CAP = 64
RH = 4
GROUPS = 3
SLOTS = 4
DIL = ((128, 1), (512, 4), (2048, 16))
TOEP = 384
EPS = 1e-6
GN_EPS = 1e-5
LAM_INIT = 0.2
SB_SCALE = 128 ** -0.5
NEG = -1e30

VEC_ROWS = (("norm_mix_g", 8), ("b_gate", 16), ("norm_ffn_g", 8), ("norm_final_g", 8), ("c", 8), ("b_ada", 48),
            ("g_mix", 8), ("g_ffn", 8), ("g_final", 8), ("subln_g", 1))
VROW = {}
for _name, _n in VEC_ROWS:
    VROW[_name] = sum(n for _, n in VEC_ROWS[:len(VROW)])
NVEC = sum(n for _, n in VEC_ROWS)

C_ID, C_NTRI, C_TRI, C_NEGM, C_SWAP, C_IOTA, C_IE, C_DIST, C_SEL = 0, 128, 256, 384, 512, 640, 768, 800, 1216
NCST = C_SEL + M


def constants():
    f = np.float32
    i = np.arange(P)
    cst = np.zeros((P, NCST), f)
    cst[:, C_ID:C_ID + P] = np.eye(P)
    cst[:, C_NTRI:C_NTRI + P] = -(i[:, None] >= i[None, :]).astype(f)
    cst[:, C_TRI:C_TRI + P] = (i[:, None] < i[None, :])
    cst[:, C_NEGM:C_NEGM + P] = np.where(i[:, None] < i[None, :], 0, NEG)
    cst[:, C_SWAP:C_SWAP + P] = np.eye(P)[(i + 64) % P]
    cst[:, C_IOTA:C_IOTA + P] = np.where(i % 64 < CAP, i % 64, -9)[None, :]
    cst[:, C_IE:C_IE + E] = np.arange(E)[None, :]
    cst[:, C_SEL:C_SEL + M] = (i[:, None] % 32 == np.arange(M)[None, :])
    keys = np.arange(TM)
    for qt in range(2):
        q = M + P * qt + i
        n = M + P * (qt + 1)
        cid = lambda t: np.where(t < M, 0, (t - M) // 64 + 1)
        dist = np.where(cid(keys[:n])[None, :] <= cid(q)[:, None], -np.abs(q[:, None] - keys[None, :n]), NEG)
        at = C_DIST + (M + P) * qt
        cst[:, at:at + n] = dist
    tab = np.zeros((P, 6, T), f)
    t = np.arange(T, dtype=f)
    logg = np.log1p(-np.exp2(-5.0 - np.arange(RH, dtype=f))).astype(f)
    diff = t[None, :] - i[:, None].astype(f)
    for h in range(RH):
        tab[:, h] = np.where(diff >= 0, np.exp(np.maximum(diff, 0).astype(f) * logg[h]), 0)
    inv = (f(10000.0) ** (-np.arange(64, dtype=f) / f(64))).astype(f)
    ang = (t[None, :] * inv[i % 64][:, None]).astype(f)
    tab[:, 4] = np.cos(ang)
    tab[:, 5] = np.sin(ang) * np.where(i < 64, -1, 1)[:, None]
    hot = np.zeros((E, GROUPS, TOEP), f)
    bad = np.zeros((SLOTS, GROUPS, TOEP), f)
    for g, (w, r) in enumerate(DIL):
        for n in range(TOEP):
            dist = 255 - n
            if dist < 0 or dist % r or dist > w:
                bad[:, g, n] = NEG
                continue
            if dist < 16:
                b = dist
            else:
                ratio = np.log(f(dist) / f(16)) / f(np.log(128.0))
                b = min(16 + int(f(ratio) * 16), 31)
            hot[b, g, n] = 1
    return cst, tab, hot, bad


def group_list(pieces):
    out = []
    for p, (kind, count, part) in enumerate(pieces):
        out += [(p, kind, n, count * part + n) for n in range(count)]
    return out


PIECES1 = ([(side + kind, n, i) for side in "sd" for i in range(2) for kind, n in (("q", 4), ("k", 4), ("v", 4))]
           + [("gate", 4, i) for i in range(4)]
           + [(k, 4, i) for k in ("ysb", "ydf", "out") for i in range(2)])
COL1 = {"sq": 0, "sk": 2, "sv": 4, "dq": 6, "dk": 8, "dv": 10}
PIECES2 = ([("rq", 4, 0), ("rk", 4, 0)] + [("rv", 2, i) for i in range(2)] + [("rg", 4, i) for i in range(2)]
           + [(k, n, i) for k, n in (("aq", 4), ("ak", 4), ("av", 2)) for i in range(3)]
           + [("gab", 4, i) for i in range(4)] + [("yatt", 8, 0)] + [("yret", 4, i) for i in range(2)]
           + [("o", 4, i) for i in range(2)])
GR1, GR2 = group_list(PIECES1), group_list(PIECES2)
DVE_KINDS = ("rg", "ysb", "ydf", "out", "yret", "yatt", "o")


def where(groups, kind, c=0):
    return next(g for g, x in enumerate(groups) if x[1] == kind and x[3] == c)


def first_of(groups, kind):
    return where(groups, kind)


def last_of(groups, kind):
    return max(g for g, x in enumerate(groups) if x[1] == kind)


def evac(groups, g):
    dve = groups[g][1] in DVE_KINDS
    return dve, sum((x[1] in DVE_KINDS) == dve for x in groups[:g + 1])


def unit_list(groups, pieces):
    out = []
    for p, (kind, _, _) in enumerate(pieces):
        mine = [g for g, x in enumerate(groups) if x[0] == p]
        if kind in ("rv", "av"):
            out += [[], [], [], mine]
        elif kind == "yatt":
            out += [mine[2 * i:2 * i + 2] for i in range(4)]
        else:
            out += [[g] for g in mine]
    return out


UNITS2 = unit_list(GR2, PIECES2)


def unit_of(kind):
    return 4 * next(p for p, x in enumerate(PIECES2) if x[0] == kind)


def weave(count, *chains):
    timed = [(g, 1, 0, "G", g) for g in range(count)]
    for start, period, heads, steps in chains:
        for h in range(heads):
            timed += [(start + period * h + at, 0, -h, s, h) for s, at in steps.items()]
    return [x[3:] for x in sorted(timed, key=lambda x: x[0:3])]


def order1():
    return weave(len(GR1), (SB_AT, 3, HEADS, {"sbA": 0, "sbB": 2, "sbC": 3}),
                 (SB_AT + 3 * HEADS + 1, 3, HEADS, {"dfA": 0, "dfB": 2, "dfC": 3, "dfD": 4}),
                 (first_of(GR1, "gate") + 4, 4, 4, {"gates": 0}),
                 (first_of(GR1, "out") + 2, 1, SQUARED, {"square": 0}),
                 (G0 - 8, 2, 2, {"sbS": 0}), (G0 + 2, 2, 2, {"dfS": 0}), (G0 + 10, 1, KT - 1, {"mS": 0}),
                 (G0 + 16, 1, 1, {"mL": 0}), (G0 - 2, 1, 3, {"split": 0}))


def order2():
    av, gab, yret = (unit_of(k) for k in ("av", "gab", "yret"))
    return weave(len(UNITS2), (4, 1, 1, {"toep": 0}), (5, 4, 2, {"rot": 0}),
                 (22, 6, RH, {"rtA": 0, "rtB": 2, "rtC": 4, "rtD": 6}),
                 (av + 7, 4, SLOTS, {"dlA": 0, "dlE": 1, "dlN": 2, "dlB": 3.9, "dlC": 5}),
                 (gab + 4, 4, 4, {"gates": 0}),
                 (gab + 16, 2, 2, {"rgS": 0}), (gab + 14, 1, 1, {"atS": 0}), (yret + 2, 1, KT - 1, {"m2S": 0}), (unit_of("o"), 1, 1, {"m2L": 0}),
                 (unit_of("o") + 2, 1, SQUARED, {"square": 0}))


SB_AT = 12
SPLIT1 = 16
G0 = next(g for g, x in enumerate(GR1) if x[0] == SPLIT1)
SQUARED = 6
ORDER1, ORDER2 = order1(), order2()


class Count:

    def __init__(self, eng, sem):
        self.eng, self.sem, self.n = eng, sem, 0

    def do(self, ins):
        ins.then_inc(self.sem, 1)
        self.n += 1
        return self.n

    def wait(self, n=None):
        self.eng.wait_ge(self.sem, self.n if n is None else n)


def program(nc, a, ctx):
    def sb(name, shape, dt=F32):
        return ctx.enter_context(nc.sbuf_tensor("s_" + name, shape, dt))

    def sem(name):
        return ctx.enter_context(nc.semaphore(name))

    def area(base, at, *dims):
        n = 1
        for d in dims:
            n *= d
        v = base[:, at:at + n]
        return v.rearrange("p (a b) -> p a b", a=dims[0]) if len(dims) == 2 else v

    base = -(-nc.sbuf_base // 32) * 32
    ring = sb("ring", [P, 6, 4096])
    W = sb("W", [P, 23680])
    hT = sb("hT", [P, KT, TM])
    cst = sb("cst", [P, NCST])
    ones = sb("ones", [P, P])
    nones = sb("nones", [P, P])
    vec = sb("vec", [P, NVEC])
    vx = sb("vx", [P, 64])
    sml = sb("sml", [P, 64])
    modT = sb("modT", [P, 48])
    taken = sml[:, 40:41]
    rks = sml[:, 42:44]
    topi = sb("topi", [P, 2, 8], U32)
    cnti = sb("cnti", [1, E + 1], I32)
    cntf = sb("cntf", [1, E + 1])
    banks = ctx.enter_context(nc.psum_tensor("banks", [P, 8, 512], F32))
    pb = [banks[:, n, :] for n in range(8)]
    hx = hT[:, :, M:TM]
    lent = ring[:, 0:3, :].rearrange("p a b -> p (a b)")
    ident = cst[:, C_ID:C_ID + P]
    ntri = cst[:, C_NTRI:C_NTRI + P]
    tri = cst[:, C_TRI:C_TRI + P]
    negm = cst[:, C_NEGM:C_NEGM + P]
    swap = cst[:, C_SWAP:C_SWAP + P]
    iotac = cst[:, C_IOTA:C_IOTA + P]
    iotae = cst[:, C_IE:C_IE + E]
    selm = cst[:, C_SEL:C_SEL + M]
    distt = cst[:, C_DIST:C_DIST + 416]
    gsub, lamc = vx[:, 16:17], vx[:, 17:20]
    gsa, gsf, epsc, gnepsc = vx[:, 20:28], vx[:, 28:36], vx[:, 36:37], vx[:, 37:38]
    onec = vx[:, 38:39]
    csil = vx[:, 40:48]

    def two(ap):
        return ap[:, 0:512].rearrange("p (a b) -> p a b", a=2)[:, :, 0:P]

    def bc(ap, n):
        return ap.unsqueeze(1).broadcast_to([ap.shape[0], n, ap.shape[1]])

    def rounded(name, in_ring, at, *dims):
        return nc.alloc_sbuf_tensor_at("r_" + name, [P, *dims], F32R, offset=base + 4 * (at + (0 if in_ring else 6 * 4096)))


    xtok = area(lent, 8192, 2, D)
    mtok = lent[0:M, 4096:4096 + D]
    vrow = lent[0:NVEC, 5120:5248]
    lamv = area(lent, 5376, 4, 64)
    sqa = area(lent, 0, KT, TM)
    sqa1 = area(W, 13696, KT, T)
    rms = lent[:, 2176:2176 + TM]
    xn = area(W, 0, KT, TM)
    sqT = area(W, 2176, HEADS, T)
    skT = area(W, 4224, HEADS, TM)
    sv = area(W, 6400, 3, D)
    dqT = area(W, 9472, HEADS, T)
    dkT = area(W, 11520, HEADS, TM)
    dv = area(W, 13696, 3, D)
    gate = area(W, 16768, 16, T)
    mT = area(W, 20864, KT, T)
    zs, ex, sp, la = (lent[:, 640 * n:640 * n + 640] for n in range(4))
    sc = area(lent, 2560, 2, 416)
    wv = lent[:, 3392:3392 + 416]
    wT = lent[:, 3808:4448]
    osq = lent[:, 4448:4704]
    ors = lent[:, 4704:4960]
    dtmp = lent[:, 4960:5216]
    xf = area(W, 0, KT, T)
    xfh, xfl = rounded("xfh", False, 7808, KT, T), rounded("xfl", False, 9856, KT, T)
    fh, fl = rounded("fh", False, 11904, FT, T), rounded("fl", False, 17536, FT, T)
    wh, wl = rounded("wh", False, 2176, 4, D), rounded("wl", True, 0, 4, D)
    fe = area(lent, 4096, 2, T)
    fr = area(lent, 4608, 2, T)
    adac = area(lent, 5120, 2, 512)
    ft = area(lent, 6144, 2, T)
    vmeta = lent[:, 6144:6656]
    xn2 = area(W, 17408, KT, T)
    x2h, x2l = rounded("x2h", False, 0, KT, T), rounded("x2l", False, 21504, KT, T)
    m2T = area(W, 0, KT, T)
    m2h, m2l = rounded("m2h", False, 2048, KT, T), rounded("m2l", False, 21504, KT, T)
    yh, yl = rounded("yh", False, 4224, KT, T), rounded("yl", False, 6400, KT, T)
    dfh, dfl = rounded("dfh", False, 11520, HEADS, T), rounded("dfl", False, 13696, HEADS, T)
    rgl, rgh = rounded("rgl", False, 9216, KT, T), rounded("rgh", False, 11264, KT, T)
    atth, attl = rounded("atth", False, 13312, SLOTS, T), rounded("attl", False, 14336, SLOTS, T)
    w2h = rounded("w2h", True, 3 * 4096, 4, 1024)
    w2l = rounded("w2l", True, 4 * 4096, 4, 2048)
    rqT = area(W, 2048, RH, T)
    rkT = area(W, 3072, RH, T)
    rv = area(W, 4096, 2, D)
    rg = area(W, 6144, KT, T)
    aqT = area(W, 8192, 12, T)
    akT = area(W, 11264, 12, T)
    av = area(W, 14336, 2, 1536)
    gab = area(W, 17408, 16, T)
    attT = area(W, 8192, SLOTS, T)
    bad = W[0:SLOTS, 8192:8192 + GROUPS * TOEP].rearrange("p (a b) -> p a b", a=GROUPS)
    raw = area(lent, 2560, 2, 1024)
    tab = area(lent, 4608, 6, T)
    BT = area(lent, 6144, 12, T)
    pT = lent[:, 9216:9600]
    ys = area(lent, 9600, 2, T)
    yq = area(lent, 10112, 2, T)
    yr = lent[:, 10624:10880]
    rsg = area(lent, 10880, 2, T)
    ds = lent[:, 0:1152]
    dwT = lent[:, 1152:2304]
    stg = lent[0:SLOTS, 9216:9216 + GROUPS * TOEP].rearrange("p (a b) -> p a b", a=GROUPS)
    hot = lent[0:E, 10368:10368 + GROUPS * TOEP].rearrange("p (a b) -> p a b", a=GROUPS)
    relb = lent[0:E, 11520:11532]
    dtmp2 = W[:, 4096:4352]
    hn = area(W, 0, KT, T)
    htok = area(W, 2048, 2, D)
    acc = area(W, 4096, KT, T)
    selU = area(W, 6144, 2, 64)
    selG = area(W, 6272, 2, P)
    selT = W[:, 6528:6784]
    XgT = area(W, 6784, KT, 64)
    gl = W[:, 7296:7808]
    li = W[:, 7808:8320]
    sg = W[:, 8320:8832]
    aa = W[:, 8832:9344]
    aT = area(W, 9344, 4, P)
    yv = W[:, 9856:10368]
    b1p = W[:, 10368:12416]
    wr = area(W, 12416, KT, E)
    b2s = W[0:E, 12672:13696]
    brow = W[:, 13696:13728]
    lg = area(W, 13728, 2, E)
    top8 = area(W, 13792, 2, 8)
    tif = area(W, 13824, 2, 8)
    gts = area(W, 13840, 2, 8)
    one = area(W, 13856, 2, E)
    msk = area(W, 13920, 2, E)
    gat = area(W, 13984, 2, E)
    rank = area(W, 18720, 2, E + 1)
    gatT = W[0:E, 14112:14368]
    otok = area(W, 14368, 2, D)
    nsq = area(W, 16416, KT, T)
    nrms = W[:, 18464:18720]

    S = {n: sem(n) for n in (
        "x_in", "vec_in", "cst_in", "lam_in", "tab_in", "hot_in", "toep_out", "toep_in", "moe_in", "b1_in", "stored",
        "x_turned", "x_kept", "vec_turned", "vec_kept", "filled", "lam_sum", "lam_exp", "csil",
        "norm_sq", "norm_ms", "norm_r", "norm_x", "norm_s",
        "gemm1", "act_evac1", "dve_evac1", "gate_done", "gemm2", "act_evac2", "dve_evac2", "gab_done", "rg_exp",
        "v_unit", "w1_hi", "w1_lo", "y_hi", "y_lo",
        "sb_scores", "sb_zs", "sb_min", "sb_ln", "sb_sp", "sb_rest", "sb_la", "sb_a", "sb_o", "sb_out",
        "df_scores", "df_s", "df_max", "df_exp", "df_w", "df_tr", "df_wt", "df_o", "df_sq", "df_ms", "df_rs", "df_out",
        "x_hi", "x_lo", "w_hi", "w_lo", "up", "up_free", "up_sig", "up_step", "ada_scaled", "ada_step", "ada_more", "ada_sum", "ada_mm", "down", "down_out", "mod_done", "toep_mm", "toep_sum",
        "rot_mm", "rot_out", "rt_s", "rt_p", "rt_y", "rt_ys", "rt_m", "rt_yc", "rt_sq", "rt_v", "rt_r", "rt_out",
        "dl_s", "dl_b", "dl_max", "dl_e", "dl_p", "dl_t", "dl_wt", "dl_o", "dl_out",
        "act_step", "dve_step", "ht_mm", "ht_kept", "log_mm", "log_exp", "route", "rank_mm", "rank_done",
        "gt_mm", "gt_kept", "b2_mm", "acc_init",
        "selu", "selg", "selt_mm", "selt", "gath", "xg", "u_mm", "u_read", "u_sig", "a_mid", "a_done", "at_mm", "at", "y_mm", "yv_done",
        "sc_mm", "acc_done",
        "over_in", "over_pe", "over_act", "over_dve", "round", "final_sum", "fin_mm", "fin_kept")}
    in1 = [sem(f"piece1_in{b}") for b in range(2)]
    inu = [sem(f"up_in{b}") for b in range(2)]
    ina = [sem(f"ada_in{b}") for b in range(2)]
    ind = [sem(f"down_in{b}") for b in range(2)]
    in2 = [sem(f"half_in{b}") for b in range(4)]
    inw = [sem(f"expert_in{b}") for b in range(6)]

    w_in, w_gate, w_in2 = a["w_in"][0], a["w_gate"][0], a["w_in_2"][0]

    def cols(w, c):
        return w[:, 512 * c:512 * c + 512].rearrange("(k p) n -> p k n", p=P)

    pieces1 = ([cols(w_in, COL1[kind] + part) for kind, _, part in PIECES1[:12]] + [cols(w_gate, c) for c in range(4)]
               + [cols(a[n][0], c) for n in ("w_br_sb", "w_br_df", "w_out") for c in range(2)])
    COL2 = {"rq": 0, "rk": 1, "rv": 2, "rg": 4, "aq": 6, "ak": 9, "av": 12, "gab": 15}
    out2 = {"yret": a["w_ret_o_2"][0], "yatt": a["w_att_o_2"][0], "o": a["w_o_2"][0]}

    def half2(m):
        kind, _, part = PIECES2[m // 2]
        c = 512 * (COL2.get(kind, 0) + part)
        w, h = out2.get(kind, w_in2), m % 2
        if kind in ("rv", "av"):
            w = w[512 * h:512 * h + 512, c:c + 512]
        elif kind == "yatt":
            w = w[:, 512 * h:512 * h + 512]
        else:
            w = w[:, c + T * h:c + T * h + T]
        return w.rearrange("(k p) n -> p k n", p=P)

    def unit2(buf, n):
        kind = PIECES2[n // 4][0]
        half = buf[:, (2, 3, 0, 1)[n // 2 % 4], :].rearrange("p (k n) -> p k n", k=KT if kind not in ("rv", "av", "yatt") else 4)
        j = n % 2
        if kind in ("rv", "av"):
            return half[:, 2 * j:2 * j + 2, :]
        w = T if kind == "yatt" else P
        return half[:, :, w * j:w * j + w]

    def unit1(buf, n):
        return buf[:, n // 2 % 4, :].rearrange("p (k n) -> p k n", k=KT)[:, :, P * (n % 2):P * (n % 2) + P]

    raw2 = ring[:, 4:6, :].rearrange("p a (b n) -> p (a b) n", b=2)

    def unit_used(eng, n):
        if UNITS2[n]:
            eng.wait_ge(S["gemm2"], UNITS2[n][-1] + 1)
        else:
            eng.wait_ge(S["v_unit"], sum(not gs for gs in UNITS2[:n + 1]))

    up_g, up_u, down, w_ada = (a[n][0] for n in ("w_ffn_gate", "w_ffn_up", "w_ffn_down", "w_ada_2"))
    w1, w2 = a["w_mlp1_2"][0], a["w_mlp2_2"][0]
    ends1 = [max(g for g, x in enumerate(GR1) if x[0] == p) + 1 for p in range(len(PIECES1))]
    UPS, ADAS = FF // T, 12
    DOWNS = [4, 4, 4, 4, 4, 2]

    ADA_SCALED = 6
    MLP_GROUPS = 4 * UPS + FT


    def slot(n, k=KT):
        return ring[:, n, :].rearrange("p (k n) -> p k n", k=k)

    def up_group(b, i):
        at = T * (i % 2) + P * (i // 2)
        return slot(4 + b)[:, :, at:at + P]

    def down_group(kk):
        return slot(4 + (kk // 4 + 1) % 2, 4)[:, kk % 4:kk % 4 + 1, :]

    def since(eng, name, n):
        if not isinstance(n, int) or n > 0:
            eng.wait_ge(S[name], n)

    def further(eng, each, begin=None):
        eng.wait_ge(S["rank_done"], 1)
        most = eng.value_load(cnti[0:1, E:E + 1], min_val=0, max_val=T)
        with eng.If(most > CAP):
            done = eng.alloc_register("passes")
            eng.reg_mov(done, 0)
            with eng.Fori(1, T // CAP) as r:
                if begin is not None:
                    begin(r)
                with eng.Fori(0, E) as e:
                    here = eng.value_load(cnti[0:1, bass.ds(e, 1)], min_val=0, max_val=T)
                    with eng.If(here > r * CAP):
                        each(e, eng.snap(done), r)
                        eng.reg_add(done, done, 1)

    block = ctx.enter_context(nc.Block())

    @block.sync
    def _(sp):
        def piece1(p):
            if p >= 2:
                sp.wait_ge(S["gemm1"], ends1[p - 2])
            sp.dma_start(slot(4 + p % 2), pieces1[p]).then_inc(in1[p % 2], 16)

        sp.dma_start(cst[:, :], a["cst"]).then_inc(S["cst_in"], 16)
        sp.dma_start(xtok, a["x"][0].rearrange("(a p) d -> p a d", p=P)).then_inc(S["x_in"], 16)
        sp.dma_start(mtok, a["meta"]).then_inc(S["x_in"], 16)
        for p in range(SPLIT1):
            piece1(p)
        for m in range(2 * (len(pieces1) - SPLIT1)):
            p = SPLIT1 + m // 2
            sp.wait_ge(S["gemm1"], ends1[p - 2] if m < 4 else G0 + 2 * m - 6)
            half = raw2[:, m % 4, :].rearrange("p (k n) -> p k n", k=KT)
            sp.dma_start(half, pieces1[p][:, :, T * (m % 2):T * (m % 2) + T]).then_inc(in2[m % 4], 16)

        def up(j, b):
            src = [w[:, bass.ds(j * T, T)].rearrange("(k p) n -> p k n", p=P) for w in (up_g, up_u)]
            sp.dma_start(slot(4 + b)[:, :, 0:T], src[0]).then_inc(inu[b], 16)
            sp.dma_start(slot(4 + b)[:, :, T:512], src[1]).then_inc(inu[b], 16)

        def ada(j, b):
            sp.dma_start(slot(2 + b), w_ada[:, bass.ds(j * 512, 512)].rearrange("(k p) n -> p k n", p=P))\
              .then_inc(ina[b], 16)

        for b in range(2):
            sp.wait_ge(S["gemm1"], ends1[len(pieces1) - 2 + b])
            up(b, b)
            ada(b, b)
        with sp.Fori(1, UPS // 2) as i:
            for b in range(2):
                sp.wait_ge(S["w_lo"], i * 8 + (4 * b - 4))
                up(i * 2 + b, b)
                sp.wait_ge(S["ada_sum"], i * 2 + (b - 1))
                ada(i * 2 + b, b)
        sp.wait_ge(S["w_lo"], 4 * (UPS - 2))
        up(UPS - 1, 0)
        sp.wait_ge(S["ada_sum"], ADAS - 3)
        ada(ADAS - 2, 0)
        for j, k in enumerate(DOWNS):
            if j == 1:
                sp.wait_ge(S["ada_sum"], ADAS - 2)
                ada(ADAS - 1, 1)
            sp.wait_ge(S["w_lo"], 4 * (UPS - 1 + j))
            b = (j + 1) % 2
            sp.dma_start(slot(4 + b, 4)[:, 0:k, :], down[512 * j:512 * j + P * k, :].rearrange("(k p) n -> p k n", p=P))\
              .then_inc(ind[b], 16)

        for m in range(2 * len(PIECES2)):
            if m < 4:
                sp.wait_ge(S["w_lo"], 4 * UPS + sum(DOWNS[:5 + m // 2]))
            else:
                unit_used(sp, 2 * m - 7)
            half = raw2[:, (2, 3, 0, 1)[m % 4], :]
            src = half2(m)
            sp.dma_start(half.rearrange("p (k n) -> p k n", k=src.shape[1]), src).then_inc(in2[m % 4], 16)

        sp.wait_ge(S["dl_out"], SLOTS)
        sp.wait_ge(S["rt_out"], RH)
        for c in range(3):
            sp.dma_start(slot(c, 2), w1[0, T * c:T * c + T, :].rearrange("(k p) n -> p k n", p=P)).then_inc(inw[c], 16)

        def first(e, c):
            sp.dma_start(slot(c, 2), w1[bass.ds(e, 1), T * c:T * c + T, :].rearrange("e (k p) n -> p (e k) n", p=P))\
              .then_inc(inw[c], 16)

        def second(e, c):
            sp.dma_start(slot(4 + c, 4), w2[bass.ds(e, 1), 512 * c:512 * c + 512, :].rearrange("e (k p) n -> p (e k) n", p=P))\
              .then_inc(inw[4 + c], 16)

        def bias(e):
            sp.dma_start(b1p[0:1, :], a["b_mlp1_2"][0, bass.ds(e, 1), :]).then_inc(S["b1_in"], 16)

        sp.wait_ge(S["filled"], 2)
        bias(0)
        sp.wait_ge(S["gemm2"], len(GR2))
        sp.dma_start(slot(3, 2), w1[0, 3 * T:4 * T, :].rearrange("(k p) n -> p k n", p=P)).then_inc(inw[3], 16)

        def load(e, w2_too=True):
            for c in range(2):
                sp.wait_ge(S["u_mm"], e * 5 + (c - 4))
                first(e, c)
            if w2_too:
                sp.wait_ge(S["y_mm"], e * 2 - 2)
                for c in range(2):
                    second(e - 1, c)
            for c in range(2, 4):
                sp.wait_ge(S["u_mm"], e * 5 + (c - 4))
                first(e, c)
            sp.wait_ge(S["u_mm"], e * 5)
            bias(e)

        for c in range(2):
            second(0, c)
        load(1, False)
        with sp.Fori(2, E) as e:
            load(e)
        sp.wait_ge(S["y_mm"], 2 * E - 2)
        for c in range(2):
            second(E - 1, c)

        def again(e, n, r):
            sp.wait_ge(S["over_pe"], n * 7 + 1)
            for c in range(4):
                sp.dma_start(slot(c, 2), w1[bass.ds(e, 1), T * c:T * c + T, :].rearrange("e (k p) n -> p (e k) n", p=P))\
                  .then_inc(S["over_in"], 16)
            for c in range(2):
                sp.dma_start(slot(4 + c, 4), w2[bass.ds(e, 1), 512 * c:512 * c + 512, :].rearrange("e (k p) n -> p (e k) n", p=P))\
                  .then_inc(S["over_in"], 16)
            sp.dma_start(b1p[0:1, :], a["b_mlp1_2"][0, bass.ds(e, 1), :]).then_inc(S["over_in"], 16)

        sp.wait_ge(S["y_mm"], 2 * E)
        further(sp, again)
        sp.wait_ge(S["fin_kept"], 4)
        sp.dma_start(a["out"][0].rearrange("(a p) d -> p a d", p=P), otok).then_inc(S["stored"], 16)
        sp.wait_ge(S["stored"], 16)

    @block.gpsimd
    def _(pool):
        pool.memset(ones[:, :], 1.0)
        pool.memset(nones[:, :], -1.0)
        pool.memset(epsc, EPS)
        pool.memset(gnepsc, GN_EPS)
        pool.memset(onec, 1.0).then_inc(S["filled"], 1)
        row = 0
        src = {"norm_mix_g": a["norm_mix_g"], "b_gate": a["b_gate"], "norm_ffn_g": a["norm_ffn_g"],
               "norm_final_g": a["norm_final_g"].unsqueeze(0), "c": a["c_2"], "b_ada": a["b_ada_2"], "g_mix": a["g_mix_2"],
               "g_ffn": a["g_ffn_2"], "g_final": a["g_final_2"].unsqueeze(0), "subln_g": a["subln_g"]}
        for name, n in VEC_ROWS:
            pool.dma_start(vrow[row:row + n, :], src[name].rearrange("a (r p) -> (a r) p", p=P)).then_inc(S["vec_in"], 16)
            row += n
        for n, name in enumerate(("lam_q1", "lam_q2", "lam_k1", "lam_k2")):
            pool.dma_start(lamv[:, n, :], a[name].partition_broadcast(P)).then_inc(S["lam_in"], 16)
        for j in range(ADAS):
            w, out = slot(2 + j % 2), adac[:, j % 2, :]
            pool.wait_ge(S["ada_scaled"], j + 1)
            pool.wait_ge(S["ada_mm"], j + 1)
            for k in range(1, ADA_SCALED):
                if k > 1:
                    pool.wait_ge(S["ada_step"], j * (ADA_SCALED - 1) + k - 1)
                nc.gpsimd.tensor_tensor(out, out if k > 1 else w[:, 0, :], w[:, k, :], ALU.add).then_inc(S["ada_step"], 1)
        pool.wait_ge(S["up_free"], FT + 2)
        pool.wait_ge(S["up_step"], 3 * FT)
        pool.wait_ge(S["ada_mm"], ADAS + 2)
        pool.wait_ge(S["norm_x"], 16)
        pool.dma_start(hot, a["hot"]).then_inc(S["hot_in"], 16)
        pool.dma_start(relb, a["rel_bias_2"]).then_inc(S["hot_in"], 16)
        pool.dma_start(tab, a["tab"]).then_inc(S["tab_in"], 16)
        pool.wait_ge(S["down"], 4)
        pool.dma_start(bad, a["bad"]).then_inc(S["hot_in"], 16)
        pool.wait_ge(S["toep_sum"], GROUPS)
        pool.dma_start(a["toep"].rearrange("(g s) n -> s g n", g=GROUPS), stg).then_inc(S["toep_out"], 16)
        pool.wait_ge(S["toep_out"], 16)
        n = GROUPS * SLOTS * TOEP
        pool.dma_start(a["toeps"], bass.AP(a["toep"].tensor, 0, [[0, P], [1, n]])).then_inc(S["toep_out"], 16)
        pool.wait_ge(S["toep_out"], 32)
        pool.dma_start(BT, bass.AP(a["toeps"].tensor, P - 1, [[n - 1, P], [TOEP, GROUPS * SLOTS], [1, T]]))\
            .then_inc(S["toep_in"], 16)
        pool.wait_ge(S["gemm2"], last_of(GR2, "yret") + 1)
        pool.memset(b1p, 0.0).then_inc(S["filled"], 1)
        pool.dma_start(wr, a["w_router_2"][0].rearrange("(k p) e -> p k e", p=P)).then_inc(S["moe_in"], 16)
        pool.dma_start(b2s, a["b_mlp2_2"][0]).then_inc(S["moe_in"], 16)
        pool.dma_start(brow, a["b_router_2"].partition_broadcast(P)).then_inc(S["moe_in"], 16)

    @block.scalar
    def _(act):
        st = Count(act, S["act_step"])

        def square(src, buf, n, t):
            act.activation(buf[:, t, 0:n], src[:, t, :], ACT.Square).then_inc(S["norm_sq"], 1)

        def root(k, r, n):
            act.wait_ge(S["norm_ms"], k + 1)
            st.do(act.activation(r[:, 0:n], pb[3][:, 0:n], ACT.Ln, bias=epsc, scale=1.0 / D))
            st.wait()
            act.activation(r[:, 0:n], r[:, 0:n], ACT.Exp, scale=-0.5).then_inc(S["norm_r"], 1)

        for t in range(KT):
            act.wait_ge(S["x_kept"], 1 + t // 2 + 1)
            square(hT[:, :, :], sqa, TM, t)
        act.wait_ge(S["vec_turned"], 1)
        act.activation(vec[:, 0:NVEC], pb[5][:, 0:NVEC], ACT.Copy).then_inc(S["vec_kept"], 1)
        act.wait_ge(S["filled"], 1)
        root(0, rms, TM)
        act.wait_ge(S["lam_sum"], 1)
        act.activation(lamc[:, 0:2], sml[:, 0:2], ACT.Exp).then_inc(S["lam_exp"], 1)
        act.wait_ge(S["vec_kept"], 1)
        act.activation(sml[:, 8:16], vec[:, VROW["c"]:VROW["c"] + KT], ACT.Exp, scale=-1.0).then_inc(S["lam_exp"], 1)

        def keep1(g):
            p, kind, n, c = GR1[g]
            act.wait_ge(S["gemm1"], g + 1)
            src = pb[g % 3]
            if kind == "sq":
                dst, src, scale = sqT[:, c, :], src[:, 0:T], 1.0
            elif kind == "sk":
                dst, src, scale = skT[:, c, :], src[:, 0:TM], 1.0
            elif kind == "dq":
                dst, src, scale = dqT[:, c, :], src[:, 0:T], 0.125
            elif kind == "dk":
                dst, src, scale = dkT[:, c, :], src[:, 0:TM], 1.0
            elif kind in ("sv", "dv"):
                buf, part = (sv, dv)[kind == "dv"], c // 4
                if n == 0:
                    dst, scale = vmeta, 1.0
                else:
                    rows = M if n == 3 else P
                    dst, src, scale = buf[0:rows, n - 1, 512 * part:512 * part + 512], src[0:rows, :], 1.0
            elif kind == "gate":
                b = VROW["b_gate"] + c
                act.activation(gate[:, c, :], src[:, 0:T], ACT.Identity, bias=vec[:, b:b + 1])\
                   .then_inc(S["act_evac1"], 1)
                return
            act.activation(dst, src, ACT.Copy, scale=scale).then_inc(S["act_evac1"], 1)

        def sb_step(s, h):
            if s == "sbA":
                act.wait_ge(S["sb_scores"], h + 1)
                if h:
                    act.wait_ge(S["sb_la"], h)
                act.activation(zs[:, 0:384], pb[3][:, 0:384], ACT.Copy, scale=SB_SCALE)
                act.activation(zs[0:M, 384:640], pb[4][0:M, 0:T], ACT.Copy, scale=SB_SCALE).then_inc(S["sb_zs"], 1)
                act.wait_ge(S["sb_min"], h + 1)
                st.do(act.activation(ex[:, 0:384], ex[:, 0:384], ACT.Exp))
                st.do(act.activation(ex[0:M, 384:640], ex[0:M, 384:640], ACT.Exp))
                st.wait()
                act.activation(sp[:, 0:384], ex[:, 0:384], ACT.Ln, bias=onec)
                act.activation(sp[0:M, 384:640], ex[0:M, 384:640], ACT.Ln, bias=onec[0:M]).then_inc(S["sb_ln"], 1)
            if s == "sbB":
                act.wait_ge(S["sb_la"], h + 1)
                act.activation(la[:, 0:384], la[:, 0:384], ACT.Exp)
                act.activation(la[0:M, 384:640], la[0:M, 384:640], ACT.Exp).then_inc(S["sb_a"], 1)
            if s == "sbC":
                act.wait_ge(S["sb_o"], h + 1)
                act.activation(sqT[:, h, :], pb[7][:, 0:T], ACT.Copy).then_inc(S["sb_out"], 1)

        def df_step(s, h):
            if s == "dfA":
                act.wait_ge(S["df_max"], h + 1)
                for qt in range(2):
                    for c in range(2):
                        v = sc[:, c, 144 * qt:144 + 272 * qt]
                        last = act.activation(v, v, ACT.Exp, bias=sml[:, 16 + 2 * qt + c:17 + 2 * qt + c],
                                              accum_out=sml[:, 20 + 2 * qt + c:21 + 2 * qt + c])
                last.then_inc(S["df_exp"], 1)
            if s == "dfB":
                act.wait_ge(S["df_tr"], h + 1)
                act.activation(wT[:, 0:384], pb[5][:, 0:384], ACT.Copy)
                act.activation(wT[0:M, 384:640], pb[6][0:M, 0:T], ACT.Copy).then_inc(S["df_wt"], 1)
            if s == "dfC":
                act.wait_ge(S["df_o"], h + 1)
                act.activation(osq, pb[7][:, 0:T], ACT.Square).then_inc(S["df_sq"], 1)
            if s == "dfD":
                act.wait_ge(S["df_ms"], h + 1)
                st.do(act.activation(ors, pb[6][:, T:512], ACT.Ln, bias=epsc, scale=1.0 / P))
                st.wait()
                act.activation(ors, ors, ACT.Exp, scale=-0.5).then_inc(S["df_rs"], 1)

        def square_out1(t):
            act.wait_ge(S["dve_evac1"], evac(GR1, where(GR1, "out", t))[1])
            square(hx, sqa1, T, t)

        def high1(n):
            if n < len(GR1) - G0:
                if n % 2 == 0:
                    act.wait_ge(in2[n // 2 % 4], 16 * (n // 8 + 1))
                if n >= 4:
                    act.wait_ge(S["gemm1"], G0 + n - 3)
                act.activation(w2h[:, n % 4, :].rearrange("p (k n) -> p k n", k=KT), unit1(raw2, n), ACT.Copy).then_inc(S["w1_hi"], 1)

        def part1(s, h):
            if s == "sbS":
                act.wait_ge(S["sb_out"], HEADS)
                dst, src = yh[:, 4 * h:4 * h + 4, :], sqT[:, 4 * h:4 * h + 4, :]
            elif s == "dfS":
                act.wait_ge(S["df_out"], HEADS)
                dst, src = dfh[:, 4 * h:4 * h + 4, :], dqT[:, 4 * h:4 * h + 4, :]
            else:
                act.wait_ge(S["dve_evac1"], evac(GR1, where(GR1, "ydf", h))[1])
                dst, src = yh[:, h, :], mT[:, h, :]
            act.activation(dst, src, ACT.Copy).then_inc(S["y_hi"], 1)

        for s, h in ORDER1:
            if s == "G":
                if h >= G0:
                    high1(h - G0 + 3)
                if not evac(GR1, h)[0]:
                    keep1(h)
            elif s == "split":
                high1(h)
            elif s in ("sbS", "dfS", "mS", "mL"):
                part1(s, h if s != "mL" else KT - 1)
            elif s[0:2] == "sb":
                sb_step(s, h)
            elif s[0:2] == "df":
                df_step(s, h)
            elif s == "square":
                square_out1(h)
            elif s == "gates":
                act.wait_ge(S["act_evac1"], evac(GR1, where(GR1, "gate", 4 * h + 3))[1])
                v = gate[:, 4 * h:4 * h + 4, :]
                act.activation(v, v, ACT.Sigmoid).then_inc(S["gate_done"], 1)

        def high(n, i, raw):
            act.wait_ge(S["up"], n + 1)
            act.activation(wh[:, i, :].rearrange("p (k n) -> p k n", k=raw.shape[1]), raw, ACT.Copy).then_inc(S["w_hi"], 1)

        act.wait_ge(inu[0], 32)
        for i in range(2):
            high(i, i, up_group(0, i))
        for t in range(SQUARED, KT):
            square_out1(t)
        root(1, rms, T)
        for t in range(KT):
            act.wait_ge(S["norm_x"], 2 * KT - KT + t + 1)
            act.activation(xfh[:, t, :], xf[:, t, :], ACT.Copy).then_inc(S["x_hi"], 1)

        def sig(f, q):
            act.wait_ge(S["up"], f * 2 + 5)
            act.wait_ge(S["up_free"], f + 1)
            act.activation(fe[:, q, :], pb[2 * q][:, 0:T], ACT.Sigmoid).then_inc(S["up_sig"], 1)

        def scale(b, n):
            act.wait_ge(ina[b], n)
            for k in range(ADA_SCALED):
                v = slot(2 + b)[:, k, :]
                last = act.activation(v, v, ACT.Copy, scale=csil[:, k:k + 1])
            last.then_inc(S["ada_scaled"], 1)

        def up(j, b, n, ada_n, before):
            act.wait_ge(inu[b], n)
            for i in range(4):
                if before or i >= 2:
                    high(j * 4 + i, i, up_group(b, i))
                if i == 1:
                    scale(b, ada_n)
                if i == 0 and before:
                    sig(j * 2 - 1, 1)
                if i == 2:
                    sig(j * 2, 0)

        act.wait_ge(S["csil"], 1)
        up(0, 0, 32, 16, False)
        with act.Fori(0, UPS // 2) as i:
            up(i * 2 + 1, 1, i * 32 + 32, i * 16 + 16, True)
            up(i * 2 + 2, 0, i * 32 + 64, i * 16 + 32, True)
        for kk in range(FT):
            j = kk // 4
            if kk % 4 == 0:
                act.wait_ge(ind[(j + 1) % 2], 16 * (j // 2 + 1))
            high(4 * UPS + kk, kk % 4, down_group(kk))
            if kk == 0:
                sig(FT - 1, 1)
            if kk == 1:
                scale(1, 16 * (ADAS // 2))

        def high2(n):
            if n >= len(UNITS2):
                return
            if n % 2 == 0:
                act.wait_ge(in2[n // 2 % 4], 16 * (n // 8 + 1 + 3))
            if n < 4:
                act.wait_ge(S["ada_sum"], ADAS)
            else:
                unit_used(act, n - 4)
            raw = unit2(raw2, n)
            act.activation(w2h[:, n % 4, :].rearrange("p (k n) -> p k n", k=raw.shape[1]), raw, ACT.Copy).then_inc(S["w_hi"], 1)

        for n in range(3):
            high2(n)
        for t in range(KT):
            act.wait_ge(S["down_out"], t // 2 + 1)
            square(hx, sqa, T, t)
        root(2, rms, T)
        for t in range(KT):
            act.wait_ge(S["norm_x"], 2 * KT + t + 1)
            square(hx, sqa, T, t)
        root(3, rms, T)
        for t in range(KT):
            act.wait_ge(S["norm_x"], 3 * KT + t + 1)
            act.activation(x2h[:, t, :], xn2[:, t, :], ACT.Identity, bias=modT[:, t:t + 1]).then_inc(S["x_hi"], 1)

        def keep2(g):
            p, kind, n, c = GR2[g]
            act.wait_ge(S["gemm2"], g + 1)
            src, scale = pb[g % 3], 1.0
            if kind == "rq":
                dst, src = raw[:, 0, T * n:T * n + T], src[:, 0:T]
            elif kind == "rk":
                dst, src, scale = raw[:, 1, T * n:T * n + T], src[:, 0:T], P ** -0.5
            elif kind == "rv":
                dst = rv[:, n, 512 * (c // 2):512 * (c // 2) + 512]
            elif kind == "aq":
                dst, src, scale = aqT[:, c, :], src[:, 0:T], P ** -0.5
            elif kind == "ak":
                dst, src = akT[:, c, :], src[:, 0:T]
            elif kind == "av":
                dst = av[:, n, 512 * (c // 2):512 * (c // 2) + 512]
            elif kind == "gab":
                dst, src = gab[:, c, :], src[:, 0:T]
            act.activation(dst, src, ACT.Copy, scale=scale).then_inc(S["act_evac2"], 1)

        def rt_step(s, h):
            if s == "rtB":
                act.wait_ge(S["rt_y"], h + 1)
                if h:
                    act.wait_ge(S["rt_out"], h)
                act.activation(ys, pb[4].rearrange("p (a n) -> p a n", a=2), ACT.Copy).then_inc(S["rt_ys"], 1)
            if s == "rtC":
                act.wait_ge(S["rt_yc"], h + 1)
                act.activation(yq, ys, ACT.Square).then_inc(S["rt_sq"], 1)
            if s == "rtD":
                act.wait_ge(S["rt_v"], h + 1)
                st.do(act.activation(yr, pb[6][:, 0:T], ACT.Ln, bias=gnepsc, scale=1.0 / T))
                st.wait()
                act.activation(yr, yr, ACT.Exp, scale=-0.5).then_inc(S["rt_r"], 1)

        def dl_step(s, h):
            if s == "dlE":
                act.wait_ge(S["dl_max"], h + 1)
                for qt, v in enumerate((ds[:, 0:384], ds[:, 384:1152])):
                    last = act.activation(v, v, ACT.Exp, bias=sml[:, 16 + qt:17 + qt], accum_out=sml[:, 18 + qt:19 + qt])
                last.then_inc(S["dl_e"], 1)
            if s == "dlB":
                act.wait_ge(S["dl_t"], h + 1)
                for g in range(GROUPS):
                    last = act.activation(dwT[:, 384 * g:384 * g + 384], pb[3 + g][:, 0:384], ACT.Copy)
                last.then_inc(S["dl_wt"], 1)
            if s == "dlC":
                act.wait_ge(S["dl_o"], h + 1)
                act.activation(attT[:, h, :], pb[7][:, 0:T], ACT.Copy).then_inc(S["dl_out"], 1)

        def silu2(g, c):
            act.wait_ge(S["gemm2"], g + 1)
            if c >= 2:
                act.wait_ge(S["dve_evac2"], c - 1)
            act.activation(rsg[:, c % 2, :], pb[g % 3][:, 0:T], ACT.Sigmoid).then_inc(S["rg_exp"], 1)

        def square_out2(t):
            act.wait_ge(S["dve_evac2"], evac(GR2, where(GR2, "o", t))[1])
            square(hx, nsq, T, t)

        for s, h in ORDER2:
            if s == "square":
                square_out2(h)
            if s == "G":
                high2(h + 3)
                for g in UNITS2[h]:
                    if GR2[g][1] == "rg":
                        silu2(g, GR2[g][3])
                    elif not evac(GR2, g)[0]:
                        keep2(g)
            elif s[0:2] == "rt":
                rt_step(s, h)
            elif s[0:2] == "dl":
                dl_step(s, h)
            elif s == "gates":
                act.wait_ge(S["act_evac2"], evac(GR2, where(GR2, "gab", 4 * h + 3))[1])
                v = gab[:, 4 * h:4 * h + 4, :]
                act.activation(v, v, ACT.Sigmoid).then_inc(S["gab_done"], 1)
            elif s == "rgS":
                act.wait_ge(S["rt_out"], RH)
                act.wait_ge(S["dl_s"], SLOTS)
                act.activation(rgh[:, 4 * h:4 * h + 4, :], rg[:, 4 * h:4 * h + 4, :], ACT.Copy).then_inc(S["x_hi"], 1)
            elif s == "atS":
                act.wait_ge(S["dl_out"], SLOTS)
                act.activation(atth[:, :, :], attT, ACT.Copy).then_inc(S["x_hi"], 1)
            elif s in ("m2S", "m2L"):
                h = h if s == "m2S" else KT - 1
                act.wait_ge(S["dve_evac2"], evac(GR2, where(GR2, "yret", h))[1])
                act.activation(m2h[:, h, :], m2T[:, h, :], ACT.Copy).then_inc(S["x_hi"], 1)
        for t in range(SQUARED, KT):
            square_out2(t)
        root(4, nrms, T)
        for t in range(KT):
            act.wait_ge(S["norm_x"], 4 * KT + t + 1)
            act.activation(hn[:, t, :], hn[:, t, :], ACT.Identity, bias=modT[:, 24 + t:25 + t]).then_inc(S["norm_s"], 1)
        for b in range(4):
            act.wait_ge(S["ht_mm"], b + 1)
            act.activation(htok[:, b // 2, 512 * (b % 2):512 * (b % 2) + 512], pb[4 + b], ACT.Copy).then_inc(S["ht_kept"], 1)
        act.wait_ge(S["route"], 1)
        act.activation(gts, gts, ACT.Exp).then_inc(S["log_exp"], 1)
        act.wait_ge(S["gt_mm"], 1)
        act.activation(gatT, pb[2][0:E, 0:T], ACT.Copy).then_inc(S["gt_kept"], 1)

        def expert(e, cur, prev):
            if cur:
                act.wait_ge(S["gath"], e + 1)
                since(act, "u_mm", e * 5)
                act.activation(XgT, pb[3].rearrange("p (a n) -> p a n", a=KT), ACT.Copy).then_inc(S["xg"], 1)
            if prev:
                act.wait_ge(S["at_mm"], e)
                since(act, "y_mm", e * 2 - 2)
                act.activation(aT, pb[4].rearrange("p (a n) -> p a n", a=4), ACT.Copy).then_inc(S["at"], 1)
                act.wait_ge(S["selt_mm"], e)
                since(act, "sc_mm", e * 2 - 2)
                act.activation(selT, pb[5][:, 0:T], ACT.Copy).then_inc(S["selt"], 1)
                act.wait_ge(S["y_mm"], e * 2)
                act.activation(yv, pb[2], ACT.Copy).then_inc(S["yv_done"], 1)
            if cur:
                act.wait_ge(S["u_read"], e + 1)
                since(act, "a_done", e)
                act.activation(sg, gl, ACT.Sigmoid, scale=1.702).then_inc(S["u_sig"], 1)

        expert(0, True, False)
        expert(1, True, True)
        with act.Fori(2, E) as e:
            expert(e, True, True)
        expert(E, False, True)

        def again(e, n, r):
            act.wait_ge(S["over_pe"], n * 7 + 2)
            act.activation(XgT, pb[3].rearrange("p (a n) -> p a n", a=KT), ACT.Copy).then_inc(S["over_act"], 1)
            act.wait_ge(S["over_pe"], n * 7 + 3)
            act.activation(selT, pb[5][:, 0:T], ACT.Copy).then_inc(S["over_act"], 1)
            act.wait_ge(S["over_dve"], n * 7 + 3)
            act.activation(sg, gl, ACT.Sigmoid, scale=1.702).then_inc(S["over_act"], 1)
            act.wait_ge(S["over_pe"], n * 7 + 5)
            act.activation(aT, pb[4].rearrange("p (a n) -> p a n", a=4), ACT.Copy).then_inc(S["over_act"], 1)
            act.wait_ge(S["over_pe"], n * 7 + 6)
            act.activation(yv, pb[2], ACT.Copy).then_inc(S["over_act"], 1)

        further(act, again)
        for t in range(KT):
            act.wait_ge(S["final_sum"], t + 1)
            square(hx, nsq, T, t)
        root(5, nrms, T)
        for b in range(4):
            act.wait_ge(S["fin_mm"], b + 1)
            act.activation(otok[:, b // 2, 512 * (b % 2):512 * (b % 2) + 512], pb[4 + b], ACT.Copy).then_inc(S["fin_kept"], 1)

    @block.vector
    def _(dve):
        st = Count(dve, S["dve_step"])
        stt, tt, ts = nc.vector.scalar_tensor_tensor, nc.vector.tensor_tensor, nc.vector.tensor_scalar

        def norm(k, dst, src, r, g):
            dve.wait_ge(S["norm_r"], k + 1)
            for t in range(KT):
                stt(dst[:, t, :], src[:, t, :], g[:, t:t + 1], r, ALU.mult, ALU.mult).then_inc(S["norm_x"], 1)

        def vrows(name, n=KT):
            return vec[:, VROW[name]:VROW[name] + n]

        for b in range(5):
            dve.wait_ge(S["x_turned"], b + 1)
            if b == 0:
                last = nc.vector.tensor_copy(hT[:, :, 0:M], pb[4][:, 0:P].rearrange("p (a n) -> p a n", a=KT))
            else:
                last = nc.vector.tensor_copy(hx[:, 2 * b - 2:2 * b, :], pb[b - 1].rearrange("p (a n) -> p a n", a=2))
            last.then_inc(S["x_kept"], 1)
        dve.wait_ge(S["x_kept"], 5)
        dve.wait_ge(S["vec_kept"], 1)
        norm(0, xn, hT, rms[:, 0:TM], vrows("norm_mix_g"))
        dve.wait_ge(S["lam_in"], 64)
        st.do(tt(lamv[:, 0:2, :], lamv[:, 0:2, :], lamv[:, 2:4, :], ALU.mult))
        st.wait()
        nc.vector.tensor_reduce(sml[:, 0:2], lamv[:, 0:2, :], AX.X, ALU.add).then_inc(S["lam_sum"], 1)
        st.do(ts(gsub, vrows("subln_g", 1), 1.0 - LAM_INIT, None, ALU.mult))
        dve.wait_ge(S["lam_exp"], 1)
        st.do(tt(lamc[:, 2:3], lamc[:, 1:2], lamc[:, 0:1], ALU.subtract))
        st.wait()
        st.do(ts(lamc[:, 2:3], lamc[:, 2:3], -LAM_INIT, None, ALU.add))
        dve.wait_ge(S["lam_exp"], 2)
        st.do(ts(sml[:, 8:16], sml[:, 8:16], 1.0, None, ALU.add))
        st.wait()
        st.do(nc.vector.reciprocal(sml[:, 8:16], sml[:, 8:16]))
        st.wait()
        tt(csil, sml[:, 8:16], vrows("c"), ALU.mult).then_inc(S["csil"], 1)


        def keep1(g):
            p, kind, n, c = GR1[g]
            src = pb[g % 3][:, 0:T]
            if kind not in DVE_KINDS:
                return
            dve.wait_ge(S["gemm1"], g + 1)
            if kind == "ysb":
                dve.wait_ge(S["gate_done"], c // 4 + 1)
                tt(mT[:, c, :], src, gate[:, c, :], ALU.mult).then_inc(S["dve_evac1"], 1)
            if kind == "ydf":
                dve.wait_ge(S["gate_done"], 2 + c // 4 + 1)
                dve.wait_ge(S["dve_evac1"], KT + c)
                st.do(tt(dtmp, src, gate[:, KT + c, :], ALU.mult))
                st.wait()
                tt(mT[:, c, :], mT[:, c, :], dtmp, ALU.add).then_inc(S["dve_evac1"], 1)
            if kind == "out":
                tt(hx[:, c, :], src, hx[:, c, :], ALU.add).then_inc(S["dve_evac1"], 1)

        def sb_step(s, h):
            if s == "sbA":
                dve.wait_ge(S["sb_zs"], h + 1)
                if h:
                    dve.wait_ge(S["sb_ln"], h)
                ts(ex[:, 0:384], zs[:, 0:384], 40.0, None, ALU.min)
                ts(ex[0:M, 384:640], zs[0:M, 384:640], 40.0, None, ALU.min).then_inc(S["sb_min"], 1)
                dve.wait_ge(S["sb_ln"], h + 1)
                st.do(tt(sp[:, 0:384], sp[:, 0:384], zs[:, 0:384], ALU.max))
                st.do(tt(sp[0:M, 384:640], sp[0:M, 384:640], zs[0:M, 384:640], ALU.max))
                st.wait()
                tt(two(sp), two(sp), bc(tri, 2), ALU.mult).then_inc(S["sb_sp"], 1)
            if s == "sbB":
                dve.wait_ge(S["sb_rest"], h + 1)
                if h:
                    dve.wait_ge(S["sb_o"], h)
                st.do(tt(la[:, 0:384], pb[5][:, 0:384], zs[:, 0:384], ALU.add))
                st.do(tt(la[0:M, 384:640], pb[6][0:M, 0:T], zs[0:M, 384:640], ALU.add))
                st.wait()
                tt(two(la), two(la), bc(negm, 2), ALU.add).then_inc(S["sb_la"], 1)

        def df_step(s, h):
            if s == "dfA":
                dve.wait_ge(S["df_scores"], h + 1)
                for c in range(2):
                    last = stt(sc[:, c, :], distt, 2.0 ** -(h + 1), pb[3 + c][:, 0:416], ALU.mult, ALU.add)
                last.then_inc(S["df_s"], 1)
                dve.wait_ge(S["df_s"], h + 1)
                for qt in range(2):
                    st.do(nc.vector.tensor_reduce(sml[:, 16 + 2 * qt:18 + 2 * qt], sc[:, :, 144 * qt:144 + 272 * qt],
                                                  AX.X, ALU.max))
                st.wait()
                ts(sml[:, 16:20], sml[:, 16:20], -1.0, None, ALU.mult).then_inc(S["df_max"], 1)
                dve.wait_ge(S["df_exp"], h + 1)
                st.do(nc.vector.reciprocal(sml[:, 24:28], sml[:, 20:24]))
                st.wait()
                for qt in range(2):
                    st.do(ts(sml[:, 25 + 2 * qt:26 + 2 * qt], sml[:, 25 + 2 * qt:26 + 2 * qt], lamc[:, 2:3], None, ALU.mult))
                if h:
                    dve.wait_ge(S["df_tr"], h)
                for qt in range(2):
                    v = slice(144 * qt, 144 + 272 * qt)
                    st.do(ts(wv[:, v], sc[:, 0, v], sml[:, 24 + 2 * qt:25 + 2 * qt], None, ALU.mult))
                st.wait()
                for qt in range(2):
                    v = slice(144 * qt, 144 + 272 * qt)
                    last = stt(wv[:, v], sc[:, 1, v], sml[:, 25 + 2 * qt:26 + 2 * qt], wv[:, v], ALU.mult, ALU.add)
                last.then_inc(S["df_w"], 1)
            if s == "dfD":
                dve.wait_ge(S["df_rs"], h + 1)
                stt(dqT[:, h, :], pb[7][:, 0:T], gsub, ors, ALU.mult, ALU.mult).then_inc(S["df_out"], 1)

        def low1(n):
            if n < len(GR1) - G0:
                dve.wait_ge(S["w1_hi"], n + 1)
                tt(unit1(w2l, n), unit1(raw2, n), w2h[:, n % 4, :].bitcast(F32).rearrange("p (k n) -> p k n", k=KT),
                   ALU.subtract).then_inc(S["w1_lo"], 1)

        def part1(s, h):
            v = slice(4 * h, 4 * h + 4)
            if s == "sbS":
                n, dst, src, high = h, yl[:, v, :], sqT[:, v, :], yh[:, v, :]
            elif s == "dfS":
                n, dst, src, high = 2 + h, dfl[:, v, :], dqT[:, v, :], dfh[:, v, :]
            else:
                n, dst, src, high = 4 + h, yl[:, h, :], mT[:, h, :], yh[:, h, :]
            dve.wait_ge(S["y_hi"], n + 1)
            tt(dst, src, high.bitcast(F32), ALU.subtract).then_inc(S["y_lo"], 1)

        dve.wait_ge(S["cst_in"], 16)
        for s, h in ORDER1:
            if s == "G":
                if h >= G0:
                    low1(h - G0 + 3)
                keep1(h)
            elif s == "split":
                low1(h)
            elif s in ("sbS", "dfS", "mS", "mL"):
                part1(s, h if s != "mL" else KT - 1)
            elif s[0:2] == "sb":
                sb_step(s, h)
            elif s[0:2] == "df":
                df_step(s, h)

        def low(n, i, raw):
            dve.wait_ge(S["w_hi"], n + 1)
            k = raw.shape[1]
            tt(wl[:, i, :].rearrange("p (k n) -> p k n", k=k), raw,
               wh[:, i, :].bitcast(F32).rearrange("p (k n) -> p k n", k=k), ALU.subtract).then_inc(S["w_lo"], 1)

        for i in range(2):
            low(i, i, up_group(0, i))
        norm(1, xf, hx, rms[:, 0:T], vrows("norm_ffn_g"))

        for t in range(KT):
            dve.wait_ge(S["x_hi"], t + 1)
            tt(xfl[:, t, :], xf[:, t, :], xfh[:, t, :].bitcast(F32), ALU.subtract).then_inc(S["x_lo"], 1)

        def modulation(j, b):
            dve.wait_ge(S["ada_step"], j * (ADA_SCALED - 1) + (ADA_SCALED - 1))
            for k in range(ADA_SCALED, KT):
                if k > ADA_SCALED:
                    dve.wait_ge(S["ada_more"], j * (KT - 1 - ADA_SCALED) + (k - ADA_SCALED))
                stt(adac[:, b, :], slot(2 + b)[:, k, :], csil[:, k:k + 1], adac[:, b, :], ALU.mult, ALU.add)\
                    .then_inc(S["ada_more" if k < KT - 1 else "ada_sum"], 1)

        def mlp(f, q):
            dve.wait_ge(S["up_sig"], f + 1)
            tt(fr[:, q, :], pb[2 * q][:, 0:T], fe[:, q, :], ALU.mult).then_inc(S["up_step"], 1)
            dve.wait_ge(S["up_step"], f * 3 + 1)
            dve.wait_ge(S["up"], f * 2 + 6)
            tt(ft[:, q, :], pb[2 * q + 1][:, 0:T], fr[:, q, :], ALU.mult).then_inc(S["up_free"], 1)
            dve.wait_ge(S["up_free"], f + 3)
            one_tile = lambda x: x[:, bass.ds(f, 1), :].rearrange("p a n -> p (a n)")
            nc.vector.tensor_copy(one_tile(fh), ft[:, q, :]).then_inc(S["up_step"], 1)
            dve.wait_ge(S["up_step"], f * 3 + 2)
            tt(one_tile(fl), ft[:, q, :], one_tile(fh).bitcast(F32), ALU.subtract).then_inc(S["up_step"], 1)

        def up(j, b, before):
            for i in range(4):
                if before or i >= 2:
                    low(j * 4 + i, i, up_group(b, i))
                if i == 1 and before:
                    modulation(j - 1, 1 - b)
                    mlp(j * 2 - 1, 1)
            mlp(j * 2, 0)

        dve.sem_inc(S["up_free"], 2)
        up(0, 0, False)
        with dve.Fori(0, UPS // 2) as i:
            up(i * 2 + 1, 1, True)
            up(i * 2 + 2, 0, True)
        dve.wait_ge(S["ada_mm"], ADAS - 2 + 2)
        tt(modT[:, 0:40], pb[7][:, 0:40], vrows("b_ada", 40), ALU.add).then_inc(S["mod_done"], 1)
        for kk in range(FT):
            low(4 * UPS + kk, kk % 4, down_group(kk))
            if kk == 1:
                modulation(ADAS - 2, 0)
                mlp(FT - 1, 1)
            if kk == 5:
                modulation(ADAS - 1, 1)
            if kk == 9:
                dve.wait_ge(S["mod_done"], 1)
                dve.wait_ge(S["ada_mm"], ADAS + 2)
                st.do(tt(modT[:, 40:48], pb[0][:, 40:48], vrows("b_ada", 48)[:, 40:48], ALU.add))
                st.do(stt(gsa, modT[:, 8:16], 1.0, vrows("g_mix"), ALU.add, ALU.mult))
                st.do(stt(gsf, modT[:, 32:40], 1.0, vrows("g_ffn"), ALU.add, ALU.mult))

        def low2(n):
            if n < len(UNITS2):
                raw = unit2(raw2, n)
                dve.wait_ge(S["w_hi"], MLP_GROUPS + n + 1)
                tt(unit2(w2l, n), raw, w2h[:, n % 4, :].bitcast(F32).rearrange("p (k n) -> p k n", k=raw.shape[1]),
                   ALU.subtract).then_inc(S["w_lo"], 1)

        for n in range(3):
            low2(n)
        for b in range(4):
            dve.wait_ge(S["down"], 1 + b)
            v = hx[:, 2 * b:2 * b + 2, :]
            tt(v, pb[4 + b].rearrange("p (a n) -> p a n", a=2), v, ALU.add).then_inc(S["down_out"], 1)
        st.wait()
        norm(2, hx, hx, rms[:, 0:T], vrows("norm_final_g"))
        norm(3, xn2, hx, rms[:, 0:T], gsa)
        for t in range(KT):
            dve.wait_ge(S["x_hi"], KT + t + 1)
            stt(x2l[:, t, :], xn2[:, t, :], modT[:, t:t + 1], x2h[:, t, :].bitcast(F32), ALU.add, ALU.subtract).then_inc(S["x_lo"], 1)

        def toeplitz():
            dve.wait_ge(S["hot_in"], 48)
            for g in range(GROUPS):
                dve.wait_ge(S["toep_mm"], g + 1)
                tt(stg[:, g, :], pb[4 + g][0:SLOTS, 0:TOEP], bad[:, g, :], ALU.add).then_inc(S["toep_sum"], 1)

        def keep2(g):
            p, kind, n, c = GR2[g]
            src = pb[g % 3][:, 0:T]
            if kind not in DVE_KINDS:
                return
            dve.wait_ge(S["gemm2"], g + 1)
            if kind == "rg":
                dve.wait_ge(S["rg_exp"], c + 1)
                tt(rg[:, c, :], src, rsg[:, c % 2, :], ALU.mult).then_inc(S["dve_evac2"], 1)
            if kind == "yatt":
                dve.wait_ge(S["gab_done"], 2 + c // 4 + 1)
                tt(m2T[:, c, :], src, gab[:, KT + c, :], ALU.mult).then_inc(S["dve_evac2"], 1)
            if kind == "yret":
                dve.wait_ge(S["gab_done"], c // 4 + 1)
                dve.wait_ge(S["dve_evac2"], evac(GR2, g)[1] - 1)
                st.do(tt(dtmp2, src, gab[:, c, :], ALU.mult))
                st.wait()
                tt(m2T[:, c, :], m2T[:, c, :], dtmp2, ALU.add).then_inc(S["dve_evac2"], 1)
            if kind == "o":
                stt(hx[:, c, :], src, modT[:, 16 + c:17 + c], hx[:, c, :], ALU.mult, ALU.add).then_inc(S["dve_evac2"], 1)

        def rotary(i):
            g = first_of(GR2, ("rq", "rk")[i]) + 3
            dve.wait_ge(S["act_evac2"], evac(GR2, g)[1])
            if i == 0:
                dve.wait_ge(S["tab_in"], 16)
            dst = (rqT, rkT)[i]
            r = raw[:, i, :].rearrange("p (a n) -> p a n", a=RH)
            st.do(tt(dst, r, bc(tab[:, RH, :], RH), ALU.mult))
            st.wait()
            dve.wait_ge(S["rot_mm"], i + 1)
            for j in range(2):
                st.do(tt(r[:, 2 * j:2 * j + 2, :], pb[3 + j].rearrange("p (a n) -> p a n", a=2),
                         bc(tab[:, RH + 1, :], 2), ALU.mult))
            st.wait()
            tt(dst, dst, r, ALU.add).then_inc(S["rot_out"], 1)

        def rt_step(s, h):
            if s == "rtA":
                dve.wait_ge(S["rt_s"], h + 1)
                if h:
                    dve.wait_ge(S["rt_y"], h)
                else:
                    dve.wait_ge(S["toep_out"], 16)
                tt(pT[:, 0:T], pb[3][:, 0:T], tab[:, h, :], ALU.mult)
                tt(pT[:, T:384], pb[3][:, T:384], tab[:, h, 0:P], ALU.mult).then_inc(S["rt_p"], 1)
            if s == "rtC":
                dve.wait_ge(S["rt_m"], h + 1)
                for e in range(2):
                    last = stt(ys[:, e, :], pb[5][:, 0:T], -1.0 / T, ys[:, e, :], ALU.mult, ALU.add)
                last.then_inc(S["rt_yc"], 1)
            if s == "rtD":
                dve.wait_ge(S["rt_r"], h + 1)
                st.do(tt(ys, ys, bc(yr, 2), ALU.mult))
                st.wait()
                v = rg[:, 2 * h:2 * h + 2, :]
                tt(v, v, ys, ALU.mult).then_inc(S["rt_out"], 1)

        def dl_step(s, h):
            bt = BT.rearrange("p (g s) n -> p s g n", g=GROUPS)[:, h, :, :]
            if s == "dlA":
                dve.wait_ge(S["dl_s"], h + 1)
                tt(ds[:, 0:384].rearrange("p (g n) -> p g n", g=3), pb[3][:, 0:384].rearrange("p (g n) -> p g n", g=3),
                   bt[:, :, P:T], ALU.add)
                tt(ds[:, 384:896].rearrange("p (g n) -> p g n", g=2), pb[4].rearrange("p (g n) -> p g n", g=2),
                   bt[:, 0:2, :], ALU.add)
                tt(ds[:, 896:1152], pb[5][:, 0:T], bt[:, 2, :], ALU.add).then_inc(S["dl_b"], 1)
                dve.wait_ge(S["dl_b"], h + 1)
                for qt, v in enumerate((ds[:, 0:384], ds[:, 384:1152])):
                    st.do(nc.vector.tensor_reduce(sml[:, 16 + qt:17 + qt], v, AX.X, ALU.max))
                st.wait()
                ts(sml[:, 16:18], sml[:, 16:18], -1.0, None, ALU.mult).then_inc(S["dl_max"], 1)
            if s == "dlN":
                dve.wait_ge(S["dl_e"], h + 1)
                st.do(nc.vector.reciprocal(sml[:, 20:22], sml[:, 18:20]))
                st.wait()
                for qt, v in enumerate((ds[:, 0:384], ds[:, 384:1152])):
                    last = ts(v, v, sml[:, 20 + qt:21 + qt], None, ALU.mult)
                last.then_inc(S["dl_p"], 1)

        for s, h in ORDER2:
            if s == "G":
                low2(h + 3)
                for g in UNITS2[h]:
                    keep2(g)
            elif s == "toep":
                toeplitz()
            elif s == "rot":
                rotary(h)
            elif s == "rgS":
                v = slice(4 * h, 4 * h + 4)
                dve.wait_ge(S["x_hi"], 2 * KT + 1 + h + 1)
                tt(rgl[:, v, :], rg[:, v, :], rgh[:, v, :].bitcast(F32), ALU.subtract).then_inc(S["x_lo"], 1)
            elif s == "atS":
                dve.wait_ge(S["x_hi"], 2 * KT + 1)
                tt(attl[:, :, :], attT, atth[:, :, :].bitcast(F32), ALU.subtract).then_inc(S["x_lo"], 1)
            elif s in ("m2S", "m2L"):
                h = h if s == "m2S" else KT - 1
                dve.wait_ge(S["x_hi"], 2 * KT + 3 + h + 1)
                tt(m2l[:, h, :], m2T[:, h, :], m2h[:, h, :].bitcast(F32), ALU.subtract).then_inc(S["x_lo"], 1)
            elif s[0:2] == "rt":
                rt_step(s, h)
            elif s[0:2] == "dl":
                if s == "dlA" and h == 0:
                    dve.wait_ge(S["toep_in"], 16)
                dl_step(s, h)

        norm(4, hn, hx, nrms, gsf)
        dve.wait_ge(S["moe_in"], 48)
        dve.wait_ge(S["log_mm"], 1)
        st.do(tt(lg, pb[1][:, 0:2 * E].rearrange("p (a e) -> p a e", a=2), bc(brow, 2), ALU.add))
        st.do(nc.vector.memset(msk, 0.0))
        st.do(nc.vector.memset(gat, 0.0))
        st.do(nc.vector.memset(rank, -1.0))
        st.wait()
        for t in range(2):
            st.do(nc.vector.max(top8[:, t, :], lg[:, t, :]))
        st.wait()
        for t in range(2):
            st.do(nc.vector.max_index(topi[:, t, :], top8[:, t, :], lg[:, t, :]))
            st.do(ts(gts[:, t, :], top8[:, t, :], top8[:, t, 0:1], None, ALU.subtract))
        st.wait()
        nc.vector.tensor_copy(tif, topi[:, :, :]).then_inc(S["route"], 1)
        dve.wait_ge(S["log_exp"], 1)
        st.do(nc.vector.tensor_reduce(sml[:, 32:34], gts[:, :, 0:4], AX.X, ALU.add))
        st.wait()
        st.do(nc.vector.reciprocal(sml[:, 34:36], sml[:, 32:34]))
        st.wait()
        for t in range(2):
            st.do(ts(gts[:, t, 0:4], gts[:, t, 0:4], sml[:, 34 + t:35 + t], None, ALU.mult))
        dve.wait_ge(S["route"], 1)
        for j in range(4):
            for t in range(2):
                st.do(ts(one[:, t, :], iotae, tif[:, t, j:j + 1], None, ALU.is_equal))
            st.wait()
            for t in range(2):
                st.do(stt(gat[:, t, :], one[:, t, :], gts[:, t, j:j + 1], gat[:, t, :], ALU.mult, ALU.add))
                st.do(tt(msk[:, t, :], msk[:, t, :], one[:, t, :], ALU.add))
            st.wait()
        dve.sem_inc(S["route"], 1)
        dve.wait_ge(S["rank_mm"], 1)
        st.do(stt(rank[:, :, 0:E], pb[0][:, 0:2 * E].rearrange("p (a e) -> p a e", a=2), 1.0, msk, ALU.add, ALU.mult))
        st.do(nc.vector.tensor_copy(cntf[0:1, 0:E], pb[0][0:1, 64:64 + E]))
        st.wait()
        st.do(ts(rank[:, :, 0:E], rank[:, :, 0:E], -1.0, None, ALU.add))
        st.do(nc.vector.tensor_reduce(cntf[0:1, E:E + 1], cntf[0:1, 0:E], AX.X, ALU.max))
        st.wait()
        nc.vector.tensor_copy(cnti[0:1, :], cntf[0:1, :]).then_inc(S["rank_done"], 1)
        def choose_u(e):
            for t in range(2):
                last = ts(selU[:, t, :], iotac[:, 0:64], rank[:, t, bass.ds(e, 1)], None, ALU.is_equal)
            last.then_inc(S["selu"], 1)

        def choose_g(e):
            for t in range(2):
                last = ts(selG[:, t, :], iotac, rank[:, t, bass.ds(e, 1)], gat[:, t, bass.ds(e, 1)], ALU.is_equal, ALU.mult)
            last.then_inc(S["selg"], 1)

        def add_up(r, n):
            dve.wait_ge(S["sc_mm"], n)
            for h in range(2):
                v = acc[:, 4 * h + 2 * r:4 * h + 2 * r + 2, :]
                last = tt(v, pb[6 + h].rearrange("p (a n) -> p a n", a=2), v, ALU.add)
            last.then_inc(S["acc_done"], 1)

        def expert(e, cur, prev):
            if prev:
                since(dve, "selt_mm", e - 1)
                choose_g(e - 1)
            if cur:
                dve.wait_ge(S["gath"], e + 1)
                choose_u(e + 1)
            if prev:
                since(dve, "acc_done", e * 2 - 2)
                add_up(0, e * 2 - 1)
            if cur:
                dve.wait_ge(S["u_mm"], e * 5 + 5)
                since(dve, "a_done", e)
                u = banks[:, 0:2, :].rearrange("p a (n c) -> p a n c", c=2)
                ts(gl.rearrange("p (a n) -> p a n", a=2), u[:, :, :, 0], 7.0, None, ALU.min)
                ts(li.rearrange("p (a n) -> p a n", a=2), u[:, :, :, 1], 7.0, -7.0, ALU.min, ALU.max).then_inc(S["u_read"], 1)
            if prev:
                add_up(1, e * 2)
            if cur:
                dve.wait_ge(S["u_read"], e + 1)
                since(dve, "at_mm", e)
                stt(aa, li, 1.0, gl, ALU.add, ALU.mult).then_inc(S["a_mid"], 1)
                dve.wait_ge(S["u_sig"], e + 1)
                dve.wait_ge(S["a_mid"], e + 1)
                tt(aa, aa, sg, ALU.mult).then_inc(S["a_done"], 1)

        nc.vector.memset(taken, 0.0).then_inc(S["round"], 1)
        dve.wait_ge(S["round"], 1)
        dve.wait_ge(S["rank_done"], 1)
        choose_u(0)
        expert(0, True, False)
        for b in range(4):
            dve.wait_ge(S["b2_mm"], b + 1)
            nc.vector.tensor_copy(acc[:, 2 * b:2 * b + 2, :], pb[4 + b].rearrange("p (a n) -> p a n", a=2))\
                .then_inc(S["acc_init"], 1)
        dve.wait_ge(S["acc_init"], 4)
        expert(1, True, True)
        with dve.Fori(2, E) as e:
            expert(e, True, True)
        expert(E, False, True)
        dve.wait_ge(S["acc_done"], 2 * E)

        def next_round(r):
            ts(taken, taken, float(CAP), None, ALU.add).then_inc(S["round"], 1)

        def again(e, n, r):
            dve.wait_ge(S["over_pe"], n * 7 + 1)
            dve.wait_ge(S["round"], r + 1)
            for t in range(2):
                last = tt(rks[:, t:t + 1], rank[:, t, bass.ds(e, 1)], taken, ALU.subtract)
            last.then_inc(S["over_dve"], 1)
            dve.wait_ge(S["over_dve"], n * 7 + 1)
            for t in range(2):
                ts(selU[:, t, :], iotac[:, 0:64], rks[:, t:t + 1], None, ALU.is_equal)
                last = ts(selG[:, t, :], iotac, rks[:, t:t + 1], gat[:, t, bass.ds(e, 1)], ALU.is_equal, ALU.mult)
            last.then_inc(S["over_dve"], 1)
            dve.wait_ge(S["over_pe"], n * 7 + 4)
            u = banks[:, 0:2, :].rearrange("p a (n c) -> p a n c", c=2)
            ts(gl.rearrange("p (a n) -> p a n", a=2), u[:, :, :, 0], 7.0, None, ALU.min)
            ts(li.rearrange("p (a n) -> p a n", a=2), u[:, :, :, 1], 7.0, -7.0, ALU.min, ALU.max).then_inc(S["over_dve"], 1)
            dve.wait_ge(S["over_dve"], n * 7 + 3)
            stt(aa, li, 1.0, gl, ALU.add, ALU.mult).then_inc(S["over_dve"], 1)
            dve.wait_ge(S["over_act"], n * 5 + 3)
            dve.wait_ge(S["over_dve"], n * 7 + 4)
            tt(aa, aa, sg, ALU.mult).then_inc(S["over_dve"], 1)
            for q in range(2):
                dve.wait_ge(S["over_pe"], n * 7 + (7 + q))
                for h in range(2):
                    v = acc[:, 4 * h + 2 * q:4 * h + 2 * q + 2, :]
                    last = tt(v, pb[6 + h].rearrange("p (a n) -> p a n", a=2), v, ALU.add)
                last.then_inc(S["over_dve"], 1)
            dve.wait_ge(S["over_dve"], n * 7 + 7)

        further(dve, again, next_round)
        for t in range(KT):
            stt(hx[:, t, :], acc[:, t, :], modT[:, 40 + t:41 + t], hx[:, t, :], ALU.mult, ALU.add).then_inc(S["final_sum"], 1)
        norm(5, hn, hx, nrms, vrows("g_final"))

    @block.tensor
    def _(pe):
        mm = nc.tensor.matmul

        def add_square(k, buf, n, t):
            pe.wait_ge(S["norm_sq"], KT * k + t + 1)
            last = mm(pb[3][:, 0:n], ones[:, :], buf[:, t, 0:n], start=t == 0, stop=t == KT - 1)
            if t == KT - 1:
                last.then_inc(S["norm_ms"], 1)

        def norm(k, buf, n, first=0):
            for t in range(first, KT):
                add_square(k, buf, n, t)

        pe.sem_inc(S["up"], 4)
        pe.wait_ge(S["cst_in"], 16)
        pe.wait_ge(S["x_in"], 32)
        for d in range(KT):
            last = nc.tensor.transpose(pb[4][:, M * d:M * d + M], mtok[:, P * d:P * d + P], ident[0:M, 0:M])
        last.then_inc(S["x_turned"], 1)
        for b in range(4):
            for j in range(4):
                d, t = 2 * b + j // 2, j % 2
                last = nc.tensor.transpose(pb[b][:, P * j:P * j + P], xtok[:, t, P * d:P * d + P], ident)
            last.then_inc(S["x_turned"], 1)
        pe.wait_ge(S["filled"], 1)
        pe.wait_ge(S["x_kept"], 5)
        norm(0, sqa, TM)
        pe.wait_ge(S["vec_in"], 16 * len(VEC_ROWS))
        nc.tensor.transpose(pb[5][:, 0:NVEC], vrow, ident[0:NVEC, 0:NVEC]).then_inc(S["vec_turned"], 1)

        def group(GR, g, w, x, sem_name, evacs):
            p, kind, n, _ = GR[g]
            if g >= 3:
                who, count = evac(GR, g - 3)
                pe.wait_ge(S[evacs[who]], count)
            nk = w.shape[1]
            out = pb[g % 3]
            if kind in ("sv", "dv") and n == 0:
                for k in range(2):
                    for j in range(4):
                        last = mm(out[32 * j:32 * j + 32, :], x[:, 2 * j + k, 0:32], w[:, 2 * j + k, :], start=k == 0, stop=k == 1,
                                  skip_group_check=True)
                last.then_inc(S[sem_name], 1)
                return
            if kind in ("sv", "dv") and n == 3:
                pe.wait_ge(S[evacs[0]], evac(GR, g - 3)[1])
                mm(out[0:M, :], selm, vmeta, start=True, stop=True).then_inc(S[sem_name], 1)
                return
            for k in range(nk):
                if g == 0:
                    pe.wait_ge(S["norm_x"], k + 1)
                if kind in ("sv", "dv"):
                    lhs, o, rhs = x[:, k, M + P * (n - 1):M + P * n], out, w[:, k, :]
                elif kind in ("rv", "av"):
                    lhs, o, rhs = x[:, k, P * n:P * n + P], out, w[:, k, :]
                else:
                    lhs, o, rhs = w[:, k, P * n:P * n + P], out[:, 0:x.shape[2]], x[:, k, :]
                last = mm(o, lhs, rhs, start=k == 0, stop=k == nk - 1)
            last.then_inc(S[sem_name], 1)

        def bank_free(GR, g, evacs):
            if g >= 3:
                who, count = evac(GR, g - 3)
                pe.wait_ge(S[evacs[who]], count)

        def three(out, a, b, start, stop):
            mm(out, a[0], b[0], start=start, stop=False)
            mm(out, a[0], b[1], start=False, stop=False)
            return mm(out, a[1], b[0], start=False, stop=stop)

        def split1(g, n, kind):
            pe.wait_ge(S["w1_lo"], n + 1)
            if kind == "ysb":
                pe.wait_ge(S["y_lo"], 2)
            if kind == "ydf":
                pe.wait_ge(S["y_lo"], 4)
            xh, xl = (dfh, dfl) if kind == "ydf" else (yh, yl)
            bank_free(GR1, g, ("act_evac1", "dve_evac1"))
            wlo, whi = unit1(w2l, n), w2h[:, n % 4, :].rearrange("p (k n) -> p k n", k=KT)
            for k in range(KT):
                if kind == "out":
                    pe.wait_ge(S["y_lo"], 4 + k + 1)
                last = three(pb[g % 3][:, 0:T], (whi[:, k, :], wlo[:, k, :]), (xh[:, k, :], xl[:, k, :]), k == 0, k == KT - 1)
            last.then_inc(S["gemm1"], 1)

        def gemm1(g):
            p, kind, n, c = GR1[g]
            if g >= G0:
                split1(g, g - G0, kind)
                return
            if n == 0:
                pe.wait_ge(in1[p % 2], 16 * (p // 2 + 1))
            x = xn if kind in ("sk", "dk", "sv", "dv") else xn[:, :, M:TM]
            group(GR1, g, slot(4 + p % 2), x, "gemm1", ("act_evac1", "dve_evac1"))

        def sb_step(s, h):
            if s == "sbA":
                pe.wait_ge(S["act_evac1"], evac(GR1, where(GR1, "sk", h))[1])
                if h:
                    pe.wait_ge(S["sb_zs"], h)
                q = sqT[:, h, :]
                mm(pb[3][:, 0:T], skT[:, h, M:M + P], q, start=True, stop=True)
                mm(pb[3][:, T:384], skT[:, h, M + P:TM], q[:, P:T], start=True, stop=True)
                mm(pb[4][0:M, 0:T], skT[:, h, 0:M], q, start=True, stop=True).then_inc(S["sb_scores"], 1)
            if s == "sbB":
                pe.wait_ge(S["sb_sp"], h + 1)
                if h:
                    pe.wait_ge(S["sb_la"], h)
                mm(pb[5][:, T:384], ntri, sp[:, T:384], start=True, stop=True)
                mm(pb[5][:, 0:T], ntri, sp[:, 0:T], start=True, stop=False)
                mm(pb[5][:, P:T], nones[:, :], sp[:, T:384], start=False, stop=True)
                mm(pb[6][0:M, 0:T], ntri[0:M, 0:M], sp[0:M, 384:640], start=True, stop=False)
                mm(pb[6][0:M, 0:T], nones[:, 0:M], sp[:, 0:T], start=False, stop=False)
                mm(pb[6][0:M, P:T], nones[:, 0:M], sp[:, T:384], start=False, stop=True).then_inc(S["sb_rest"], 1)
            if s == "sbC":
                pe.wait_ge(S["sb_a"], h + 1)
                if h % 4 == 0:
                    pe.wait_ge(S["act_evac1"], evac(GR1, where(GR1, "sv", 4 * (h // 4) + 3))[1])
                if h:
                    pe.wait_ge(S["sb_out"], h)
                v = slice(P * h, P * h + P)
                mm(pb[7][:, 0:T], sv[:, 0, v], la[:, 0:T], start=True, stop=False)
                mm(pb[7][:, P:T], sv[:, 1, v], la[:, T:384], start=False, stop=False)
                mm(pb[7][:, 0:T], sv[0:M, 2, v], la[0:M, 384:640], start=False, stop=True).then_inc(S["sb_o"], 1)

        def df_step(s, h):
            if s == "dfA":
                pe.wait_ge(S["act_evac1"], evac(GR1, where(GR1, "dk", h))[1])
                if h:
                    pe.wait_ge(S["df_s"], h)
                else:
                    pe.wait_ge(S["sb_zs"], HEADS)
                for qt in range(2):
                    for c in range(2):
                        v = slice(64 * c, 64 * c + 64)
                        last = mm(pb[3 + c][:, 144 * qt:144 + 272 * qt], dqT[v, h, P * qt:P * qt + P],
                                  dkT[v, h, 0:144 + P * qt], start=True, stop=True)
                last.then_inc(S["df_scores"], 1)
            if s == "dfB":
                pe.wait_ge(S["df_w"], h + 1)
                if h:
                    pe.wait_ge(S["df_wt"], h)
                    pe.wait_ge(S["df_rs"], h)
                else:
                    pe.wait_ge(S["sb_la"], HEADS)
                tr = nc.tensor.transpose
                tr(pb[5][:, 0:P], wv[:, M:144], ident)
                tr(pb[5][:, P:T], wv[:, 160:288], ident)
                tr(pb[5][:, T:384], wv[:, 288:416], ident)
                tr(pb[6][0:M, 0:P], wv[:, 0:M], ident)
                tr(pb[6][0:M, P:T], wv[:, 144:160], ident).then_inc(S["df_tr"], 1)
            if s == "dfC":
                pe.wait_ge(S["df_wt"], h + 1)
                if h % 4 == 0:
                    pe.wait_ge(S["act_evac1"], evac(GR1, where(GR1, "dv", 4 * (h // 4) + 3))[1])
                if h:
                    pe.wait_ge(S["df_out"], h)
                else:
                    pe.wait_ge(S["sb_out"], HEADS)
                v = slice(P * h, P * h + P)
                mm(pb[7][:, 0:T], dv[:, 0, v], wT[:, 0:T], start=True, stop=False)
                mm(pb[7][:, P:T], dv[:, 1, v], wT[:, T:384], start=False, stop=False)
                mm(pb[7][:, 0:T], dv[0:M, 2, v], wT[0:M, 384:640], start=False, stop=True).then_inc(S["df_o"], 1)
            if s == "dfD":
                pe.wait_ge(S["df_sq"], h + 1)
                mm(pb[6][:, T:512], ones[:, :], osq, start=True, stop=True).then_inc(S["df_ms"], 1)

        for s, h in ORDER1:
            if s == "G":
                gemm1(h)
            elif s[0:2] == "sb":
                sb_step(s, h)
            elif s[0:2] == "df":
                df_step(s, h)
            elif s == "square":
                add_square(1, sqa1, T, h)

        norm(1, sqa1, T, SQUARED)
        pe.wait_ge(S["norm_x"], 2 * KT)

        def product(out, i, at, xh, xl, start, stop):
            v = slice(at, at + P)
            mm(out, wh[:, i, v], xh, start=start, stop=False, skip_group_check=True)
            mm(out, wh[:, i, v], xl, start=False, stop=False, skip_group_check=True)
            return mm(out, wl[:, i, v], xh, start=False, stop=stop, skip_group_check=True)

        def up(f, n, first=False):
            for q in range(2):
                pe.wait_ge(S["up_free"], f + (q + 1))
                for side in range(2):
                    i = 2 * q + side
                    pe.wait_ge(S["w_lo"], n + (i + 1))
                    for k in range(KT):
                        if first and i == 0:
                            pe.wait_ge(S["x_lo"], k + 1)
                        last = product(pb[i][:, 0:T], i, P * k, xfh[:, k, :], xfl[:, k, :], k == 0, k == KT - 1)
                    last.then_inc(S["up"], 1)

        def ada_mm(j, b, bank=7):
            pe.wait_ge(S["ada_sum"], j + 1)
            for n in range(4):
                last = mm(pb[bank][:, bass.ds(j * 4 + n, 1)], adac[:, b, P * n:P * n + P], ones[:, 0:1], start=True, stop=True)
            last.then_inc(S["ada_mm"], 1)

        pe.sem_inc(S["ada_mm"], 2)
        up(0, 0, True)
        with pe.Fori(0, UPS // 2) as i:
            for b in range(2):
                up(i * 4 + (2 + 2 * b), i * 8 + (4 + 4 * b))
                ada_mm(i * 2 + b, b)
        pe.wait_ge(S["mod_done"], 1)
        for kk in range(FT):
            pe.wait_ge(S["w_lo"], 4 * UPS + kk + 1)
            if kk == 0:
                pe.wait_ge(S["up_step"], 3 * (FT - 2))
            if kk == FT - 2:
                pe.wait_ge(S["up_step"], 3 * FT)
            if kk in (3, 7):
                ada_mm(ADAS - 2 + kk // 4, kk // 4, 0)
            for n in range(KT):
                last = product(pb[4 + n // 2][:, T * (n % 2):T * (n % 2) + T], kk % 4, P * n, fh[:, kk, :], fl[:, kk, :],
                               kk == 0 and n % 2 == 0, kk == FT - 1)
                if kk == FT - 1 and n % 2:
                    last.then_inc(S["down"], 1)
            if kk < FT - 1:
                last.then_inc(S["up"], 1)
        norm(2, sqa, T)
        norm(3, sqa, T)

        def toeplitz():
            pe.wait_ge(S["hot_in"], 48)
            for g in range(GROUPS):
                mm(pb[4 + g][0:SLOTS, 0:TOEP], relb[:, SLOTS * g:SLOTS * g + SLOTS], hot[:, g, :], start=True, stop=True)\
                    .then_inc(S["toep_mm"], 1)

        def unit(n):
            kind, both = PIECES2[n // 4][0], ("act_evac2", "dve_evac2")
            pe.wait_ge(S["w_lo"], MLP_GROUPS + n + 1)
            if n == unit_of("yret"):
                pe.wait_ge(S["x_lo"], 2 * KT + 3)
            if n == unit_of("yatt"):
                pe.wait_ge(S["x_lo"], 2 * KT + 1)
            wlo = unit2(w2l, n)
            whi = w2h[:, n % 4, :].rearrange("p (k n) -> p k n", k=wlo.shape[1])
            if kind in ("rv", "av"):
                g = UNITS2[n // 4 * 4 + 3]
                for kk in range(2):
                    k = 2 * (n % 4) + kk
                    for t in range(2):
                        if k == 0:
                            bank_free(GR2, g[t], both)
                        v = slice(P * t, P * t + P)
                        last = three(pb[g[t] % 3], (x2h[:, k, v], x2l[:, k, v]), (whi[:, kk, :], wlo[:, kk, :]), k == 0, k == KT - 1)
                        if k == KT - 1:
                            last.then_inc(S["gemm2"], 1)
                if n % 4 < 3:
                    last.then_inc(S["v_unit"], 1)
                return
            xh, xl = {"yret": (rgh, rgl), "yatt": (atth, attl), "o": (m2h, m2l)}.get(kind, (x2h, x2l))
            for j, g in enumerate(UNITS2[n]):
                bank_free(GR2, g, both)
                v = slice(P * j, P * j + P)
                for k in range(wlo.shape[1]):
                    if n == unit_of("o"):
                        pe.wait_ge(S["x_lo"], 2 * KT + 3 + k + 1)
                    if n == 0:
                        pe.wait_ge(S["x_lo"], KT + k + 1)
                    last = three(pb[g % 3][:, 0:T], (whi[:, k, v], wlo[:, k, v]), (xh[:, k, :], xl[:, k, :]),
                                 k == 0, k == wlo.shape[1] - 1)
                last.then_inc(S["gemm2"], 1)

        def rotary(i):
            g = first_of(GR2, ("rq", "rk")[i]) + 3
            pe.wait_ge(S["act_evac2"], evac(GR2, g)[1])
            if i:
                pe.wait_ge(S["rot_out"], 1)
            else:
                pe.wait_ge(S["toep_sum"], GROUPS)
            for j in range(2):
                last = mm(pb[3 + j], swap, raw[:, i, 512 * j:512 * j + 512], start=True, stop=True)
            last.then_inc(S["rot_mm"], 1)

        def rt_step(s, h):
            if s == "rtA":
                pe.wait_ge(S["rot_out"], 2)
                if h:
                    pe.wait_ge(S["rt_p"], h)
                mm(pb[3][:, 0:T], rkT[:, h, 0:P], rqT[:, h, :], start=True, stop=True)
                mm(pb[3][:, T:384], rkT[:, h, P:T], rqT[:, h, P:T], start=True, stop=True).then_inc(S["rt_s"], 1)
            if s == "rtB":
                pe.wait_ge(S["rt_p"], h + 1)
                if h:
                    pe.wait_ge(S["rt_ys"], h)
                else:
                    pe.wait_ge(S["act_evac2"], evac(GR2, last_of(GR2, "rv"))[1])
                for e in range(2):
                    v = slice(T * h + P * e, T * h + P * e + P)
                    mm(pb[4][:, T * e:T * e + T], rv[:, 0, v], pT[:, 0:T], start=True, stop=False)
                    last = mm(pb[4][:, T * e + P:T * e + T], rv[:, 1, v], pT[:, T:384], start=False, stop=True)
                last.then_inc(S["rt_y"], 1)
            if s == "rtC":
                pe.wait_ge(S["rt_ys"], h + 1)
                for e in range(2):
                    last = mm(pb[5][:, 0:T], ones[:, :], ys[:, e, :], start=e == 0, stop=e == 1)
                last.then_inc(S["rt_m"], 1)
            if s == "rtD":
                pe.wait_ge(S["rt_sq"], h + 1)
                for e in range(2):
                    last = mm(pb[6][:, 0:T], ones[:, :], yq[:, e, :], start=e == 0, stop=e == 1)
                last.then_inc(S["rt_v"], 1)

        def dl_step(s, h):
            if s == "dlA":
                if h == 0:
                    pe.wait_ge(S["act_evac2"], evac(GR2, last_of(GR2, "ak"))[1])
                    pe.wait_ge(S["rt_yc"], RH)
                else:
                    pe.wait_ge(S["dl_wt"], h)
                for g in range(GROUPS):
                    n = SLOTS * g + h
                    mm(pb[3][:, P * g:P * g + P], aqT[:, n, 0:P], akT[:, n, 0:P], start=True, stop=True)
                for g in range(GROUPS):
                    n = SLOTS * g + h
                    last = mm(pb[4 + g // 2][:, T * (g % 2):T * (g % 2) + T], aqT[:, n, P:T], akT[:, n, :], start=True, stop=True)
                last.then_inc(S["dl_s"], 1)
            if s == "dlB":
                pe.wait_ge(S["dl_p"], h + 1)
                for g in range(GROUPS):
                    for j, at in enumerate((P * g, 384 + T * g, 384 + T * g + P)):
                        last = nc.tensor.transpose(pb[3 + g][:, P * j:P * j + P], ds[:, at:at + P], ident)
                last.then_inc(S["dl_t"], 1)
            if s == "dlC":
                pe.wait_ge(S["dl_wt"], h + 1)
                if h:
                    pe.wait_ge(S["dl_out"], h)
                else:
                    pe.wait_ge(S["act_evac2"], evac(GR2, last_of(GR2, "av"))[1])
                for g in range(GROUPS):
                    v = slice(P * (SLOTS * g + h), P * (SLOTS * g + h) + P)
                    mm(pb[7][:, 0:T], av[:, 0, v], dwT[:, 384 * g:384 * g + T], start=g == 0, stop=False)
                    last = mm(pb[7][:, P:T], av[:, 1, v], dwT[:, 384 * g + T:384 * g + 384], start=False, stop=g == 2)
                last.then_inc(S["dl_o"], 1)

        for s, h in ORDER2:
            if s == "G":
                unit(h)
            elif s == "square":
                add_square(4, nsq, T, h)
            elif s == "toep":
                toeplitz()
            elif s == "rot":
                rotary(h)
            elif s[0:2] == "rt":
                rt_step(s, h)
            elif s[0:2] == "dl":
                dl_step(s, h)

        norm(4, nsq, T, SQUARED)

        def turn_back(name, wait):
            for b in range(4):
                t, half = b // 2, b % 2
                for j in range(4):
                    if wait is not None:
                        pe.wait_ge(*wait(4 * half + j))
                    last = nc.tensor.transpose(pb[4 + b][:, P * j:P * j + P], hn[:, 4 * half + j, P * t:P * t + P], ident)
                last.then_inc(S[name], 1)

        pe.wait_ge(S["moe_in"], 48)
        for t in range(2):
            for k in range(KT):
                pe.wait_ge(S["norm_s"], k + 1)
                last = mm(pb[1][:, E * t:E * t + E], hn[:, k, P * t:P * t + P], wr[:, k, :], start=k == 0, stop=k == KT - 1)
        last.then_inc(S["log_mm"], 1)
        turn_back("ht_mm", None)
        pe.wait_ge(S["route"], 2)
        mm(pb[0][:, 0:E], tri, msk[:, 0, :], start=True, stop=True)
        mm(pb[0][:, E:2 * E], ones[:, :], msk[:, 0, :], start=True, stop=False)
        mm(pb[0][:, E:2 * E], tri, msk[:, 1, :], start=False, stop=True)
        mm(pb[0][0:1, 2 * E:3 * E], ones[:, 0:1], msk[:, 0, :], start=True, stop=False)
        mm(pb[0][0:1, 2 * E:3 * E], ones[:, 0:1], msk[:, 1, :], start=False, stop=True).then_inc(S["rank_mm"], 1)
        for t in range(2):
            last = nc.tensor.transpose(pb[2][0:E, P * t:P * t + P], gat[:, t, :], ident)
        last.then_inc(S["gt_mm"], 1)
        pe.wait_ge(S["ht_kept"], 4)
        pe.wait_ge(S["rank_done"], 1)

        def scatter(r, n):
            since(pe, "acc_done", n)
            for j in range(2):
                for h in range(2):
                    v = slice(64 * h, 64 * h + 64)
                    last = mm(pb[6 + h][:, T * j:T * j + T], yv[v, P * (2 * r + j):P * (2 * r + j) + P], selT[v, :],
                              start=True, stop=True)
            last.then_inc(S["sc_mm"], 1)

        def up1(e, c):
            pe.wait_ge(inw[c], e * 16 + 16)
            for k in range(2):
                for b in range(2):
                    for h in range(2):
                        last = mm(pb[b][64 * h:64 * h + 64, :], XgT[:, 2 * c + k, :], slot(c, 2)[:, k, 1024 * h + 512 * b:1024 * h + 512 * b + 512],
                                  start=c == 0 and k == 0, stop=False, skip_group_check=True)
            last.then_inc(S["u_mm"], 1)

        def expert(e, cur, prev):
            if cur:
                pe.wait_ge(S["selu"], e + 1)
                since(pe, "xg", e)
                for k in range(KT):
                    for t in range(2):
                        last = mm(pb[3][:, 64 * k:64 * k + 64], htok[:, t, P * k:P * k + P], selU[:, t, :], start=t == 0, stop=t == 1)
                last.then_inc(S["gath"], 1)
            if prev:
                since(pe, "a_done", e)
                since(pe, "at", e - 1)
                for j in range(4):
                    last = nc.tensor.transpose(pb[4][:, P * j:P * j + P], aa[:, P * j:P * j + P], ident)
                last.then_inc(S["at_mm"], 1)
                since(pe, "selg", e)
                since(pe, "selt", e - 1)
                for t in range(2):
                    last = nc.tensor.transpose(pb[5][:, P * t:P * t + P], selG[:, t, :], ident)
                last.then_inc(S["selt_mm"], 1)
            if cur:
                pe.wait_ge(S["xg"], e + 1)
                since(pe, "u_read", e)
                up1(e, 0)
                up1(e, 1)
            if prev:
                since(pe, "at", e)
                since(pe, "yv_done", e - 1)
                for c in range(2):
                    pe.wait_ge(inw[4 + c], e * 16)
                    for k in range(4):
                        for h in range(2):
                            last = mm(pb[2][64 * h:64 * h + 64, :], aT[:, k, 64 * c:64 * c + 64], slot(4 + c, 4)[:, k, 512 * h:512 * h + 512],
                                      start=c == 0 and k == 0, stop=c == 1 and k == 3, skip_group_check=True)
                    last.then_inc(S["y_mm"], 1)
            if cur:
                up1(e, 2)
            if prev:
                since(pe, "yv_done", e)
                since(pe, "selt", e)
                scatter(0, e * 2 - 2)
            if cur:
                up1(e, 3)
                pe.wait_ge(S["b1_in"], e * 16 + 16)
                for b in range(2):
                    for h in range(2):
                        last = mm(pb[b][64 * h:64 * h + 64, :], ones[:, 0:64], b1p[:, 1024 * h + 512 * b:1024 * h + 512 * b + 512],
                                  start=False, stop=True, skip_group_check=True)
                last.then_inc(S["u_mm"], 1)
            if prev:
                scatter(1, e * 2 - 1)

        expert(0, True, False)
        pe.wait_ge(S["gt_kept"], 1)
        for b in range(4):
            for j in range(2):
                n = 2 * b + j
                last = mm(pb[4 + b][:, T * j:T * j + T], b2s[:, P * n:P * n + P], gatT, start=True, stop=True)
            last.then_inc(S["b2_mm"], 1)
        pe.wait_ge(S["acc_init"], 4)
        expert(1, True, True)
        with pe.Fori(2, E) as e:
            expert(e, True, True)
        expert(E, False, True)

        def again(e, n, r):
            pe.wait_ge(S["over_dve"], n * 7 + 2)
            for k in range(KT):
                for t in range(2):
                    last = mm(pb[3][:, 64 * k:64 * k + 64], htok[:, t, P * k:P * k + P], selU[:, t, :], start=t == 0, stop=t == 1)
            last.then_inc(S["over_pe"], 1)
            for t in range(2):
                last = nc.tensor.transpose(pb[5][:, P * t:P * t + P], selG[:, t, :], ident)
            last.then_inc(S["over_pe"], 1)
            pe.wait_ge(S["over_act"], n * 5 + 1)
            pe.wait_ge(S["over_in"], n * 112 + 112)
            for k in range(KT):
                for b in range(2):
                    for h in range(2):
                        mm(pb[b][64 * h:64 * h + 64, :], XgT[:, k, :], slot(k // 2, 2)[:, k % 2, 1024 * h + 512 * b:1024 * h + 512 * b + 512],
                           start=k == 0, stop=False, skip_group_check=True)
            for b in range(2):
                for h in range(2):
                    last = mm(pb[b][64 * h:64 * h + 64, :], ones[:, 0:64], b1p[:, 1024 * h + 512 * b:1024 * h + 512 * b + 512],
                              start=False, stop=True, skip_group_check=True)
            last.then_inc(S["over_pe"], 1)
            pe.wait_ge(S["over_dve"], n * 7 + 5)
            for j in range(4):
                last = nc.tensor.transpose(pb[4][:, P * j:P * j + P], aa[:, P * j:P * j + P], ident)
            last.then_inc(S["over_pe"], 1)
            pe.wait_ge(S["over_act"], n * 5 + 4)
            for k in range(KT):
                for h in range(2):
                    last = mm(pb[2][64 * h:64 * h + 64, :], aT[:, k % 4, 64 * (k // 4):64 * (k // 4) + 64],
                              slot(4 + k // 4, 4)[:, k % 4, 512 * h:512 * h + 512], start=k == 0, stop=k == KT - 1, skip_group_check=True)
            last.then_inc(S["over_pe"], 1)
            pe.wait_ge(S["over_act"], n * 5 + 5)
            for q in range(2):
                if q:
                    pe.wait_ge(S["over_dve"], n * 7 + 6)
                for j in range(2):
                    for h in range(2):
                        v = slice(64 * h, 64 * h + 64)
                        last = mm(pb[6 + h][:, T * j:T * j + T], yv[v, P * (2 * q + j):P * (2 * q + j) + P], selT[v, :],
                                  start=True, stop=True)
                last.then_inc(S["over_pe"], 1)

        pe.sem_inc(S["over_pe"], 1)
        further(pe, again)
        norm(5, nsq, T)
        turn_back("fin_mm", lambda t: (S["norm_x"], 5 * KT + t + 1))


_INS = ["x", "meta", "norm_mix_g", "w_in", "w_gate", "b_gate", "lam_q1", "lam_k1", "lam_q2", "lam_k2", "subln_g",
        "w_br_sb", "w_br_df", "w_out", "norm_ffn_g", "w_ffn_gate", "w_ffn_up", "w_ffn_down", "norm_final_g", "c_2",
        "w_ada_2", "b_ada_2", "g_mix_2", "w_in_2", "rel_bias_2", "w_ret_o_2", "w_att_o_2", "w_o_2", "g_ffn_2",
        "w_router_2", "b_router_2", "w_mlp1_2", "b_mlp1_2", "w_mlp2_2", "b_mlp2_2", "g_final_2"]


def kernel(**inputs):
    import numpy as _np
    import concourse.bacc as _bacc
    from concourse import mybir as _mybir
    from concourse.bass_utils import run_bass_kernel_spmd as _run

    nc = _bacc.Bacc("TRN2", target_bir_lowering=False, num_devices=1)
    arrays, args = {}, {}
    for name in _INS:
        arrays[f"in_{name}"] = _np.ascontiguousarray(inputs[name])
    for name, table in zip(("cst", "tab", "hot", "bad"), constants()):
        arrays[f"in_{name}"] = table
    for name, v in arrays.items():
        args[name[3:]] = nc.dram_tensor(name, v.shape, _mybir.dt.from_np(v.dtype), kind="ExternalInput").ap()
    args["toep"] = nc.dram_tensor("toep", (GROUPS * SLOTS, TOEP), F32, kind="Internal").ap()
    args["toeps"] = nc.dram_tensor("toeps", (P, GROUPS * SLOTS * TOEP), F32, kind="Internal").ap()
    args["out"] = nc.dram_tensor("out_0", (1, T, D), F32, kind="ExternalOutput").ap()
    with ExitStack() as ctx:
        program(nc, args, ctx)
    r = _run(nc, [arrays], core_ids=[0])
    return r.results[0]["out_0"]
```
